# Optimizing a Trainium2 kernel written in Bass

```python
import math
import jax, jax.numpy as jnp
from jax import lax
import numpy as np

D_MODEL = 1024
BATCH = 1
SEQ = 1024
DEPTH = 1

CHUNK = 64
A_HEADS = 8
A_KV_HEADS = 2
A_HEAD_DIM = 64
A_GROUP = A_HEADS // A_KV_HEADS
A_WINDOW = 128
A_WIN_CHUNKS = A_WINDOW // CHUNK
A_KEYS = A_WIN_CHUNKS * CHUNK
B_HEADS = 4
B_HEAD_DIM = 128
CONV_WIDTH = 4
PEER_HEADS = 8
N_KEYS = 128
N_EXPERTS = N_KEYS * N_KEYS
PEER_QUERY_DIM = 256
PEER_TOPK = 16
PEER_TOKEN_BLOCK = 128
LN_EPS = 1e-5
NORM_EPS = 1e-6
DN_ALPHA = (2 * DEPTH) ** 0.25
DN_BETA = (8 * DEPTH) ** -0.25

A_Q_W = A_HEADS * A_HEAD_DIM
A_KV_W = A_KV_HEADS * A_HEAD_DIM
B_W = B_HEADS * B_HEAD_DIM
MIX_WIDTH = A_Q_W + B_W
IN_WIDTHS = (A_Q_W, A_KV_W, A_KV_W, 3 * B_W, B_W, B_HEADS, B_HEADS)
IN_PROJ_W = sum(IN_WIDTHS)
IN_SPLITS = tuple(int(s) for s in np.cumsum(IN_WIDTHS)[:-1])

kernel_name = 'hybrid_swa_gdn_peer_deepnorm'

def layer_norm(x, g, b):
    x32 = x.astype(jnp.float32)
    mu = jnp.mean(x32, axis=-1, keepdims=True)
    var = jnp.mean(jnp.square(x32 - mu), axis=-1, keepdims=True)
    y = (x32 - mu) * lax.rsqrt(var + LN_EPS) * g.astype(jnp.float32) + b.astype(jnp.float32)
    return y.astype(x.dtype)

def alibi_slopes(n_heads):
    return jnp.exp2(-8.0 * jnp.arange(1, n_heads + 1, dtype=jnp.float32) / n_heads)

def shift_chunks(t, n):
    if n == 0:
        return t
    return jnp.concatenate([jnp.zeros_like(t[:, :n]), t[:, :-n]], axis=1)

def window_attention(q, k, v, sinks):
    B, S = q.shape[0], q.shape[1]
    nC = S // CHUNK
    qc = q.reshape(B, nC, CHUNK, A_KV_HEADS, A_GROUP, A_HEAD_DIM)
    kc = k.reshape(B, nC, CHUNK, A_KV_HEADS, A_HEAD_DIM)
    vc = v.reshape(B, nC, CHUNK, A_KV_HEADS, A_HEAD_DIM)
    offs = range(A_WIN_CHUNKS - 1, -1, -1)
    kb = jnp.concatenate([shift_chunks(kc, o) for o in offs], axis=2)
    vb = jnp.concatenate([shift_chunks(vc, o) for o in offs], axis=2)
    scores = jnp.einsum('bcqkgd,bcskd->bkgcqs', qc, kb).astype(jnp.float32) * (A_HEAD_DIM ** -0.5)
    i = jnp.arange(CHUNK)[:, None]
    j = jnp.arange(A_KEYS)[None, :]
    dist = jnp.abs((A_WIN_CHUNKS - 1) * CHUNK + i - j).astype(jnp.float32)
    slopes = alibi_slopes(A_HEADS).reshape(A_KV_HEADS, A_GROUP)
    scores = scores - slopes[:, :, None, None, None] * dist
    key_chunk_back = (A_WIN_CHUNKS - 1) - j // CHUNK
    valid = jnp.arange(nC)[:, None] >= key_chunk_back
    scores = jnp.where(valid[:, None, :], scores, -jnp.inf)
    sink = jnp.broadcast_to(sinks.astype(jnp.float32).reshape(A_KV_HEADS, A_GROUP)[:, :, None, None, None],
                            scores.shape[:-1] + (1,))
    p = jax.nn.softmax(jnp.concatenate([scores, sink], axis=-1), axis=-1)[..., :-1]
    out = jnp.einsum('bkgcqs,bcskd->bcqkgd', p.astype(v.dtype), vb)
    return out.reshape(B, S, A_Q_W)

def causal_conv_silu(x, w):
    S = x.shape[1]
    xp = jnp.pad(x, ((0, 0), (CONV_WIDTH - 1, 0), (0, 0)))
    y = sum(xp[:, t:t + S] * w[t] for t in range(CONV_WIDTH))
    return jax.nn.silu(y)

def l2norm(t):
    return t * lax.rsqrt(jnp.sum(t * t, axis=-1, keepdims=True) + NORM_EPS)

def gated_delta_rule(q, k, v, g, beta):
    B, S, H, dk = q.shape
    dv = v.shape[-1]
    nC = S // CHUNK
    f32 = jnp.float32

    def to_chunks(t):
        return jnp.moveaxis(t.reshape(B, nC, CHUNK, H, -1), 3, 1)

    q = to_chunks(l2norm(q.astype(f32)) * (dk ** -0.5))
    k = to_chunks(l2norm(k.astype(f32)))
    v = to_chunks(v.astype(f32))
    gc = jnp.cumsum(to_chunks(g.astype(f32)[..., None])[..., 0], axis=-1)
    bt = to_chunks(beta.astype(f32)[..., None])
    tri = jnp.tril(jnp.ones((CHUNK, CHUNK), dtype=bool))
    strict = jnp.tril(jnp.ones((CHUNK, CHUNK), dtype=bool), -1)
    decay = jnp.exp(jnp.where(tri, gc[..., :, None] - gc[..., None, :], -jnp.inf))
    kb = k * bt
    vb = v * bt
    m = jnp.where(strict, jnp.einsum('bhnid,bhnjd->bhnij', kb, k) * decay, 0.0)
    eye = jnp.eye(CHUNK, dtype=f32)
    t_inv = lax.linalg.triangular_solve(eye + m, jnp.broadcast_to(eye, m.shape),
                                        left_side=True, lower=True, unit_diagonal=True)
    w_val = jnp.einsum('bhnij,bhnjd->bhnid', t_inv, vb)
    kcd = jnp.einsum('bhnij,bhnjd->bhnid', t_inv, kb * jnp.exp(gc)[..., None])
    intra = jnp.where(tri, jnp.einsum('bhnid,bhnjd->bhnij', q, k) * decay, 0.0)
    q_dec = q * jnp.exp(gc)[..., None]
    g_last = gc[..., -1]
    k_dec = k * jnp.exp(g_last[..., None] - gc)[..., None]

    def step(state, xs):
        q_c, kcd_c, w_c, intra_c, kd_c, gl_c = xs
        v_new = w_c - jnp.einsum('bhck,bhkv->bhcv', kcd_c, state)
        o = jnp.einsum('bhck,bhkv->bhcv', q_c, state) + jnp.einsum('bhij,bhjv->bhiv', intra_c, v_new)
        state = state * jnp.exp(gl_c)[..., None, None] + jnp.einsum('bhck,bhcv->bhkv', kd_c, v_new)
        return state, o

    xs = tuple(jnp.moveaxis(t, 2, 0) for t in (q_dec, kcd, w_val, intra, k_dec, g_last))
    _, o = lax.scan(step, jnp.zeros((B, H, dk, dv), f32), xs)
    return o.transpose(1, 0, 3, 2, 4).reshape(B, S, H, dv)

def gated_rmsnorm(o, z, w):
    o32 = o.astype(jnp.float32)
    var = jnp.mean(o32 * o32, axis=-1, keepdims=True)
    return o32 * lax.rsqrt(var + NORM_EPS) * w.astype(jnp.float32) * jax.nn.silu(z.astype(jnp.float32))

def mixing_sublayer(h, w_in, conv_w, a_sinks, b_a_log, b_dt_bias, b_norm_w, w_out):
    B, S, _ = h.shape
    proj = jnp.einsum('bsd,de->bse', h, w_in)
    a_q, a_k, a_v, b_qkv, b_z, b_a, b_b = jnp.split(proj, IN_SPLITS, axis=-1)
    y_a = window_attention(a_q.reshape(B, S, A_HEADS, A_HEAD_DIM),
                           a_k.reshape(B, S, A_KV_HEADS, A_HEAD_DIM),
                           a_v.reshape(B, S, A_KV_HEADS, A_HEAD_DIM), a_sinks)
    b_qkv = causal_conv_silu(b_qkv, conv_w)
    b_q, b_k, b_v = jnp.split(b_qkv, 3, axis=-1)
    shp = (B, S, B_HEADS, B_HEAD_DIM)
    log_decay = -jnp.exp(b_a_log.astype(jnp.float32)) * jax.nn.softplus(
        b_a.astype(jnp.float32) + b_dt_bias.astype(jnp.float32))
    beta = jax.nn.sigmoid(b_b.astype(jnp.float32))
    o_b = gated_delta_rule(b_q.reshape(shp), b_k.reshape(shp), b_v.reshape(shp), log_decay, beta)
    y_b = gated_rmsnorm(o_b, b_z.reshape(shp), b_norm_w).reshape(B, S, B_W).astype(h.dtype)
    y = jnp.concatenate([y_a, y_b], axis=-1)
    return jnp.einsum('bse,ed->bsd', y, w_out)

def peer_sublayer(h, w_query, sub_keys, expert_u, expert_v):
    B, S, D = h.shape
    K = PEER_TOPK
    q = jnp.einsum('bsd,de->bse', h, w_query).reshape(B, S, PEER_HEADS, 2, PEER_QUERY_DIM // 2)
    scores = jnp.einsum('bshpd,hpnd->bshpn', q, sub_keys).astype(jnp.float32)
    s_top, i_top = lax.top_k(scores, K)
    cand = (s_top[..., 0, :, None] + s_top[..., 1, None, :]).reshape(B, S, PEER_HEADS, K * K)
    best, ci = lax.top_k(cand, K)
    i1 = jnp.take_along_axis(i_top[..., 0, :], ci // K, axis=-1)
    i2 = jnp.take_along_axis(i_top[..., 1, :], ci % K, axis=-1)
    expert = i1 * N_KEYS + i2
    gates = jax.nn.softmax(best, axis=-1).astype(h.dtype)
    nb = (B * S) // PEER_TOKEN_BLOCK
    xb = h.reshape(nb, PEER_TOKEN_BLOCK, D)
    eb = expert.reshape(nb, PEER_TOKEN_BLOCK, PEER_HEADS * K)
    gb = gates.reshape(nb, PEER_TOKEN_BLOCK, PEER_HEADS * K)

    def block(args):
        xt, et, gt = args
        u = jnp.take(expert_u, et, axis=0)
        act = jax.nn.gelu(jnp.einsum('tkd,td->tk', u, xt), approximate=False) * gt
        return jnp.einsum('tk,tkd->td', act, jnp.take(expert_v, et, axis=0))

    return lax.map(block, (xb, eb, gb)).reshape(B, S, D)

def setup_inputs(seed: int = 0) -> dict:
    key = jax.random.key(seed)
    ks = jax.random.split(key, 20)
    f32 = jnp.float32
    L = DEPTH
    nrm = jax.random.normal
    x = nrm(ks[0], (BATCH, SEQ, D_MODEL), f32)
    ln_in_g = 1.0 + 0.02 * nrm(ks[1], (D_MODEL,), f32)
    ln_in_b = 0.02 * nrm(ks[2], (D_MODEL,), f32)
    col_scale = np.concatenate([np.ones(A_Q_W + A_KV_W), np.full(A_KV_W, DN_BETA),
                                np.ones(2 * B_W), np.full(B_W, DN_BETA),
                                np.ones(B_W + 2 * B_HEADS)]).astype(np.float32)
    w_in = nrm(ks[3], (L, D_MODEL, IN_PROJ_W), f32) * (D_MODEL ** -0.5) * jnp.asarray(col_scale)
    conv_w = nrm(ks[4], (L, CONV_WIDTH, 3 * B_W), f32) * (CONV_WIDTH ** -0.5)
    a_sinks = nrm(ks[5], (L, A_HEADS), f32)
    b_a_log = jnp.log(jax.random.uniform(ks[6], (L, B_HEADS), f32, minval=1.0, maxval=16.0))
    dt = jnp.exp(jax.random.uniform(ks[7], (L, B_HEADS), f32, minval=math.log(1e-3), maxval=math.log(1e-1)))
    b_dt_bias = dt + jnp.log(-jnp.expm1(-dt))
    b_norm_w = 1.0 + 0.02 * nrm(ks[8], (L, B_HEAD_DIM), f32)
    w_out = nrm(ks[9], (L, MIX_WIDTH, D_MODEL), f32) * (MIX_WIDTH ** -0.5) * DN_BETA
    ln1_g = 1.0 + 0.02 * nrm(ks[10], (L, D_MODEL), f32)
    ln1_b = 0.02 * nrm(ks[11], (L, D_MODEL), f32)
    w_query = nrm(ks[12], (L, D_MODEL, PEER_HEADS * PEER_QUERY_DIM), f32) * (D_MODEL ** -0.5)
    sub_keys = nrm(ks[13], (L, PEER_HEADS, 2, N_KEYS, PEER_QUERY_DIM // 2), f32) * ((PEER_QUERY_DIM // 2) ** -0.5)
    expert_u = nrm(ks[14], (L, N_EXPERTS, D_MODEL), f32) * (D_MODEL ** -0.5)
    expert_v = nrm(ks[15], (L, N_EXPERTS, D_MODEL), f32) * DN_BETA
    ln2_g = 1.0 + 0.02 * nrm(ks[16], (L, D_MODEL), f32)
    ln2_b = 0.02 * nrm(ks[17], (L, D_MODEL), f32)
    return {'x': x, 'ln_in_g': ln_in_g, 'ln_in_b': ln_in_b, 'w_in': w_in, 'conv_w': conv_w,
            'a_sinks': a_sinks, 'b_a_log': b_a_log, 'b_dt_bias': b_dt_bias, 'b_norm_w': b_norm_w,
            'w_out': w_out, 'ln1_g': ln1_g, 'ln1_b': ln1_b, 'w_query': w_query, 'sub_keys': sub_keys,
            'expert_u': expert_u, 'expert_v': expert_v, 'ln2_g': ln2_g, 'ln2_b': ln2_b}

def reference(x, ln_in_g, ln_in_b, w_in, conv_w, a_sinks, b_a_log, b_dt_bias, b_norm_w, w_out,
              ln1_g, ln1_b, w_query, sub_keys, expert_u, expert_v, ln2_g, ln2_b):
    h = layer_norm(x, ln_in_g, ln_in_b)
    for l in range(DEPTH):
        mix = mixing_sublayer(h, w_in[l], conv_w[l], a_sinks[l], b_a_log[l], b_dt_bias[l],
                              b_norm_w[l], w_out[l])
        h = layer_norm(DN_ALPHA * h + mix, ln1_g[l], ln1_b[l])
        ffn = peer_sublayer(h, w_query[l], sub_keys[l], expert_u[l], expert_v[l])
        h = layer_norm(DN_ALPHA * h + ffn, ln2_g[l], ln2_b[l])
    return h


_drawn_inputs = setup_inputs


def setup_inputs(seed=0):
    import zlib

    import numpy as np

    out = dict(_drawn_inputs(seed))
    spreads = {}
    factors = {'a_sinks': 4.608, 'b_norm_w': 3.216, 'ln2_g': 2.858, 'ln2_b': 2.874}
    for name, (base, spread) in spreads.items():
        noise = np.random.default_rng([zlib.crc32(name.encode()), seed]).standard_normal(out[name].shape)
        drawn = base * np.exp(spread * noise) if base else spread * noise
        out[name] = __import__('jax').numpy.asarray(drawn.astype(out[name].dtype))
    for name, factor in factors.items():
        out[name] = (out[name] * factor).astype(out[name].dtype)
    return out
```

```python
import concourse.bass as bass
from concourse import mybir
from contextlib import ExitStack
import numpy as np

P = 128
S = 1024
D = 1024
T = S // P
KD = D // P
CHUNK = 64
AH, AKV, AD = 8, 2, 64
BH, BD = 4, 128
TAPS = 4
PH, NK, TOPK = 8, 128, 16
SLOTS = PH * TOPK
NCQ = AH * AD // P
NCONV = 3 * BH
NZ = BH
IN_W = 2824
AV, CONV0, Z0 = NCQ, NCQ + 1, NCQ + 1 + NCONV
NPROJ = Z0 + NZ
PAIR_ROWS = [(0, 1, 16, 0), (1, 2, 8, 16), (2, 3, 5, 24), (3, 4, 4, 29), (4, 5, 3, 33), (5, 8, 2, 36), (8, 16, 1, 42)]
NCAND = 50
LEAST = -3.0e38
LN_EPS = 1e-5
NORM_EPS = 1e-6
ALPHA = 2.0 ** 0.25
NEG = -1.0e30

CONST_COLS = {}
_at = 0
for _name, _n in (("ident", P), ("upto", P), ("after", P), ("decay_mask", P), ("ones", P), ("chunk_of", 2 * P),
                  ("level", 6 * P), ("bias", AH * 192), ("bias_first", AH * 64), ("iota50", 50)):
    CONST_COLS[_name] = (_at, _at + _n)
    _at += _n
NCONST = _at


def constant_table():
    t = np.zeros((P, NCONST), np.float32)

    def put(name, a):
        lo, hi = CONST_COLS[name]
        t[:, lo:hi] = a.reshape(a.shape[0], -1)

    r = np.arange(P)
    same = (r[:, None] // CHUNK) == (r[None, :] // CHUNK)
    put("ident", np.eye(P, dtype=np.float32))
    put("upto", (same & (r[:, None] <= r[None, :])).astype(np.float32))
    put("after", (same & (r[:, None] > r[None, :])).astype(np.float32))
    put("decay_mask", np.where(same & (r[:, None] <= r[None, :]), 0.0, NEG).astype(np.float32))
    put("ones", np.ones((P, P), np.float32))
    put("chunk_of", np.stack([np.repeat((r // CHUNK == c)[:, None], P, 1) for c in range(2)], 1).astype(np.float32))
    lv = []
    for l in range(6):
        b = 1 << l
        j, i = r[:, None], r[None, :]
        lv.append((j // (2 * b) == i // (2 * b)) & (j % (2 * b) < b) & (i % (2 * b) >= b))
    put("level", np.stack(lv, 1).astype(np.float32))
    q = np.arange(P)[:, None]
    k = np.arange(192)[None, :] - 64
    qc, kc = q // 64, np.floor_divide(k, 64)
    ok = (kc == qc) | (kc == qc - 1)
    bias = np.zeros((P, AH, 192), np.float32)
    for h in range(AH):
        slope = np.float32(2.0 ** (-(h + 1)))
        bias[:, h] = np.where(ok, -slope * np.abs(q - k), NEG)
    put("bias", bias)
    put("bias_first", np.full((P, AH * 64), NEG, np.float32))
    put("iota50", np.tile(np.arange(50, dtype=np.float32)[None], (P, 1)))
    return t


def build(nc, consts, x, ln_in_g, ln_in_b, w_in, conv_w, a_sinks, b_a_log, b_dt_bias, b_norm_w, w_out,
          ln1_g, ln1_b, w_query, sub_keys, expert_u, expert_v, ln2_g, ln2_b, out):
    fp32, u32 = mybir.dt.float32, mybir.dt.uint32
    ALU, ACT, AX = mybir.AluOpType, mybir.ActivationFunctionType, mybir.AxisListType

    ctx = ExitStack()
    with ctx:
        def sb(name, shape, dt=fp32, c=ctx):
            return c.enter_context(nc.sbuf_tensor(name, shape, dt))

        scope = [ctx]

        def sem(name):
            return scope[0].enter_context(nc.semaphore(name))

        s_dve = sem("s_dve")
        s_act = sem("s_act")
        s_pool = sem("s_pool")

        C = sb("C", [P, NCONST])

        def const(name):
            lo, hi = CONST_COLS[name]
            return C[:, lo:hi]

        ident = const("ident")
        nhalf = sb("nhalf", [P, 8])
        hres = sb("hres", [P, T, D])
        banks = [ctx.enter_context(nc.psum_tensor(f"bank{i}", [P, 1024], fp32)) for i in range(4)]

        mix = ExitStack()
        hT = sb("hT", [P, KD, S], c=mix)
        proj_dram = nc.dram_tensor("proj_dram", (P, NPROJ, S), fp32).ap()
        ak_dram = nc.dram_tensor("ak_dram", (P, CHUNK + S), fp32).ap()
        gates = sb("gates", [P, 2, T, BH], c=mix)
        cw = sb("cw", [P, TAPS * NCONV + 1], c=mix)
        bc = sb("bc", [P, 2 * D], c=mix)

        a = ExitStack()
        scope[0] = a
        xin = sb("xin", [P, 2, D], c=a)
        wbuf = sb("wbuf", [P, 2, KD, P], c=a)
        ybuf = sb("ybuf", [P, 2, S], c=a)
        obuf = sb("obuf", [P, 2, S], c=a)
        zpad = sb("zpad", [P, CHUNK], c=a)
        st = sb("st", [P, 2, 18], c=a)
        wab = sb("wab", [P, KD, 8], c=a)
        abT = sb("abT", [8, S], c=a)
        cwr = sb("cwr", [TAPS * NCONV + 1, P], c=a)
        hb = sb("hb", [P, 2, BH], c=a)
        gt = sb("gt", [P, 6, T * BH], c=a)

        s_const = sem("s_const")
        s_small = sem("s_small")
        s_x = [sem(f"s_x{u}") for u in range(2)]
        s_stats = [sem(f"s_stats{u}") for u in range(2)]
        s_norm = [sem(f"s_norm{u}") for u in range(2)]
        s_h_pe = [sem(f"s_h_pe{u}") for u in range(2)]
        s_h_pool = [sem(f"s_h_pool{u}") for u in range(2)]
        s_hT_ps = [sem(f"s_hT_ps{u}") for u in range(2)]
        s_x_free = [sem(f"s_x_free{u}") for u in range(2)]
        s_tr_free = [sem(f"s_tr_free{u}") for u in range(2)]
        s_hT = sem("s_hT")
        s_w = [sem(f"s_w{u}") for u in range(2)]
        s_w_free = [sem(f"s_w_free{u}") for u in range(2)]
        s_proj = [sem(f"s_proj{u}") for u in range(2)]
        s_proj_free = [sem(f"s_proj_free{u}") for u in range(2)]
        s_tap0 = [sem(f"s_tap0{u}") for u in range(2)]
        s_conv = [sem(f"s_conv{u}") for u in range(2)]
        s_y_free = [sem(f"s_y_free{u}") for u in range(2)]
        s_cw_ps = sem("s_cw_ps")
        s_cw = sem("s_cw")
        s_ab_ps = sem("s_ab_ps")
        s_abT = sem("s_abT")
        s_ab_tok = sem("s_ab_tok")
        s_soft = sem("s_soft")
        s_soft2 = sem("s_soft2")
        s_pad = sem("s_pad")
        s_root_in = sem("s_root_in")
        s_root = sem("s_root")
        s_pad_out = sem("s_pad_out")
        s_stored = [sem(f"s_stored{u}") for u in range(2)]

        NTAP = TAPS * NCONV
        w_in_v = w_in[0].rearrange("(k p) e -> p k e", p=P)
        x_v = x[0].rearrange("(t p) d -> t p d", p=P)

        with nc.Block() as block:
            @block.sync
            def _(sp):
                sp.dma_start(C[:, :], consts).then_inc(s_const, 16)
                sp.dma_start(bc[:, 0:D], ln_in_g.partition_broadcast(P)).then_inc(s_small, 16)
                sp.dma_start(bc[:, D:2 * D], ln_in_b.partition_broadcast(P)).then_inc(s_small, 16)
                sp.dma_start(cwr[0:NTAP, :], conv_w[0].rearrange("t (c p) -> (t c) p", p=P)).then_inc(s_small, 16)
                sp.dma_start(cwr[NTAP:NTAP + 1, :], b_norm_w).then_inc(s_small, 16)
                sp.dma_start(hb[:, 0, :], b_dt_bias[0].partition_broadcast(P)).then_inc(s_small, 16)
                sp.dma_start(hb[:, 1, :], b_a_log[0].partition_broadcast(P)).then_inc(s_small, 16)
                sp.dma_start(wab[:, :, :], w_in_v[:, :, IN_W - 8:IN_W]).then_inc(s_small, 16)
                with sp.Fori(0, T // 2) as j:
                    for u in range(2):
                        sp.wait_ge(s_x_free[u], 2)
                        sp.sem_inc(s_x_free[u], -2)
                        sp.dma_start(xin[:, u, :], x_v[2 * j + u]).then_inc(s_x[u], 16)
                with sp.Fori(0, NCQ // 2) as j:
                    for u in range(2):
                        sp.wait_ge(s_w_free[u], 1)
                        sp.sem_inc(s_w_free[u], -1)
                        for half in range(2):
                            sp.dma_start(wbuf[:, u, :, 64 * half:64 * half + 64],
                                         w_in_v[:, :, bass.ds(j * 128 + u * 64 + 256 * half, 64)]).then_inc(s_w[u], 16)
                with sp.Fori(0, (2 + NCONV + NZ) // 2) as j:
                    for u in range(2):
                        sp.wait_ge(s_w_free[u], 1)
                        sp.sem_inc(s_w_free[u], -1)
                        sp.dma_start(wbuf[:, u, :, :],
                                     w_in_v[:, :, bass.ds(j * 256 + (NCQ + u) * P, P)]).then_inc(s_w[u], 16)

            @block.gpsimd
            def _(pool):
                nc.gpsimd.memset(zpad[:, :], 0.0).then_inc(s_pad, 1)
                nc.gpsimd.memset(nhalf[:, :], -0.5).then_inc(s_pool, 1)
                pool.wait_ge(s_pool, 1)
                pool.sem_inc(s_pool, -1)
                with pool.Fori(0, T // 2) as j:
                    for u in range(2):
                        pool.wait_ge(s_root_in, 1)
                        pool.sem_inc(s_root_in, -1)
                        nc.gpsimd.tensor_tensor(st[:, u, 14:15], st[:, u, 14:15], nhalf[:, 0:1], ALU.pow).then_inc(s_root, 1)
                        pool.wait_ge(s_h_pool[u], 1)
                        pool.sem_inc(s_h_pool[u], -1)
                        nc.gpsimd.tensor_copy(hres[:, 2 * j + u, :], xin[:, u, :]).then_inc(s_pool, 1)
                        pool.wait_ge(s_pool, 1)
                        pool.sem_inc(s_pool, -1)
                        pool.sem_inc(s_x_free[u], 1)

            @block.vector
            def _(dve):
                dve.wait_ge(s_small, 16 * 7)
                with dve.Fori(0, T // 2) as j:
                    for u in range(2):
                        dve.wait_ge(s_x[u], 16)
                        dve.sem_inc(s_x[u], -16)
                        for half in range(2):
                            nc.vector.bn_stats(st[:, u, 6 * half:6 * half + 6],
                                               xin[:, u, 512 * half:512 * half + 512]).then_inc(s_dve, 1)
                        dve.wait_ge(s_dve, 2)
                        dve.sem_inc(s_dve, -2)
                        nc.vector.bn_aggr(st[:, u, 12:14], st[:, u, 0:12]).then_inc(s_dve, 1)
                        dve.wait_ge(s_dve, 1)
                        dve.sem_inc(s_dve, -1)
                        nc.vector.tensor_scalar(st[:, u, 14:15], st[:, u, 13:14], LN_EPS, None, ALU.add).then_inc(s_root_in, 1)
                        dve.wait_ge(s_root, 1)
                        dve.sem_inc(s_root, -1)
                        nc.vector.tensor_scalar(st[:, u, 15:16], st[:, u, 12:13], st[:, u, 14:15], -1.0,
                                                ALU.mult, ALU.mult).then_inc(s_stats[u], 1)
                        dve.wait_ge(s_norm[u], 1)
                        dve.sem_inc(s_norm[u], -1)
                        nc.vector.tensor_tensor(xin[:, u, :], xin[:, u, :], bc[:, 0:D], ALU.mult).then_inc(s_dve, 1)
                        dve.wait_ge(s_dve, 1)
                        dve.sem_inc(s_dve, -1)
                        nc.vector.tensor_tensor(xin[:, u, :], xin[:, u, :], bc[:, D:2 * D], ALU.add).then_inc(s_dve, 1)
                        dve.wait_ge(s_dve, 1)
                        dve.sem_inc(s_dve, -1)
                        dve.sem_inc(s_h_pe[u], 1)
                        dve.sem_inc(s_h_pool[u], 1)
                dve.wait_ge(s_ab_tok, 1)
                dve.sem_inc(s_ab_tok, -1)
                tok = banks[3][:, 0:8 * T].rearrange("p (t g h) -> p t g h", g=2, h=BH)
                g4 = lambda i: gt[:, i, :].rearrange("p (t h) -> p t h", h=BH)
                nc.vector.tensor_tensor(g4(0), tok[:, :, 0, :], hb[:, 0, :].unsqueeze(1).to_broadcast([P, T, BH]),
                                        ALU.add).then_inc(s_dve, 1)
                dve.wait_ge(s_dve, 1)
                dve.sem_inc(s_dve, -1)
                nc.vector.scalar_tensor_tensor(gt[:, 1, :], gt[:, 0, :], -1.0, gt[:, 0, :], ALU.mult, ALU.min).then_inc(s_dve, 1)
                nc.vector.tensor_copy(g4(2), tok[:, :, 1, :]).then_inc(s_dve, 1)
                dve.wait_ge(s_dve, 2)
                dve.sem_inc(s_dve, -2)
                dve.sem_inc(s_soft, 1)
                dve.wait_ge(s_soft2, 1)
                dve.sem_inc(s_soft2, -1)
                nc.vector.tensor_scalar(gt[:, 4, :], gt[:, 3, :], 1.0, None, ALU.subtract).then_inc(s_dve, 1)
                dve.wait_ge(s_dve, 1)
                dve.sem_inc(s_dve, -1)
                nc.vector.tensor_scalar(gt[:, 5, :], gt[:, 4, :], 0.0, None, ALU.is_equal).then_inc(s_dve, 1)
                dve.wait_ge(s_dve, 1)
                dve.sem_inc(s_dve, -1)
                nc.vector.tensor_tensor(gt[:, 4, :], gt[:, 4, :], gt[:, 5, :], ALU.add).then_inc(s_dve, 1)
                dve.wait_ge(s_dve, 1)
                dve.sem_inc(s_dve, -1)
                nc.vector.reciprocal(gt[:, 4, :], gt[:, 4, :]).then_inc(s_dve, 1)
                dve.wait_ge(s_dve, 1)
                dve.sem_inc(s_dve, -1)
                nl = ybuf[:, 0, 0:T * BH]
                nc.vector.tensor_tensor(nl, nl, gt[:, 5, :], ALU.add).then_inc(s_dve, 1)
                dve.wait_ge(s_dve, 1)
                dve.sem_inc(s_dve, -1)
                nc.vector.tensor_tensor(nl, nl, gt[:, 4, :], ALU.mult).then_inc(s_dve, 1)
                dve.wait_ge(s_dve, 1)
                dve.sem_inc(s_dve, -1)
                nc.vector.tensor_tensor(nl, nl, gt[:, 1, :], ALU.mult).then_inc(s_dve, 1)
                dve.wait_ge(s_dve, 1)
                dve.sem_inc(s_dve, -1)
                nc.vector.scalar_tensor_tensor(gt[:, 0, :], gt[:, 0, :], 0.0, nl, ALU.max, ALU.add).then_inc(s_dve, 1)
                dve.wait_ge(s_dve, 1)
                dve.sem_inc(s_dve, -1)
                nc.vector.tensor_scalar(hb[:, 1, :], hb[:, 1, :], -1.0, None, ALU.mult).then_inc(s_dve, 1)
                dve.wait_ge(s_dve, 1)
                dve.sem_inc(s_dve, -1)
                nc.vector.tensor_tensor(gates[:, 0, :, :], g4(0), hb[:, 1, :].unsqueeze(1).to_broadcast([P, T, BH]),
                                        ALU.mult).then_inc(s_dve, 1)
                dve.wait_ge(s_dve, 1)
                dve.sem_inc(s_dve, -1)
                nc.vector.tensor_scalar(gt[:, 2, :], gt[:, 2, :], 1.0, None, ALU.add).then_inc(s_dve, 1)
                dve.wait_ge(s_dve, 1)
                dve.sem_inc(s_dve, -1)
                nc.vector.reciprocal(gates[:, 1, :, :].rearrange("p t h -> p (t h)"), gt[:, 2, :]).then_inc(s_dve, 1)
                dve.wait_ge(s_dve, 1)
                dve.sem_inc(s_dve, -1)
                dve.sem_inc(s_y_free[0], 1)
                dve.wait_ge(s_cw, 1)
                dve.sem_inc(s_cw, -1)
                with dve.Fori(0, NCONV // 2) as j:
                    for u in range(2):
                        ps = banks[u]
                        dve.wait_ge(s_tap0[u], 1)
                        dve.sem_inc(s_tap0[u], -1)
                        for back in range(1, TAPS):
                            nc.vector.scalar_tensor_tensor(
                       ybuf[:, u, back:S], ps[:, 0:S - back],
                       cw[:, bass.ds(2 * j + u + (TAPS - 1 - back) * NCONV, 1)],
                       ybuf[:, u, back:S], ALU.mult, ALU.add).then_inc(s_dve, 1)
                            dve.wait_ge(s_dve, 1)
                            dve.sem_inc(s_dve, -1)
                        dve.sem_inc(s_conv[u], 1)
                        dve.sem_inc(s_proj_free[u], 1)

            @block.tensor
            def _(pe):
                pe.wait_ge(s_const, 16)
                pe.sem_inc(s_const, -16)
                pe.wait_ge(s_small, 16 * 7)
                nc.tensor.transpose(banks[3][:, 512:512 + NTAP + 1], cwr[:, :], ident[0:NTAP + 1, 0:NTAP + 1]).then_inc(s_cw_ps, 1)
                with pe.Fori(0, T // 2) as j:
                    for u in range(2):
                        pe.wait_ge(s_h_pe[u], 1)
                        pe.sem_inc(s_h_pe[u], -1)
                        pe.wait_ge(s_tr_free[u], 1)
                        pe.sem_inc(s_tr_free[u], -1)
                        for k in range(KD):
                            last = nc.tensor.transpose(banks[u][:, k * P:(k + 1) * P], xin[:, u, k * P:(k + 1) * P], ident)
                        last.then_inc(s_hT_ps[u], 1)
                pe.wait_ge(s_hT, T)
                pe.sem_inc(s_hT, -T)
                for half in range(2):
                    for k in range(KD):
                        last = nc.tensor.matmul(banks[2][0:8, 512 * half:512 * half + 512], wab[:, k, :],
                                                hT[:, k, 512 * half:512 * half + 512], start=k == 0, stop=k == KD - 1)
                last.then_inc(s_ab_ps, 1)
                pe.wait_ge(s_abT, 1)
                pe.sem_inc(s_abT, -1)
                pe.wait_ge(s_tr_free[0], 1)
                pe.sem_inc(s_tr_free[0], -1)
                for t in range(T):
                    last = nc.tensor.transpose(banks[3][:, 8 * t:8 * t + 8], abT[:, t * P:(t + 1) * P], ident[0:8, 0:8])
                last.then_inc(s_ab_tok, 1)

                def project(u, parts):
                    pe.wait_ge(s_w[u], 16 * parts)
                    pe.sem_inc(s_w[u], -(16 * parts))
                    pe.wait_ge(s_proj_free[u], 1)
                    pe.sem_inc(s_proj_free[u], -1)
                    for half in range(2):
                        for k in range(KD):
                            last = nc.tensor.matmul(banks[u][:, 512 * half:512 * half + 512], wbuf[:, u, k, :],
                                                    hT[:, k, 512 * half:512 * half + 512], start=k == 0, stop=k == KD - 1)
                    last.then_inc(s_proj[u], 1)

                with pe.Fori(0, NCQ // 2) as j:
                    for u in range(2):
                        project(u, 2)
                with pe.Fori(0, (2 + NCONV + NZ) // 2) as j:
                    for u in range(2):
                        project(u, 1)

            @block.scalar
            def _(act):
                act.sem_inc(s_x_free[0], 2)
                act.sem_inc(s_x_free[1], 2)
                act.sem_inc(s_tr_free[0], 1)
                act.sem_inc(s_tr_free[1], 1)
                act.sem_inc(s_w_free[0], 1)
                act.sem_inc(s_w_free[1], 1)
                act.wait_ge(s_cw_ps, 1)
                act.sem_inc(s_cw_ps, -1)
                nc.scalar.copy(cw[:, :], banks[3][:, 512:512 + NTAP + 1]).then_inc(s_cw, 1)
                with act.Fori(0, T // 2) as j:
                    for u in range(2):
                        act.wait_ge(s_stats[u], 1)
                        act.sem_inc(s_stats[u], -1)
                        nc.scalar.activation(xin[:, u, :], xin[:, u, :], ACT.Identity, bias=st[:, u, 15:16],
                                             scale=st[:, u, 14:15]).then_inc(s_norm[u], 1)
                        act.wait_ge(s_hT_ps[u], 1)
                        act.sem_inc(s_hT_ps[u], -1)
                        nc.scalar.copy(hT[:, :, bass.ts(2 * j + u, P)],
                                       banks[u][:, :].rearrange("p (k n) -> p k n", n=P)).then_inc(s_act, 1)
                        act.wait_ge(s_act, 1)
                        act.sem_inc(s_act, -1)
                        act.sem_inc(s_tr_free[u], 1)
                        act.sem_inc(s_x_free[u], 1)
                        act.sem_inc(s_hT, 1)
                act.wait_ge(s_ab_ps, 1)
                act.sem_inc(s_ab_ps, -1)
                nc.scalar.copy(abT[:, :], banks[2][0:8, :]).then_inc(s_abT, 1)
                act.wait_ge(s_soft, 1)
                act.sem_inc(s_soft, -1)
                nl = ybuf[:, 0, 0:T * BH]
                nc.scalar.activation(gt[:, 1, :], gt[:, 1, :], ACT.Exp).then_inc(s_act, 1)
                nc.scalar.activation(gt[:, 2, :], gt[:, 2, :], ACT.Exp, scale=-1.0).then_inc(s_act, 1)
                nc.scalar.activation(hb[:, 1, :], hb[:, 1, :], ACT.Exp).then_inc(s_act, 1)
                act.wait_ge(s_act, 3)
                act.sem_inc(s_act, -3)
                nc.scalar.activation(gt[:, 3, :], gt[:, 1, :], ACT.Copy, bias=1.0).then_inc(s_act, 1)
                act.wait_ge(s_act, 1)
                act.sem_inc(s_act, -1)
                nc.scalar.activation(nl, gt[:, 3, :], ACT.Ln).then_inc(s_act, 1)
                act.wait_ge(s_act, 1)
                act.sem_inc(s_act, -1)
                act.sem_inc(s_soft2, 1)
                act.sem_inc(s_proj_free[0], 1)
                act.sem_inc(s_proj_free[1], 1)

                act.wait_ge(s_pad, 1)
                act.sem_inc(s_pad, -1)
                act.dma_start(ak_dram[:, 0:CHUNK], zpad[:, :]).then_inc(s_pad_out, 16)
                for u in range(2):
                    act.sem_inc(s_stored[u], 16)

                def store(u, dst):
                    act.wait_ge(s_act, 1)
                    act.sem_inc(s_act, -1)
                    act.dma_start(dst, obuf[:, u, :]).then_inc(s_stored[u], 16)

                def plain(u, dst):
                    act.wait_ge(s_proj[u], 1)
                    act.sem_inc(s_proj[u], -1)
                    act.wait_ge(s_stored[u], 16)
                    act.sem_inc(s_stored[u], -16)
                    nc.scalar.copy(obuf[:, u, :], banks[u][:, :]).then_inc(s_act, 1)
                    store(u, dst)
                    act.sem_inc(s_w_free[u], 1)
                    act.sem_inc(s_proj_free[u], 1)

                with act.Fori(0, NCQ // 2) as j:
                    for u in range(2):
                        plain(u, proj_dram[:, 2 * j + u, :])
                plain(0, ak_dram[:, CHUNK:CHUNK + S])
                plain(1, proj_dram[:, AV, :])
                act.wait_ge(s_y_free[0], 1)
                act.sem_inc(s_y_free[0], -1)
                with act.Fori(0, NCONV // 2) as j:
                    for u in range(2):
                        act.wait_ge(s_proj[u], 1)
                        act.sem_inc(s_proj[u], -1)
                        act.sem_inc(s_w_free[u], 1)
                        nc.scalar.activation(ybuf[:, u, :], banks[u][:, :], ACT.Copy,
                                             scale=cw[:, bass.ds(2 * j + u + (TAPS - 1) * NCONV, 1)]).then_inc(s_tap0[u], 1)
                        act.wait_ge(s_conv[u], 1)
                        act.sem_inc(s_conv[u], -1)
                        act.wait_ge(s_stored[u], 16)
                        act.sem_inc(s_stored[u], -16)
                        nc.scalar.activation(obuf[:, u, :], ybuf[:, u, :], ACT.Silu).then_inc(s_act, 1)
                        store(u, proj_dram[:, 2 * j + (CONV0 + u), :])
                with act.Fori(0, NZ // 2) as j:
                    for u in range(2):
                        act.wait_ge(s_proj[u], 1)
                        act.sem_inc(s_proj[u], -1)
                        act.sem_inc(s_w_free[u], 1)
                        nc.scalar.activation(ybuf[:, u, :], banks[u][:, :], ACT.Silu).then_inc(s_act, 1)
                        act.wait_ge(s_act, 1)
                        act.sem_inc(s_act, -1)
                        act.sem_inc(s_proj_free[u], 1)
                        act.wait_ge(s_stored[u], 16)
                        act.sem_inc(s_stored[u], -16)
                        nc.scalar.activation(obuf[:, u, :], ybuf[:, u, :], ACT.Copy,
                                             scale=cw[:, NTAP:NTAP + 1]).then_inc(s_act, 1)
                        store(u, proj_dram[:, 2 * j + (Z0 + u), :])
                for u in range(2):
                    act.wait_ge(s_stored[u], 16)
                    act.sem_inc(s_stored[u], -16)
                act.wait_ge(s_pad_out, 16)
                act.sem_inc(s_pad_out, -16)
        a.close()
        b = ExitStack()
        scope[0] = b
        NB = NPROJ
        raw = sb("raw", [P, NB, P], c=b)
        akt = sb("akt", [P, CHUNK + P], c=b)
        zt = raw[:, Z0:Z0 + NZ, :]
        vtok = sb("vtok", [P, 2, P], c=b)
        sq = sb("sq", [P, 8, P], c=b)
        sml = sb("sml", [P, 64], c=b)
        qk_tok = sb("qk_tok", [P, 12, P], c=b)
        qk_ch = sb("qk_ch", [P, 12, P], c=b)
        kdec = sb("kdec", [P, BH, P], c=b)
        kbe = sb("kbe", [P, BH, P], c=b)
        vb = sb("vb", [P, BH, P], c=b)
        gU = sb("gU", [P, BH, P], c=b)
        bI = sb("bI", [P, BH, P], c=b)
        DT = sb("DT", [P, BH, P], c=b)
        MT = sb("MT", [P, BH, P], c=b)
        ML = sb("ML", [P, 6, BH, P], c=b)
        intraT = sb("intraT", [P, BH, P], c=b)
        X = sb("X", [P, BH, P], c=b)
        XT = sb("XT", [P, BH, P], c=b)
        Pm = sb("Pm", [P, BH, P], c=b)
        wk = sb("wk", [P, 2, BH, P], c=b)
        vnew = sb("vnew", [P, BH, P], c=b)
        St = sb("St", [P, BH, P], c=b)
        sc = sb("sc", [P, BH, 192], c=b)
        pr = sb("pr", [P, BH, 256], c=b)
        prT = sb("prT", [P, 2 * BH, P], c=b)
        bias = sb("bias", [P, AH, 192], c=b)
        sink = sb("sink", [P, AH], c=b)
        nsink = sb("nsink", [P, AH], c=b)
        att = sb("att", [P, 8 * AH], c=b)
        ytok = sb("ytok", [P, AH * AD], c=b)
        on = sb("on", [P, BH, P], c=b)
        yT = sb("yT", [P, KD, P], c=b)
        pre = sb("pre", [P, D], c=b)
        stb = sb("stb", [P, 18], c=b)
        wo = hT

        g = [banks[1][:, 0:512], banks[1][:, 512:1024], banks[2][:, 0:512], banks[2][:, 512:1024]]
        m = [banks[3][:, 0:512], banks[3][:, 512:1024]]
        heads = lambda a: a.rearrange("p (h n) -> p h n", h=BH)
        SS, RS, EG = sml[:, 0:8], sml[:, 8:16], sml[:, 16:32]
        CO = sml[:, 32:56].rearrange("p (c h) -> p c h", h=BH)
        SO = sml[:, 56:60]
        e_gc, e_rest, e_last = EG[:, 0:4], EG[:, 4:8], EG[:, 8:16]
        MX, SE, DEN, RD = att[:, 0:8], att[:, 8:16], att[:, 16:24], att[:, 24:32]

        b_raw = sem("b_raw")
        b_ak_in = sem("b_ak_in")
        b_raw_free = sem("b_raw_free")
        b_bload = sem("b_bload")
        b_wo_in = sem("b_wo_in")
        b_tok_raw = sem("b_tok_raw")
        b_squared = sem("b_squared")
        b_sumsq = sem("b_sumsq")
        b_root = sem("b_root")
        b_tok_done = sem("b_tok_done")
        b_tokT = sem("b_tokT")
        b_qkch = sem("b_qkch")
        b_qkch_free = sem("b_qkch_free")
        b_gu = sem("b_gu")
        b_gates_ps = sem("b_gates_ps")
        b_gexp = sem("b_gexp")
        b_coef = sem("b_coef")
        b_kk = sem("b_kk")
        b_arg = sem("b_arg")
        b_decayed = sem("b_decayed")
        b_masked = sem("b_masked")
        b_levels = sem("b_levels")
        b_lvP0 = sem("b_lvP0")
        b_lvP = sem("b_lvP")
        b_lvPs = sem("b_lvPs")
        b_lvQ = sem("b_lvQ")
        b_lvX = sem("b_lvX")
        b_wk_ps = sem("b_wk_ps")
        b_wk_done = sem("b_wk_done")
        b_vps = sem("b_vps")
        b_vnew = sem("b_vnew")
        b_o_ds = sem("b_o_ds")
        b_state_used = sem("b_state_used")
        b_state = sem("b_state")
        b_o_done = sem("b_o_done")
        b_o_free = sem("b_o_free")
        b_on_ready = sem("b_on_ready")
        b_onT_ps = sem("b_onT_ps")
        b_yT_b = sem("b_yT_b")
        b_sc_ps = sem("b_sc_ps")
        b_sc_done = sem("b_sc_done")
        b_sc_s = sem("b_sc_s")
        b_pexp = sem("b_pexp")
        b_prT_ps = sem("b_prT_ps")
        b_prT_done = sem("b_prT_done")
        b_pv = sem("b_pv")
        b_ya = sem("b_ya")
        b_yaT_ps = sem("b_yaT_ps")
        b_yT_a = sem("b_yT_a")
        b_mix_ps = sem("b_mix_ps")
        b_pre_stats = sem("b_pre_stats")
        b_pre_norm = sem("b_pre_norm")
        b_h1 = sem("b_h1")
        b_att_free = sem("b_att_free")
        b_exp_s = sem("b_exp_s")
        b_bias_ok = sem("b_bias_ok")
        b_vt_ps = sem("b_vt_ps")
        b_vt = sem("b_vt")
        b_kv_root = sem("b_kv_root")
        b_kv_root_in = sem("b_kv_root_in")
        b_sin = sem("b_sin")
        b_osq = sem("b_osq")
        b_oroot = sem("b_oroot")
        b_oroot_in = sem("b_oroot_in")
        b_raw_q = sem("b_raw_q")
        b_raw_pe = sem("b_raw_pe")
        b_tok_free = sem("b_tok_free")
        b_end = sem("b_end")

        def bc3(a, n=P):
            return a.unsqueeze(2).to_broadcast([a.shape[0], a.shape[1], n])

        def per_head(a):
            return a.unsqueeze(1).to_broadcast([P, BH, P])

        with nc.Block() as block:
            @block.sync
            def _(sp):
                for half in range(2):
                    sp.dma_start(wo[:, 4 * half:4 * half + 4, :],
                                 w_out[0].rearrange("(k p) d -> p k d", p=P)[:, 4 * half:4 * half + 4, :]).then_inc(b_wo_in, 16)
                sp.dma_start(bc[:, 0:D], ln1_g[0].partition_broadcast(P)).then_inc(b_bload, 16)
                sp.dma_start(bc[:, D:2 * D], ln1_b[0].partition_broadcast(P)).then_inc(b_bload, 16)
                sp.dma_start(sink[:, :], a_sinks[0].partition_broadcast(P)).then_inc(b_bload, 16)
                with sp.Fori(0, T) as t:
                    sp.wait_ge(b_raw_free, 1)
                    sp.sem_inc(b_raw_free, -1)
                    sp.dma_start(raw[:, :, :], proj_dram[:, :, bass.ts(t, P)]).then_inc(b_raw, 16)
                    sp.dma_start(akt[:, :], ak_dram[:, bass.ds(t * P, CHUNK + P)]).then_inc(b_raw, 16)

            @block.gpsimd
            def _(pool):
                pool.sem_inc(b_raw_free, 1)
                nc.gpsimd.tensor_copy(bias[:, :, :], const("bias").rearrange("p (h k) -> p h k", h=AH)).then_inc(s_pool, 1)
                nc.gpsimd.memset(vtok[:, 1, :], 0.0).then_inc(s_pool, 1)
                nc.gpsimd.memset(pr[:, :, :], 0.0).then_inc(s_pool, 1)
                pool.wait_ge(s_pool, 3)
                pool.sem_inc(s_pool, -3)
                nc.gpsimd.tensor_copy(bias[:, :, 0:CHUNK], const("bias_first").rearrange("p (h k) -> p h k", h=AH)).then_inc(s_pool, 1)
                pool.wait_ge(s_pool, 1)
                pool.sem_inc(s_pool, -1)
                nc.gpsimd.memset(St[:, :, :], 0.0).then_inc(s_pool, 1)
                pool.wait_ge(s_pool, 1)
                pool.sem_inc(s_pool, -1)
                pool.sem_inc(b_bias_ok, 1)
                with pool.Fori(0, T) as t:
                    pool.wait_ge(b_kv_root_in, 1)
                    pool.sem_inc(b_kv_root_in, -1)
                    nc.gpsimd.tensor_tensor(RS, SS, nhalf[:, :], ALU.pow).then_inc(b_kv_root, 1)
                    pool.wait_ge(b_masked, 1)
                    pool.sem_inc(b_masked, -1)
                    for l in range(6):
                        nc.gpsimd.tensor_tensor(ML[:, l, :, :], MT[:, :, :], per_head(const("level")[:, l * P:(l + 1) * P]),
                                                ALU.mult).then_inc(b_levels, 1)
                    pool.wait_ge(b_sc_done, 2)
                    pool.sem_inc(b_sc_done, -2)
                    nc.gpsimd.tensor_copy(
              bias[:, :, 0:CHUNK], const("bias").rearrange("p (h k) -> p h k", h=AH)[:, :, 0:CHUNK]).then_inc(s_pool, 1)
                    pool.wait_ge(s_pool, 1)
                    pool.sem_inc(s_pool, -1)
                    pool.sem_inc(b_bias_ok, 1)
                    pool.wait_ge(b_oroot_in, 1)
                    pool.sem_inc(b_oroot_in, -1)
                    nc.gpsimd.tensor_tensor(SO, SO, nhalf[:, 0:BH], ALU.pow).then_inc(b_oroot, 1)
                    pool.wait_ge(b_pre_stats, 1)
                    pool.sem_inc(b_pre_stats, -1)
                    nc.gpsimd.tensor_tensor(stb[:, 14:15], stb[:, 14:15], nhalf[:, 0:1], ALU.pow).then_inc(b_pre_norm, 1)

            @block.tensor
            def _(pe):
                def scores(hh):
                    lo = 64 * hh
                    for i in range(4):
                        last = nc.tensor.matmul(banks[0][:, 256 * i:256 * i + 192], raw[lo:lo + 64, i, :],
                                                akt[lo:lo + 64, :], start=True, stop=True)
                    last.then_inc(b_sc_ps, 1)

                def turn_probs(hh):
                    pe.wait_ge(b_pexp, 1)
                    pe.sem_inc(b_pexp, -1)
                    for i in range(4):
                        for w in range(2):
                            last = nc.tensor.transpose(banks[0][:, (2 * i + w) * P:(2 * i + w + 1) * P],
                                                       pr[:, i, w * P:(w + 1) * P], ident)
                    last.then_inc(b_prT_ps, 1)

                def values(hh):
                    pe.wait_ge(b_prT_done, 1)
                    pe.sem_inc(b_prT_done, -1)
                    if hh == 0:
                        pe.wait_ge(b_vt, 1)
                        pe.sem_inc(b_vt, -1)
                    for i in range(4):
                        o = m[0][:, (4 * hh + i) * 64:(4 * hh + i + 1) * 64]
                        nc.tensor.matmul(o, prT[64:128, 2 * i, :], vtok[64:128, 1, 64 * hh:64 * hh + 64], start=True, stop=False)
                        last = nc.tensor.matmul(o, prT[:, 2 * i + 1, :], vtok[:, 0, 64 * hh:64 * hh + 64], start=False, stop=True)
                    last.then_inc(b_pv, 1)

                def level(l):
                    if l:
                        pe.wait_ge(b_lvX, 1)
                        pe.sem_inc(b_lvX, -1)
                    pe.wait_ge(b_levels, 1)
                    pe.sem_inc(b_levels, -1)
                    for h in range(BH):
                        last = nc.tensor.matmul(g[0][:, h * P:(h + 1) * P], ML[:, l, h, :], ident if l == 0 else X[:, h, :],
                                                start=True, stop=True)
                    last.then_inc(b_lvP if l else b_lvP0, 1)
                    if l == 0:
                        return
                    pe.wait_ge(b_lvPs, 1)
                    pe.sem_inc(b_lvPs, -1)
                    for h in range(BH):
                        if l < 5:
                            nc.tensor.matmul(g[1][:, h * P:(h + 1) * P], XT[:, h, :], Pm[:, h, :], start=True, stop=True)
                        last = nc.tensor.matmul(g[2][:, h * P:(h + 1) * P], Pm[:, h, :], XT[:, h, :], start=True, stop=True)
                    last.then_inc(b_lvQ, 1)

                pe.wait_ge(b_wo_in, 32)
                pe.sem_inc(b_wo_in, -32)
                with pe.Fori(0, T) as t:
                    pe.wait_ge(b_raw, 32)
                    pe.sem_inc(b_raw, -32)
                    for i in range(8):
                        last = nc.tensor.transpose(banks[1][:, i * P:(i + 1) * P], raw[:, CONV0 + i, :], ident)
                    for i in range(4):
                        last = nc.tensor.transpose(g[2][:, i * P:(i + 1) * P], raw[:, CONV0 + 8 + i, :], ident)
                    last.then_inc(b_tok_raw, 1)
                    nc.tensor.matmul(g[3][:, 0:4], const("upto"), gates[:, 0, t, :], start=True, stop=True)
                    nc.tensor.matmul(g[3][:, 4:8], const("after"), gates[:, 0, t, :], start=True, stop=True)
                    for c in range(2):
                        nc.tensor.matmul(g[3][:, 8 + 4 * c:12 + 4 * c], const("chunk_of")[:, c * P:(c + 1) * P],
                                         gates[:, 0, t, :], start=True, stop=True)
                    nc.tensor.transpose(g[3][:, 128:256], raw[:, AV, :], ident).then_inc(b_gates_ps, 1)
                    scores(0)
                    pe.wait_ge(b_tok_done, 1)
                    pe.sem_inc(b_tok_done, -1)
                    for i in range(8):
                        nc.tensor.transpose(banks[1][:, i * P:(i + 1) * P], qk_tok[:, i, :], ident)
                    for i in range(8, 12):
                        last = nc.tensor.transpose(g[2][:, (i - 8) * P:(i - 7) * P], qk_tok[:, i, :], ident)
                    last.then_inc(b_tokT, 1)
                    turn_probs(0)
                    pe.wait_ge(b_gu, 1)
                    pe.sem_inc(b_gu, -1)
                    nc.tensor.matmul(m[1], const("ones"), gU[:, :, :], start=True, stop=False)
                    nc.tensor.matmul(m[1], const("upto"), bc3(sml[:, 60:64]), start=False, stop=False)
                    nc.tensor.matmul(m[1], ident, per_head(const("decay_mask")), start=False, stop=True).then_inc(b_arg, 1)
                    pe.wait_ge(b_qkch, 1)
                    pe.sem_inc(b_qkch, -1)
                    for h in range(BH):
                        nc.tensor.matmul(g[0][:, h * P:(h + 1) * P], qk_ch[:, 8 + h, :], qk_ch[:, 8 + h, :], start=True, stop=True)
                        nc.tensor.matmul(g[1][:, h * P:(h + 1) * P], qk_ch[:, 8 + h, :], qk_ch[:, h, :], start=True, stop=True)
                    last = nc.tensor.matmul(g[2], const("after"), bI[:, :, :], start=True, stop=True)
                    last.then_inc(b_kk, 1)
                    values(0)
                    scores(1)
                    level(0)
                    turn_probs(1)
                    level(1)
                    values(1)
                    level(2)
                    pe.wait_ge(b_ya, 1)
                    pe.sem_inc(b_ya, -1)
                    for i in range(4):
                        last = nc.tensor.transpose(banks[0][:, i * P:(i + 1) * P], ytok[:, i * P:(i + 1) * P], ident)
                    last.then_inc(b_yaT_ps, 1)
                    level(3)
                    level(4)
                    level(5)
                    pe.wait_ge(b_lvX, 1)
                    pe.sem_inc(b_lvX, -1)
                    for h in range(BH):
                        nc.tensor.matmul(g[0][:, h * P:(h + 1) * P], XT[:, h, :], vb[:, h, :], start=True, stop=True)
                        last = nc.tensor.matmul(g[1][:, h * P:(h + 1) * P], kbe[:, h, :], XT[:, h, :], start=True, stop=True)
                    last.then_inc(b_wk_ps, 1)
                    pe.wait_ge(b_wk_done, 1)
                    pe.sem_inc(b_wk_done, -1)
                    for c in range(2):
                        lo = 64 * c
                        if c:
                            pe.wait_ge(b_state, 1)
                            pe.sem_inc(b_state, -1)
                        for h in range(BH):
                            last = nc.tensor.matmul(g[2][lo:lo + 64, h * P:(h + 1) * P], wk[:, 1, h, lo:lo + 64], St[:, h, :],
                                                    start=True, stop=True)
                        last.then_inc(b_vps, 1)
                        for h in range(BH):
                            nc.tensor.matmul(g[3][lo:lo + 64, h * P:(h + 1) * P], qk_ch[:, 4 + h, lo:lo + 64], St[:, h, :],
                                             start=True, stop=False, skip_group_check=True)
                            if h == 0:
                                pe.wait_ge(b_vnew, 1)
                                pe.sem_inc(b_vnew, -1)
                            nc.tensor.matmul(g[3][lo:lo + 64, h * P:(h + 1) * P], intraT[lo:lo + 64, h, lo:lo + 64],
                                             vnew[lo:lo + 64, h, :], start=False, stop=True, skip_group_check=True)
                        for h in range(BH):
                            last = nc.tensor.matmul(m[1][:, h * P:(h + 1) * P], kdec[lo:lo + 64, h, :], vnew[lo:lo + 64, h, :],
                                                    start=True, stop=True)
                        last.then_inc(b_o_ds, 1)
                    pe.wait_ge(b_on_ready, 1)
                    pe.sem_inc(b_on_ready, -1)
                    for i in range(4):
                        last = nc.tensor.transpose(g[0][:, i * P:(i + 1) * P], on[:, i, :], ident)
                    last.then_inc(b_onT_ps, 1)
                    pe.wait_ge(b_yT_b, 1)
                    pe.sem_inc(b_yT_b, -1)
                    pe.wait_ge(b_yT_a, 1)
                    pe.sem_inc(b_yT_a, -1)
                    for n in range(2):
                        for k in range(KD):
                            last = nc.tensor.matmul(banks[0][:, 512 * n:512 * n + 512], yT[:, k, :], wo[:, k, 512 * n:512 * n + 512],
                                                    start=k == 0, stop=k == KD - 1)
                    last.then_inc(b_mix_ps, 1)
                    pe.wait_ge(b_end, 1)
                    pe.sem_inc(b_end, -1)

            @block.scalar
            def _(act):
                def probs(hh):
                    act.wait_ge(b_sc_s, 1)
                    act.sem_inc(b_sc_s, -1)
                    for i in range(4):
                        h = 4 * hh + i
                        nc.scalar.activation(pr[:, i, CHUNK:CHUNK + 192], sc[:, i, :], ACT.Exp, bias=MX[:, h:h + 1],
                                             accum_out=DEN[:, h:h + 1]).then_inc(s_act, 1)
                    act.wait_ge(s_act, 4)
                    act.sem_inc(s_act, -4)
                    act.sem_inc(b_pexp, 1)
                    nc.scalar.activation(SE[:, 4 * hh:4 * hh + 4], SE[:, 4 * hh:4 * hh + 4], ACT.Exp).then_inc(s_act, 1)
                    act.wait_ge(s_act, 1)
                    act.sem_inc(s_act, -1)
                    act.sem_inc(b_exp_s, 1)

                def turned(hh):
                    act.wait_ge(b_prT_ps, 1)
                    act.sem_inc(b_prT_ps, -1)
                    nc.scalar.copy(prT[:, :, :].rearrange("p a n -> p (a n)"), banks[0][:, :]).then_inc(b_prT_done, 1)

                with act.Fori(0, T) as t:
                    act.wait_ge(b_tok_raw, 1)
                    act.sem_inc(b_tok_raw, -1)
                    nc.scalar.activation(sq[:, :, :].rearrange("p a n -> p (a n)"), banks[1][:, :], ACT.Square).then_inc(b_squared, 1)
                    act.wait_ge(b_gates_ps, 1)
                    act.sem_inc(b_gates_ps, -1)
                    nc.scalar.activation(EG, g[3][:, 0:16], ACT.Exp).then_inc(b_gexp, 1)
                    nc.scalar.copy(vtok[:, 0, :], g[3][:, 128:256]).then_inc(b_vt, 1)
                    probs(0)
                    act.wait_ge(b_tokT, 1)
                    act.sem_inc(b_tokT, -1)
                    nc.scalar.copy(qk_ch[:, 0:8, :].rearrange("p a n -> p (a n)"), banks[1][:, :]).then_inc(s_act, 1)
                    nc.scalar.copy(qk_ch[:, 8:12, :].rearrange("p a n -> p (a n)"), g[2]).then_inc(s_act, 1)
                    act.wait_ge(s_act, 2)
                    act.sem_inc(s_act, -2)
                    act.sem_inc(b_qkch, 1)
                    turned(0)
                    act.wait_ge(b_arg, 1)
                    act.sem_inc(b_arg, -1)
                    nc.scalar.activation(DT[:, :, :].rearrange("p a n -> p (a n)"), m[1], ACT.Exp).then_inc(b_decayed, 1)
                    probs(1)
                    turned(1)
                    for l in range(1, 6):
                        act.wait_ge(b_lvP, 1)
                        act.sem_inc(b_lvP, -1)
                        nc.scalar.copy(Pm[:, :, :].rearrange("p a n -> p (a n)"), g[0]).then_inc(b_lvPs, 1)
                        if l == 2:
                            act.wait_ge(b_yaT_ps, 1)
                            act.sem_inc(b_yaT_ps, -1)
                            nc.scalar.copy(yT[:, 0:4, :].rearrange("p a n -> p (a n)"), banks[0][:, 0:512]).then_inc(b_yT_a, 1)
                    act.wait_ge(b_wk_ps, 1)
                    act.sem_inc(b_wk_ps, -1)
                    nc.scalar.copy(wk[:, :, :, :].rearrange("p b a n -> p (b a n)"), banks[1][:, :]).then_inc(b_wk_done, 1)
                    act.wait_ge(b_o_done, 1)
                    act.sem_inc(b_o_done, -1)
                    nc.scalar.activation(on[:, :, :].rearrange("p a n -> p (a n)"), g[3], ACT.Square).then_inc(b_osq, 1)
                    act.wait_ge(b_h1, 1)
                    act.sem_inc(b_h1, -1)
                    nc.scalar.activation(pre[:, :], pre[:, :], ACT.Identity, bias=stb[:, 15:16], scale=stb[:, 14:15]).then_inc(s_act, 1)
                    act.wait_ge(s_act, 1)
                    act.sem_inc(s_act, -1)
                    act.sem_inc(b_pre_norm, 1)

            @block.vector
            def _(dve):
                def soften(hh):
                    dve.wait_ge(b_sc_ps, 1)
                    dve.sem_inc(b_sc_ps, -1)
                    if hh == 0:
                        dve.wait_ge(b_bias_ok, 1)
                        dve.sem_inc(b_bias_ok, -1)
                    nc.vector.scalar_tensor_tensor(
               sc[:, :, :], banks[0][:, :].rearrange("p (h k) -> p h k", k=256)[:, :, 0:192], float(AD) ** -0.5,
               bias[:, 4 * hh:4 * hh + 4, :], ALU.mult, ALU.add).then_inc(s_dve, 1)
                    dve.wait_ge(s_dve, 1)
                    dve.sem_inc(s_dve, -1)
                    dve.sem_inc(b_sc_done, 1)
                    mx = MX[:, 4 * hh:4 * hh + 4]
                    nc.vector.reduce_max(mx, sc[:, :, :], AX.X).then_inc(s_dve, 1)
                    dve.wait_ge(s_dve, 1)
                    dve.sem_inc(s_dve, -1)
                    nc.vector.tensor_tensor(mx, mx, sink[:, 4 * hh:4 * hh + 4], ALU.max).then_inc(s_dve, 1)
                    dve.wait_ge(s_dve, 1)
                    dve.sem_inc(s_dve, -1)
                    nc.vector.tensor_scalar(mx, mx, -1.0, None, ALU.mult).then_inc(s_dve, 1)
                    dve.wait_ge(s_dve, 1)
                    dve.sem_inc(s_dve, -1)
                    nc.vector.tensor_tensor(SE[:, 4 * hh:4 * hh + 4], sink[:, 4 * hh:4 * hh + 4], mx, ALU.add).then_inc(s_dve, 1)
                    dve.wait_ge(s_dve, 1)
                    dve.sem_inc(s_dve, -1)
                    dve.sem_inc(b_sc_s, 1)

                def divide(hh):
                    dve.wait_ge(b_exp_s, 1)
                    dve.sem_inc(b_exp_s, -1)
                    d, r = DEN[:, 4 * hh:4 * hh + 4], RD[:, 4 * hh:4 * hh + 4]
                    nc.vector.tensor_tensor(d, d, SE[:, 4 * hh:4 * hh + 4], ALU.add).then_inc(s_dve, 1)
                    dve.wait_ge(s_dve, 1)
                    dve.sem_inc(s_dve, -1)
                    nc.vector.reciprocal(r, d).then_inc(s_dve, 1)
                    dve.wait_ge(s_dve, 1)
                    dve.sem_inc(s_dve, -1)
                    dve.wait_ge(b_pv, 1)
                    dve.sem_inc(b_pv, -1)
                    nc.vector.tensor_tensor(ytok[:, 256 * hh:256 * hh + 256].rearrange("p (h d) -> p h d", d=AD),
                                            m[0][:, 256 * hh:256 * hh + 256].rearrange("p (h d) -> p h d", d=AD),
                                            bc3(r, AD), ALU.mult).then_inc(s_dve, 1)
                    dve.wait_ge(s_dve, 1)
                    dve.sem_inc(s_dve, -1)

                def grow(l):
                    if l == 0:
                        dve.wait_ge(b_lvP0, 1)
                        dve.sem_inc(b_lvP0, -1)
                        nc.vector.tensor_tensor(X[:, :, :], per_head(ident), heads(g[0]), ALU.subtract).then_inc(s_dve, 1)
                        nc.vector.tensor_tensor(XT[:, :, :], per_head(ident), ML[:, 0, :, :], ALU.subtract).then_inc(s_dve, 1)
                        dve.wait_ge(s_dve, 2)
                        dve.sem_inc(s_dve, -2)
                    else:
                        dve.wait_ge(b_lvQ, 1)
                        dve.sem_inc(b_lvQ, -1)
                        if l < 5:
                            nc.vector.tensor_tensor(X[:, :, :], X[:, :, :], heads(g[1]), ALU.subtract).then_inc(s_dve, 1)
                        nc.vector.tensor_tensor(XT[:, :, :], XT[:, :, :], heads(g[2]), ALU.subtract).then_inc(s_dve, 1)
                        dve.wait_ge(s_dve, 2 if l < 5 else 1)
                        dve.sem_inc(s_dve, -(2 if l < 5 else 1))
                    dve.sem_inc(b_lvX, 1)

                dve.wait_ge(b_bload, 48)
                with dve.Fori(0, T) as t:
                    beta = gates[:, 1, t, :]
                    dve.wait_ge(b_squared, 1)
                    dve.sem_inc(b_squared, -1)
                    nc.vector.reduce_sum(SS, sq[:, :, :], AX.X).then_inc(s_dve, 1)
                    dve.wait_ge(s_dve, 1)
                    dve.sem_inc(s_dve, -1)
                    nc.vector.tensor_scalar(SS, SS, NORM_EPS, None, ALU.add).then_inc(s_dve, 1)
                    dve.wait_ge(s_dve, 1)
                    dve.sem_inc(s_dve, -1)
                    dve.sem_inc(b_kv_root_in, 1)
                    nc.vector.tensor_tensor(gU[:, :, :], per_head(const("upto")), bc3(gates[:, 0, t, :]), ALU.mult).then_inc(s_dve, 1)
                    nc.vector.tensor_tensor(bI[:, :, :], per_head(ident), bc3(beta), ALU.mult).then_inc(s_dve, 1)
                    nc.vector.tensor_scalar(sml[:, 60:64], gates[:, 0, t, :], -1.0, None, ALU.mult).then_inc(s_dve, 1)
                    dve.wait_ge(s_dve, 3)
                    dve.sem_inc(s_dve, -3)
                    dve.sem_inc(b_gu, 1)
                    soften(0)
                    dve.wait_ge(b_kv_root, 1)
                    dve.sem_inc(b_kv_root, -1)
                    dve.wait_ge(b_gexp, 1)
                    dve.sem_inc(b_gexp, -1)
                    nc.vector.tensor_scalar(CO[:, 0, :], RS[:, 0:4], float(BD) ** -0.5, None, ALU.mult).then_inc(s_dve, 1)
                    nc.vector.tensor_scalar(CO[:, 2, :], RS[:, 4:8], 1.0, None, ALU.mult).then_inc(s_dve, 1)
                    nc.vector.tensor_tensor(CO[:, 3, :], RS[:, 4:8], e_rest, ALU.mult).then_inc(s_dve, 1)
                    nc.vector.tensor_tensor(CO[:, 4, :], RS[:, 4:8], e_gc, ALU.mult).then_inc(s_dve, 1)
                    dve.wait_ge(s_dve, 4)
                    dve.sem_inc(s_dve, -4)
                    nc.vector.tensor_tensor(CO[:, 1, :], CO[:, 0, :], e_gc, ALU.mult).then_inc(s_dve, 1)
                    nc.vector.tensor_tensor(CO[:, 4, :], CO[:, 4, :], beta, ALU.mult).then_inc(s_dve, 1)
                    dve.wait_ge(s_dve, 2)
                    dve.sem_inc(s_dve, -2)
                    q_ps, k_ps, v_ps = heads(g[0]), heads(g[1]), heads(g[2])
                    for dst, src, i in ((qk_tok[:, 0:4, :], q_ps, 0), (qk_tok[:, 4:8, :], q_ps, 1), (qk_tok[:, 8:12, :], k_ps, 2),
                                        (kdec[:, :, :], k_ps, 3), (kbe[:, :, :], k_ps, 4)):
                        nc.vector.tensor_tensor(dst, src, bc3(CO[:, i, :]), ALU.mult).then_inc(s_dve, 1)
                    nc.vector.tensor_tensor(vb[:, :, :], v_ps, bc3(beta), ALU.mult).then_inc(s_dve, 1)
                    dve.wait_ge(s_dve, 6)
                    dve.sem_inc(s_dve, -6)
                    dve.sem_inc(b_tok_done, 1)
                    divide(0)
                    dve.wait_ge(b_decayed, 1)
                    dve.sem_inc(b_decayed, -1)
                    dve.wait_ge(b_kk, 1)
                    dve.sem_inc(b_kk, -1)
                    nc.vector.tensor_tensor(MT[:, :, :], DT[:, :, :], heads(g[2]), ALU.mult).then_inc(s_dve, 1)
                    dve.wait_ge(s_dve, 1)
                    dve.sem_inc(s_dve, -1)
                    nc.vector.tensor_tensor(MT[:, :, :], MT[:, :, :], heads(g[0]), ALU.mult).then_inc(s_dve, 1)
                    dve.wait_ge(s_dve, 1)
                    dve.sem_inc(s_dve, -1)
                    dve.sem_inc(b_masked, 1)
                    nc.vector.tensor_tensor(intraT[:, :, :], DT[:, :, :], heads(g[1]), ALU.mult).then_inc(s_dve, 1)
                    dve.wait_ge(s_dve, 1)
                    dve.sem_inc(s_dve, -1)
                    soften(1)
                    grow(0)
                    grow(1)
                    divide(1)
                    dve.sem_inc(b_ya, 1)
                    for l in range(2, 6):
                        grow(l)
                    for c in range(2):
                        lo = 64 * c
                        dve.wait_ge(b_vps, 1)
                        dve.sem_inc(b_vps, -1)
                        nc.vector.tensor_tensor(vnew[lo:lo + 64, :, :], wk[lo:lo + 64, 0, :, :], heads(g[2])[lo:lo + 64], ALU.subtract).then_inc(b_vnew, 1)
                        dve.wait_ge(b_o_ds, 1)
                        dve.sem_inc(b_o_ds, -1)
                        nc.vector.tensor_tensor(St[:, :, :], St[:, :, :], bc3(e_last[:, 4 * c:4 * c + 4]), ALU.mult).then_inc(s_dve, 1)
                        dve.wait_ge(s_dve, 1)
                        dve.sem_inc(s_dve, -1)
                        nc.vector.tensor_tensor(St[:, :, :], St[:, :, :], heads(m[1]), ALU.add).then_inc(s_dve, 1)
                        dve.wait_ge(s_dve, 1)
                        dve.sem_inc(s_dve, -1)
                        if c == 0:
                            dve.sem_inc(b_state, 1)
                    dve.sem_inc(b_o_done, 1)
                    dve.wait_ge(b_osq, 1)
                    dve.sem_inc(b_osq, -1)
                    nc.vector.reduce_sum(SO, on[:, :, :], AX.X).then_inc(s_dve, 1)
                    dve.wait_ge(s_dve, 1)
                    dve.sem_inc(s_dve, -1)
                    nc.vector.tensor_scalar(SO, SO, 1.0 / BD, NORM_EPS, ALU.mult, ALU.add).then_inc(s_dve, 1)
                    dve.wait_ge(s_dve, 1)
                    dve.sem_inc(s_dve, -1)
                    dve.sem_inc(b_oroot_in, 1)
                    dve.wait_ge(b_oroot, 1)
                    dve.sem_inc(b_oroot, -1)
                    nc.vector.tensor_tensor(on[:, :, :], heads(g[3]), bc3(SO), ALU.mult).then_inc(s_dve, 1)
                    dve.wait_ge(s_dve, 1)
                    dve.sem_inc(s_dve, -1)
                    dve.sem_inc(b_on_ready, 1)
                    dve.wait_ge(b_onT_ps, 1)
                    dve.sem_inc(b_onT_ps, -1)
                    nc.vector.tensor_tensor(yT[:, 4:8, :], zt, heads(g[0]), ALU.mult).then_inc(b_yT_b, 1)
                    nc.vector.tensor_copy(vtok[:, 1, :], vtok[:, 0, :]).then_inc(s_dve, 1)
                    dve.wait_ge(s_dve, 1)
                    dve.sem_inc(s_dve, -1)
                    dve.wait_ge(b_mix_ps, 1)
                    dve.sem_inc(b_mix_ps, -1)
                    dve.sem_inc(b_raw_free, 1)
                    nc.vector.scalar_tensor_tensor(pre[:, :], hres[:, t, :], ALPHA, banks[0][:, :], ALU.mult, ALU.add).then_inc(s_dve, 1)
                    dve.wait_ge(s_dve, 1)
                    dve.sem_inc(s_dve, -1)
                    for half in range(2):
                        nc.vector.bn_stats(stb[:, 6 * half:6 * half + 6], pre[:, 512 * half:512 * half + 512]).then_inc(s_dve, 1)
                    dve.wait_ge(s_dve, 2)
                    dve.sem_inc(s_dve, -2)
                    nc.vector.bn_aggr(stb[:, 12:14], stb[:, 0:12]).then_inc(s_dve, 1)
                    dve.wait_ge(s_dve, 1)
                    dve.sem_inc(s_dve, -1)
                    nc.vector.tensor_scalar(stb[:, 14:15], stb[:, 13:14], LN_EPS, None, ALU.add).then_inc(s_dve, 1)
                    dve.wait_ge(s_dve, 1)
                    dve.sem_inc(s_dve, -1)
                    dve.sem_inc(b_pre_stats, 1)
                    dve.wait_ge(b_pre_norm, 1)
                    dve.sem_inc(b_pre_norm, -1)
                    nc.vector.tensor_scalar(stb[:, 15:16], stb[:, 12:13], stb[:, 14:15], -1.0, ALU.mult, ALU.mult).then_inc(s_dve, 1)
                    dve.wait_ge(s_dve, 1)
                    dve.sem_inc(s_dve, -1)
                    dve.sem_inc(b_h1, 1)
                    dve.wait_ge(b_pre_norm, 1)
                    dve.sem_inc(b_pre_norm, -1)
                    nc.vector.tensor_tensor(pre[:, :], pre[:, :], bc[:, 0:D], ALU.mult).then_inc(s_dve, 1)
                    dve.wait_ge(s_dve, 1)
                    dve.sem_inc(s_dve, -1)
                    nc.vector.tensor_tensor(hres[:, t, :], pre[:, :], bc[:, D:2 * D], ALU.add).then_inc(s_dve, 1)
                    dve.wait_ge(s_dve, 1)
                    dve.sem_inc(s_dve, -1)
                    dve.sem_inc(b_end, 1)
        b.close()
        mix.close()
        eidx = sb("eidx", [P, T, SLOTS], u32)
        egate = sb("egate", [P, T, SLOTS])
        c_ = ExitStack()
        scope[0] = c_
        wq = sb("wq", [P, KD, 2 * PH * P], c=c_)
        skT = sb("skT", [P, 2 * PH, P], c=c_)
        skr = sb("skr", [P, 2 * PH, P], c=c_)
        h1s = sb("h1s", [P, D], c=c_)
        h1T = sb("h1T", [P, KD, P], c=c_)
        qT = sb("qT", [P, 2 * PH, P], c=c_)
        rest = sb("rest", [P, 2 * PH, NK], c=c_)
        top = sb("top", [P, 2 * PH, TOPK], c=c_)
        itop = sb("itop", [P, 2 * PH, TOPK], u32, c=c_)
        ftop = sb("ftop", [P, PH, 2, TOPK], c=c_)
        cand = sb("cand", [P, PH, NCAND], c=c_)
        cid = sb("cid", [P, PH, NCAND], c=c_)
        crest = sb("crest", [P, PH, NCAND], c=c_)
        best = sb("best", [P, PH, TOPK], c=c_)
        ibest = sb("ibest", [P, PH, TOPK], u32, c=c_)
        fbest = sb("fbest", [P, PH, TOPK], c=c_)
        eq = sb("eq", [P, 2, TOPK, NCAND], c=c_)
        fex = sb("fex", [P, PH, TOPK], c=c_)
        den = sb("den", [P, 2, PH], c=c_)
        r_wq = sem("r_wq")
        r_sk = sem("r_sk")
        r_sk_ps = sem("r_sk_ps")
        r_skT = sem("r_skT")
        r_h1s = sem("r_h1s")
        r_h1s_free = sem("r_h1s_free")
        r_h1T_ps = sem("r_h1T_ps")
        r_h1T = sem("r_h1T")
        r_q_ps = sem("r_q_ps")
        r_qT = sem("r_qT")
        r_scores = sem("r_scores")
        r_scored = sem("r_scored")
        r_soft = sem("r_soft")
        r_exped = sem("r_exped")
        score_bank = lambda hp: (banks[0] if hp < 8 else banks[3])[:, (hp % 8) * P:(hp % 8 + 1) * P]
        with nc.Block() as block:
            @block.sync
            def _(sp):
                sp.dma_start(skr[:, :, :], sub_keys[0].rearrange("h q n d -> n (h q) d")).then_inc(r_sk, 16)
                wq_v = w_query[0].rearrange("(k p) e -> p k e", p=P)
                for i in range(4):
                    sp.dma_start(wq[:, 2 * i:2 * i + 2, :], wq_v[:, 2 * i:2 * i + 2, :]).then_inc(r_wq, 16)

            @block.tensor
            def _(pe):
                pe.wait_ge(r_sk, 16)
                pe.sem_inc(r_sk, -16)
                for half in range(2):
                    for i in range(8):
                        last = nc.tensor.transpose(banks[1 + half][:, i * P:(i + 1) * P], skr[:, 8 * half + i, :], ident)
                    last.then_inc(r_sk_ps, 1)
                pe.wait_ge(r_skT, 1)
                pe.sem_inc(r_skT, -1)
                pe.wait_ge(r_wq, 64)
                pe.sem_inc(r_wq, -64)
                with pe.Fori(0, T) as t:
                    pe.wait_ge(r_h1s, 1)
                    pe.sem_inc(r_h1s, -1)
                    pe.wait_ge(r_scored, 1)
                    pe.sem_inc(r_scored, -1)
                    for k in range(KD):
                        last = nc.tensor.transpose(banks[0][:, k * P:(k + 1) * P], h1s[:, k * P:(k + 1) * P], ident)
                    last.then_inc(r_h1T_ps, 1)
                    pe.wait_ge(r_h1T, 1)
                    pe.sem_inc(r_h1T, -1)
                    for half in range(2):
                        for i in range(8):
                            for k in range(KD):
                                last = nc.tensor.matmul(banks[1 + half][:, i * P:(i + 1) * P],
                                                        wq[:, k, (8 * half + i) * P:(8 * half + i + 1) * P],
                                                        h1T[:, k, :], start=k == 0, stop=k == KD - 1)
                        last.then_inc(r_q_ps, 1)
                    pe.wait_ge(r_qT, 1)
                    pe.sem_inc(r_qT, -1)
                    for hp in range(2 * PH):
                        last = nc.tensor.matmul(score_bank(hp), qT[:, hp, :], skT[:, hp, :], start=True, stop=True)
                    last.then_inc(r_scores, 1)

            @block.scalar
            def _(act):
                for half in range(2):
                    act.wait_ge(r_sk_ps, 1)
                    act.sem_inc(r_sk_ps, -1)
                    nc.scalar.copy(skT[:, 8 * half:8 * half + 8, :].rearrange("p a n -> p (a n)"), banks[1 + half][:, :]).then_inc(s_act, 1)
                    act.wait_ge(s_act, 1)
                    act.sem_inc(s_act, -1)
                act.sem_inc(r_skT, 1)
                with act.Fori(0, T) as t:
                    nc.scalar.copy(h1s[:, :], hres[:, t, :]).then_inc(r_h1s, 1)
                    act.wait_ge(r_h1T_ps, 1)
                    act.sem_inc(r_h1T_ps, -1)
                    nc.scalar.copy(h1T[:, :, :].rearrange("p a n -> p (a n)"), banks[0][:, :]).then_inc(r_h1T, 1)
                    for half in range(2):
                        act.wait_ge(r_q_ps, 1)
                        act.sem_inc(r_q_ps, -1)
                        nc.scalar.copy(qT[:, 8 * half:8 * half + 8, :].rearrange("p a n -> p (a n)"), banks[1 + half][:, :]).then_inc(s_act, 1)
                        act.wait_ge(s_act, 1)
                        act.sem_inc(s_act, -1)
                    act.sem_inc(r_qT, 1)
                    act.wait_ge(r_soft, 1)
                    act.sem_inc(r_soft, -1)
                    nc.scalar.activation(best[:, :, :], best[:, :, :], ACT.Exp).then_inc(r_exped, 1)

            @block.vector
            def _(dve):
                dve.sem_inc(r_scored, 1)
                with dve.Fori(0, T) as t:
                    dve.wait_ge(r_scores, 1)
                    dve.sem_inc(r_scores, -1)
                    for hp in range(2 * PH):
                        nc.vector.max(top[:, hp, 0:8], score_bank(hp)).then_inc(s_dve, 1)
                    dve.wait_ge(s_dve, 2 * PH)
                    dve.sem_inc(s_dve, -(2 * PH))
                    for hp in range(2 * PH):
                        nc.vector.max_index(itop[:, hp, 0:8], top[:, hp, 0:8], score_bank(hp)).then_inc(s_dve, 1)
                        nc.vector.match_replace(rest[:, hp, :], top[:, hp, 0:8], score_bank(hp), LEAST).then_inc(s_dve, 1)
                    dve.wait_ge(s_dve, 4 * PH)
                    dve.sem_inc(s_dve, -(4 * PH))
                    dve.sem_inc(r_scored, 1)
                    for hp in range(2 * PH):
                        nc.vector.max(top[:, hp, 8:16], rest[:, hp, :]).then_inc(s_dve, 1)
                    dve.wait_ge(s_dve, 2 * PH)
                    dve.sem_inc(s_dve, -(2 * PH))
                    for hp in range(2 * PH):
                        nc.vector.max_index(itop[:, hp, 8:16], top[:, hp, 8:16], rest[:, hp, :]).then_inc(s_dve, 1)
                    dve.wait_ge(s_dve, 2 * PH)
                    dve.sem_inc(s_dve, -(2 * PH))
                    nc.vector.tensor_copy(ftop[:, :, :, :].rearrange("p h q k -> p (h q k)"),
                                          itop[:, :, :].rearrange("p a k -> p (a k)")).then_inc(s_dve, 1)
                    dve.wait_ge(s_dve, 1)
                    dve.sem_inc(s_dve, -1)
                    nc.vector.tensor_scalar(ftop[:, :, 0, :], ftop[:, :, 0, :], float(NK), None, ALU.mult).then_inc(s_dve, 1)
                    dve.wait_ge(s_dve, 1)
                    dve.sem_inc(s_dve, -1)
                    tv = top[:, :, :].rearrange("p (h q) k -> p h q k", q=2)
                    for dst, src in ((cand, tv), (cid, ftop)):
                        for i0, i1, w, at in PAIR_ROWS:
                            o = dst[:, :, at:at + (i1 - i0) * w].rearrange("p h (i j) -> p h i j", j=w)
                            nc.vector.tensor_tensor(o, src[:, :, 0, i0:i1].unsqueeze(3).to_broadcast([P, PH, i1 - i0, w]),
                                                    src[:, :, 1, 0:w].unsqueeze(2).to_broadcast([P, PH, i1 - i0, w]),
                                                    ALU.add).then_inc(s_dve, 1)
                    dve.wait_ge(s_dve, 2 * len(PAIR_ROWS))
                    dve.sem_inc(s_dve, -(2 * len(PAIR_ROWS)))
                    for h in range(PH):
                        nc.vector.max(best[:, h, 0:8], cand[:, h, :]).then_inc(s_dve, 1)
                    dve.wait_ge(s_dve, PH)
                    dve.sem_inc(s_dve, -PH)
                    for h in range(PH):
                        nc.vector.max_index(ibest[:, h, 0:8], best[:, h, 0:8], cand[:, h, :]).then_inc(s_dve, 1)
                        nc.vector.match_replace(crest[:, h, :], best[:, h, 0:8], cand[:, h, :], LEAST).then_inc(s_dve, 1)
                    dve.wait_ge(s_dve, 2 * PH)
                    dve.sem_inc(s_dve, -(2 * PH))
                    for h in range(PH):
                        nc.vector.max(best[:, h, 8:16], crest[:, h, :]).then_inc(s_dve, 1)
                    dve.wait_ge(s_dve, PH)
                    dve.sem_inc(s_dve, -PH)
                    for h in range(PH):
                        nc.vector.max_index(ibest[:, h, 8:16], best[:, h, 8:16], crest[:, h, :]).then_inc(s_dve, 1)
                    dve.wait_ge(s_dve, PH)
                    dve.sem_inc(s_dve, -PH)
                    nc.vector.tensor_copy(fbest[:, :, :], ibest[:, :, :]).then_inc(s_dve, 1)
                    dve.wait_ge(s_dve, 1)
                    dve.sem_inc(s_dve, -1)
                    nc.vector.tensor_copy(den[:, 0, :], best[:, :, 0]).then_inc(s_dve, 1)
                    dve.wait_ge(s_dve, 1)
                    dve.sem_inc(s_dve, -1)
                    nc.vector.tensor_tensor(best[:, :, :], best[:, :, :], den[:, 0, :].unsqueeze(2).to_broadcast([P, PH, TOPK]),
                                            ALU.subtract).then_inc(s_dve, 1)
                    dve.wait_ge(s_dve, 1)
                    dve.sem_inc(s_dve, -1)
                    dve.sem_inc(r_soft, 1)
                    for h in range(PH):
                        e = eq[:, h % 2, :, :]
                        nc.vector.tensor_tensor(e, const("iota50").unsqueeze(1).to_broadcast([P, TOPK, NCAND]),
                                                fbest[:, h, :].unsqueeze(2).to_broadcast([P, TOPK, NCAND]), ALU.is_equal).then_inc(s_dve, 1)
                        dve.wait_ge(s_dve, 1)
                        dve.sem_inc(s_dve, -1)
                        nc.vector.tensor_tensor(e, e, cid[:, h, :].unsqueeze(1).to_broadcast([P, TOPK, NCAND]), ALU.mult).then_inc(s_dve, 1)
                        dve.wait_ge(s_dve, 1)
                        dve.sem_inc(s_dve, -1)
                        nc.vector.reduce_sum(fex[:, h, :], e, AX.X).then_inc(s_dve, 1)
                        dve.wait_ge(s_dve, 1)
                        dve.sem_inc(s_dve, -1)
                    nc.vector.tensor_copy(eidx[:, t, :], fex[:, :, :].rearrange("p h k -> p (h k)")).then_inc(s_dve, 1)
                    dve.wait_ge(s_dve, 1)
                    dve.sem_inc(s_dve, -1)
                    dve.wait_ge(r_exped, 1)
                    dve.sem_inc(r_exped, -1)
                    nc.vector.reduce_sum(den[:, 0, :], best[:, :, :], AX.X).then_inc(s_dve, 1)
                    dve.wait_ge(s_dve, 1)
                    dve.sem_inc(s_dve, -1)
                    nc.vector.reciprocal(den[:, 1, :], den[:, 0, :]).then_inc(s_dve, 1)
                    dve.wait_ge(s_dve, 1)
                    dve.sem_inc(s_dve, -1)
                    nc.vector.tensor_tensor(egate[:, t, :].rearrange("p (h k) -> p h k", h=PH), best[:, :, :],
                                            den[:, 1, :].unsqueeze(2).to_broadcast([P, PH, TOPK]), ALU.mult).then_inc(s_dve, 1)
                    dve.wait_ge(s_dve, 1)
                    dve.sem_inc(s_dve, -1)
        c_.close()

        d_ = ExitStack()
        scope[0] = d_
        G = 8
        NG = SLOTS // G
        U = sb("U", [P, G, D], c=d_)
        V = sb("V", [P, G, D], c=d_)
        ixu = sb("ixu", [P, 2, G], u32, c=d_)
        ixv = sb("ixv", [P, 2, G], u32, c=d_)
        dots = sb("dots", [P, 2, G], c=d_)
        gl = sb("gl", [P, 2, G], c=d_)
        acc = sb("acc", [P, 2, D], c=d_)
        h1c = sb("h1c", [P, D], c=d_)
        bc2 = sb("bc2", [P, 2 * D], c=d_)
        ob = sb("ob", [P, D], c=d_)
        st2 = sb("st2", [P, 18], c=d_)
        g_u = [sem(f"g_u{k}") for k in range(G)]
        g_v = [sem(f"g_v{k}") for k in range(G)]
        g_step = sem("g_step")
        g_dots = sem("g_dots")
        g_gelu = sem("g_gelu")
        g_seq = sem("g_seq")
        g_bc = sem("g_bc")
        g_tile = sem("g_tile")
        g_norm_in = sem("g_norm_in")
        g_norm = sem("g_norm")
        g_root_in = sem("g_root_in")
        g_root = sem("g_root")
        g_out = sem("g_out")
        g_stored = sem("g_stored")
        rows = bass.IndirectOffsetOnAxis
        with nc.Block() as block:
            @block.sync
            def _(sp):
                sp.dma_start(bc2[:, 0:D], ln2_g[0].partition_broadcast(P)).then_inc(g_bc, 16)
                sp.dma_start(bc2[:, D:2 * D], ln2_b[0].partition_broadcast(P)).then_inc(g_bc, 16)
                with sp.Fori(0, T) as t:
                    sp.wait_ge(g_out, 1)
                    sp.sem_inc(g_out, -1)
                    sp.dma_start(out[0, bass.ts(t, P), :], ob[:, :]).then_inc(g_stored, 16)

            @block.gpsimd
            def _(pool):
                def step(t, g, par, u, v):
                    if u:
                        nc.gpsimd.tensor_copy(ixu[:, par, :], eidx[:, t, bass.ds(g * G, G)]).then_inc(s_pool, 1)
                        pool.wait_ge(s_pool, 1)
                        pool.sem_inc(s_pool, -1)
                    if v:
                        nc.gpsimd.tensor_copy(ixv[:, 1 - par, :], eidx[:, t, bass.ds(g * G - G, G)]).then_inc(s_pool, 1)
                        pool.wait_ge(s_pool, 1)
                        pool.sem_inc(s_pool, -1)
                    for k in range(G):
                        pool.wait_ge(g_step, 1)
                        pool.sem_inc(g_step, -1)
                        if u:
                            pool.indirect_dma_start(U[:, k, :], None, expert_u[0],
                                                    rows(ap=ixu[:, par, k:k + 1], axis=0)).then_inc(g_u[k], 16)
                        if v:
                            pool.indirect_dma_start(V[:, k, :], None, expert_v[0],
                                                    rows(ap=ixv[:, 1 - par, k:k + 1], axis=0)).then_inc(g_v[k], 16)

                with pool.Fori(0, T) as t:
                    step(t, 0, 0, True, False)
                    with pool.Fori(0, NG // 2 - 1) as j:
                        step(t, 2 * j + 1, 1, True, True)
                        step(t, 2 * j + 2, 0, True, True)
                    step(t, NG - 1, 1, True, True)
                    step(t, NG, 0, False, True)
                    pool.wait_ge(g_root_in, 1)
                    pool.sem_inc(g_root_in, -1)
                    nc.gpsimd.tensor_tensor(st2[:, 14:15], st2[:, 14:15], nhalf[:, 0:1], ALU.pow).then_inc(g_root, 1)

            @block.scalar
            def _(act):
                act.sem_inc(g_stored, 16)
                with act.Fori(0, T) as t:
                    with act.Fori(0, NG // 2) as j:
                        for par in range(2):
                            act.wait_ge(g_dots, 1)
                            act.sem_inc(g_dots, -1)
                            nc.scalar.activation(gl[:, par, :], dots[:, par, :], ACT.Gelu).then_inc(g_gelu, 1)
                    act.wait_ge(g_norm_in, 1)
                    act.sem_inc(g_norm_in, -1)
                    act.wait_ge(g_stored, 16)
                    act.sem_inc(g_stored, -16)
                    nc.scalar.activation(ob[:, :], acc[:, 0, :], ACT.Identity, bias=st2[:, 15:16], scale=st2[:, 14:15]).then_inc(g_norm, 1)
                act.wait_ge(g_stored, 16)
                act.sem_inc(g_stored, -16)

            @block.vector
            def _(dve):
                dve.sem_inc(g_step, G)
                dve.wait_ge(g_bc, 32)

                def dot(par, k):
                    return nc.vector.tensor_tensor_reduce(out=U[:, k, :], in0=U[:, k, :], in1=h1c[:, :], scale=1.0, scalar=0.0,
                                                          op0=ALU.mult, op1=ALU.add, accum_out=dots[:, par, k:k + 1])

                def step(t, g, par, u, v):
                    if v:
                        w = gl[:, 1 - par, :]
                        dve.wait_ge(g_gelu, 1)
                        dve.sem_inc(g_gelu, -1)
                        nc.vector.tensor_tensor(w, w, egate[:, t, bass.ds(g * G - G, G)], ALU.mult).then_inc(s_dve, 1)
                        dve.wait_ge(s_dve, 1)
                        dve.sem_inc(s_dve, -1)
                    for k in range(G):
                        if u:
                            dve.wait_ge(g_u[k], (t * NG + g) * 16 + 16)
                            ins = dot(par, k)
                            if k == G - 1:
                                ins.then_inc(g_dots, 1) if v else ins.then_inc(s_dve, 1)
                            elif v and k > 0:
                                ins.then_inc(g_seq, 1)
                            elif not v:
                                ins.then_inc(g_step, 1)
                        if v:
                            dve.wait_ge(g_v[k], (t * NG + g) * 16)
                            if k > 1 and u:
                                dve.wait_ge(g_seq, 1)
                                dve.sem_inc(g_seq, -1)
                            if not u and k:
                                dve.wait_ge(s_dve, 1)
                                dve.sem_inc(s_dve, -1)
                            ins = nc.vector.scalar_tensor_tensor(out=acc[:, k % 2, :], in0=V[:, k, :], scalar=w[:, k:k + 1],
                                                                 in1=acc[:, k % 2, :], op0=ALU.mult, op1=ALU.add)
                            if u:
                                ins.then_inc(g_step, 1)
                            else:
                                ins.then_inc(s_dve, 1)
                    if not v:
                        dve.wait_ge(s_dve, 1)
                        dve.sem_inc(s_dve, -1)
                        dve.sem_inc(g_step, 1)
                        dve.sem_inc(g_dots, 1)
                    if not u:
                        dve.wait_ge(s_dve, 1)
                        dve.sem_inc(s_dve, -1)
                        dve.sem_inc(g_step, G)

                with dve.Fori(0, T) as t:
                    nc.vector.tensor_copy(h1c[:, :], hres[:, t, :]).then_inc(s_dve, 1)
                    nc.vector.memset(acc[:, :, :], 0.0).then_inc(s_dve, 1)
                    dve.wait_ge(s_dve, 2)
                    dve.sem_inc(s_dve, -2)
                    step(t, 0, 0, True, False)
                    with dve.Fori(0, NG // 2 - 1) as j:
                        step(t, 2 * j + 1, 1, True, True)
                        step(t, 2 * j + 2, 0, True, True)
                    step(t, NG - 1, 1, True, True)
                    step(t, NG, 0, False, True)
                    nc.vector.tensor_tensor(acc[:, 0, :], acc[:, 0, :], acc[:, 1, :], ALU.add).then_inc(s_dve, 1)
                    dve.wait_ge(s_dve, 1)
                    dve.sem_inc(s_dve, -1)
                    nc.vector.scalar_tensor_tensor(acc[:, 0, :], h1c[:, :], ALPHA, acc[:, 0, :], ALU.mult, ALU.add).then_inc(s_dve, 1)
                    dve.wait_ge(s_dve, 1)
                    dve.sem_inc(s_dve, -1)
                    for half in range(2):
                        nc.vector.bn_stats(st2[:, 6 * half:6 * half + 6], acc[:, 0, 512 * half:512 * half + 512]).then_inc(s_dve, 1)
                    dve.wait_ge(s_dve, 2)
                    dve.sem_inc(s_dve, -2)
                    nc.vector.bn_aggr(st2[:, 12:14], st2[:, 0:12]).then_inc(s_dve, 1)
                    dve.wait_ge(s_dve, 1)
                    dve.sem_inc(s_dve, -1)
                    nc.vector.tensor_scalar(st2[:, 14:15], st2[:, 13:14], LN_EPS, None, ALU.add).then_inc(s_dve, 1)
                    dve.wait_ge(s_dve, 1)
                    dve.sem_inc(s_dve, -1)
                    dve.sem_inc(g_root_in, 1)
                    dve.wait_ge(g_root, 1)
                    dve.sem_inc(g_root, -1)
                    nc.vector.tensor_scalar(st2[:, 15:16], st2[:, 12:13], st2[:, 14:15], -1.0, ALU.mult, ALU.mult).then_inc(s_dve, 1)
                    dve.wait_ge(s_dve, 1)
                    dve.sem_inc(s_dve, -1)
                    dve.sem_inc(g_norm_in, 1)
                    dve.wait_ge(g_norm, 1)
                    dve.sem_inc(g_norm, -1)
                    nc.vector.tensor_tensor(ob[:, :], ob[:, :], bc2[:, 0:D], ALU.mult).then_inc(s_dve, 1)
                    dve.wait_ge(s_dve, 1)
                    dve.sem_inc(s_dve, -1)
                    nc.vector.tensor_tensor(ob[:, :], ob[:, :], bc2[:, D:2 * D], ALU.add).then_inc(s_dve, 1)
                    dve.wait_ge(s_dve, 1)
                    dve.sem_inc(s_dve, -1)
                    dve.sem_inc(g_out, 1)
        d_.close()


_INS = ['x', 'ln_in_g', 'ln_in_b', 'w_in', 'conv_w', 'a_sinks', 'b_a_log', 'b_dt_bias', 'b_norm_w', 'w_out',
        'ln1_g', 'ln1_b', 'w_query', 'sub_keys', 'expert_u', 'expert_v', 'ln2_g', 'ln2_b']


def kernel(**inputs):
    import numpy as _np
    import concourse.bacc as _bacc
    from concourse import mybir as _mybir
    from concourse.bass_utils import run_bass_kernel_spmd as _run

    nc = _bacc.Bacc("TRN2", target_bir_lowering=False, num_devices=1)
    arrays, args = {}, []
    arrays["constants"] = constant_table()
    args.append(nc.dram_tensor("constants", (P, NCONST), _mybir.dt.float32, kind="ExternalInput").ap())
    for name in _INS:
        a = _np.ascontiguousarray(inputs[name])
        arrays[f"in_{name}"] = a
        args.append(nc.dram_tensor(f"in_{name}", a.shape, _mybir.dt.from_np(a.dtype), kind="ExternalInput").ap())
    args.append(nc.dram_tensor("out_0", (1, S, D), _mybir.dt.float32, kind="ExternalOutput").ap())
    build(nc, *args)
    r = _run(nc, [arrays], core_ids=[0])
    return r.results[0]["out_0"]
```

```python
import concourse.bass as bass
from concourse import mybir
from contextlib import ExitStack
import numpy as np

P = 128
S = 1024
D = 1024
T = S // P
KD = D // P
CHUNK = 64
AH, AKV, AD = 8, 2, 64
BH, BD = 4, 128
TAPS = 4
PH, NK, TOPK = 8, 128, 16
SLOTS = PH * TOPK
NCQ = AH * AD // P
NCONV = 3 * BH
NZ = BH
IN_W = 2824
AV, CONV0, Z0 = NCQ, NCQ + 1, NCQ + 1 + NCONV
NPROJ = Z0 + NZ
PAIR_ROWS = [(0, 1, 16, 0), (1, 2, 8, 16), (2, 3, 5, 24), (3, 4, 4, 29), (4, 5, 3, 33), (5, 8, 2, 36), (8, 16, 1, 42)]
NCAND = 50
LEAST = -3.0e38
GS = 4
NGROUP = SLOTS // GS
NPIECE = 40
PIECES = [0, 1, 3, 5, 7, 9, 11, 13, 15, 17, 19, 21, 23, 24, 26, 28, 30, 31, 33, 35, 36, 37, 39, 41, 43, 45, 47,
          48, 49, 51, 52, 53, 55, 56, 57, 59, 60, 61, 62, 63]
ARENA = 9216
LN_EPS = 1e-5
NORM_EPS = 1e-6
ALPHA = 2.0 ** 0.25
NEG = -1.0e30
FAR = 1.0e30

CONST_COLS = {}
_at = 0
for _name, _n in (("ident", P), ("upto", P), ("after", P), ("decay_mask", P), ("ones", P), ("chunk_of", 2 * P),
                  ("level", 6 * P), ("dist", 192), ("dist_past", 64), ("iota50", 50)):
    CONST_COLS[_name] = (_at, _at + _n)
    _at += _n
NCONST = _at


def constant_table():
    t = np.zeros((P, NCONST), np.float32)

    def put(name, a):
        lo, hi = CONST_COLS[name]
        t[:, lo:hi] = a.reshape(a.shape[0], -1)

    r = np.arange(P)
    same = (r[:, None] // CHUNK) == (r[None, :] // CHUNK)
    put("ident", np.eye(P, dtype=np.float32))
    put("upto", (same & (r[:, None] <= r[None, :])).astype(np.float32))
    put("after", (same & (r[:, None] > r[None, :])).astype(np.float32))
    put("decay_mask", np.where(same & (r[:, None] <= r[None, :]), 0.0, NEG).astype(np.float32))
    put("ones", np.ones((P, P), np.float32))
    put("chunk_of", np.stack([np.repeat((r // CHUNK == c)[:, None], P, 1) for c in range(2)], 1).astype(np.float32))
    lv = []
    for l in range(6):
        b = 1 << l
        j, i = r[:, None], r[None, :]
        lv.append((j // (2 * b) == i // (2 * b)) & (j % (2 * b) < b) & (i % (2 * b) >= b))
    put("level", np.stack(lv, 1).astype(np.float32))
    q = np.arange(P)[:, None]
    k = np.arange(192)[None, :] - 64
    qc, kc = q // 64, np.floor_divide(k, 64)
    ok = (kc == qc) | (kc == qc - 1)
    dist = np.where(ok, np.abs(q - k), FAR).astype(np.float32)
    put("dist_past", dist[:, 0:64])
    dist[:, 0:64] = FAR
    put("dist", dist)
    put("iota50", np.tile(np.arange(50, dtype=np.float32)[None], (P, 1)))
    return t


def build(nc, consts, x, ln_in_g, ln_in_b, w_in, conv_w, a_sinks, b_a_log, b_dt_bias, b_norm_w, w_out,
          ln1_g, ln1_b, w_query, sub_keys, expert_u, expert_v, ln2_g, ln2_b, out):
    fp32, u32 = mybir.dt.float32, mybir.dt.uint32
    ALU, ACT, AX = mybir.AluOpType, mybir.ActivationFunctionType, mybir.AxisListType

    ctx = ExitStack()
    with ctx:
        def sb(name, shape, dt=fp32, c=ctx):
            return c.enter_context(nc.sbuf_tensor(name, shape, dt))

        scope = [ctx]

        def sem(name):
            return scope[0].enter_context(nc.semaphore(name))

        s_dve = sem("s_dve")
        s_act = sem("s_act")
        s_pool = sem("s_pool")

        C = sb("C", [P, NCONST])

        def const(name):
            lo, hi = CONST_COLS[name]
            return C[:, lo:hi]

        ident = const("ident")
        nhalf = sb("nhalf", [P, 8])
        banks = [ctx.enter_context(nc.psum_tensor(f"bank{i}", [P, 1024], fp32)) for i in range(4)]

        proj_dram = nc.dram_tensor("proj_dram", (P, NPROJ, S), fp32).ap()
        h_dram = nc.dram_tensor("h_dram", (T, P, D), fp32).ap()
        ak_dram = nc.dram_tensor("ak_dram", (P, CHUNK + S), fp32).ap()
        gates = sb("gates", [P, 2, T, BH])

        wq = sb("wq", [P, KD, 2 * PH * P])
        skT = sb("skT", [P, 2 * PH, P])
        s_wq = sem("s_wq")
        s_sk = sem("s_sk")

        a = ExitStack()
        scope[0] = a
        hT = sb("hT", [P, KD, S], c=a)
        cw = sb("cw", [P, TAPS * NCONV + 1], c=a)
        bc = sb("bc", [P, 2 * D], c=a)
        skr = sb("skr", [P, 2 * PH, P], c=a)
        xin = sb("xin", [P, 2, D], c=a)
        wbuf = sb("wbuf", [P, 2, KD, P], c=a)
        ybuf = sb("ybuf", [P, 2, S], c=a)
        obuf = sb("obuf", [P, 2, S], c=a)
        zpad = sb("zpad", [P, CHUNK], c=a)
        st = sb("st", [P, 2, 18], c=a)
        wab = sb("wab", [P, KD, 8], c=a)
        abT = sb("abT", [8, S], c=a)
        cwr = sb("cwr", [TAPS * NCONV + 1, P], c=a)
        hb = sb("hb", [P, 2, BH], c=a)
        gt = sb("gt", [P, 6, T * BH], c=a)

        s_const = sem("s_const")
        s_small = sem("s_small")
        s_x = [sem(f"s_x{u}") for u in range(2)]
        s_stats = [sem(f"s_stats{u}") for u in range(2)]
        s_norm = [sem(f"s_norm{u}") for u in range(2)]
        s_h_pe = [sem(f"s_h_pe{u}") for u in range(2)]
        s_h_out = [sem(f"s_h_out{u}") for u in range(2)]
        s_hT_ps = [sem(f"s_hT_ps{u}") for u in range(2)]
        s_x_free = [sem(f"s_x_free{u}") for u in range(2)]
        s_tr_free = [sem(f"s_tr_free{u}") for u in range(2)]
        s_hT = sem("s_hT")
        s_w = [sem(f"s_w{u}") for u in range(2)]
        s_w_free = [sem(f"s_w_free{u}") for u in range(2)]
        s_proj = [sem(f"s_proj{u}") for u in range(2)]
        s_proj_free = [sem(f"s_proj_free{u}") for u in range(2)]
        s_tap0 = [sem(f"s_tap0{u}") for u in range(2)]
        s_conv = [sem(f"s_conv{u}") for u in range(2)]
        s_y_free = [sem(f"s_y_free{u}") for u in range(2)]
        s_cw_ps = sem("s_cw_ps")
        s_cw = sem("s_cw")
        s_ab_ps = sem("s_ab_ps")
        s_abT = sem("s_abT")
        s_ab_tok = sem("s_ab_tok")
        s_soft = sem("s_soft")
        s_soft2 = sem("s_soft2")
        s_pad = sem("s_pad")
        s_root_in = sem("s_root_in")
        s_root = sem("s_root")
        s_pad_out = sem("s_pad_out")
        s_sk_ps = sem("s_sk_ps")
        s_stored = [sem(f"s_stored{u}") for u in range(2)]

        NTAP = TAPS * NCONV
        w_in_v = w_in[0].rearrange("(k p) e -> p k e", p=P)
        x_v = x[0].rearrange("(t p) d -> t p d", p=P)

        with nc.Block() as block:
            @block.sync
            def _(sp):
                sp.dma_start(C[:, :], consts).then_inc(s_const, 16)
                sp.dma_start(bc[:, 0:D], ln_in_g.partition_broadcast(P)).then_inc(s_small, 16)
                sp.dma_start(bc[:, D:2 * D], ln_in_b.partition_broadcast(P)).then_inc(s_small, 16)
                sp.dma_start(cwr[0:NTAP, :], conv_w[0].rearrange("t (c p) -> (t c) p", p=P)).then_inc(s_small, 16)
                sp.dma_start(cwr[NTAP:NTAP + 1, :], b_norm_w).then_inc(s_small, 16)
                sp.dma_start(hb[:, 0, :], b_dt_bias[0].partition_broadcast(P)).then_inc(s_small, 16)
                sp.dma_start(hb[:, 1, :], b_a_log[0].partition_broadcast(P)).then_inc(s_small, 16)
                sp.dma_start(wab[:, :, :], w_in_v[:, :, IN_W - 8:IN_W]).then_inc(s_small, 16)
                with sp.Fori(0, T // 2) as j:
                    for u in range(2):
                        sp.wait_ge(s_x_free[u], 1)
                        sp.sem_inc(s_x_free[u], -1)
                        sp.wait_ge(s_h_out[u], 16)
                        sp.sem_inc(s_h_out[u], -16)
                        sp.dma_start(xin[:, u, :], x_v[2 * j + u]).then_inc(s_x[u], 16)
                for u in range(2):
                    sp.wait_ge(s_h_out[u], 16)
                    sp.sem_inc(s_h_out[u], -16)
                with sp.Fori(0, NCQ // 2) as j:
                    for u in range(2):
                        sp.wait_ge(s_w_free[u], 1)
                        sp.sem_inc(s_w_free[u], -1)
                        for half in range(2):
                            sp.dma_start(wbuf[:, u, :, 64 * half:64 * half + 64],
                                         w_in_v[:, :, bass.ds(j * 128 + u * 64 + 256 * half, 64)]).then_inc(s_w[u], 16)
                with sp.Fori(0, (2 + NCONV + NZ) // 2) as j:
                    for u in range(2):
                        sp.wait_ge(s_w_free[u], 1)
                        sp.sem_inc(s_w_free[u], -1)
                        sp.dma_start(wbuf[:, u, :, :],
                                     w_in_v[:, :, bass.ds(j * 256 + (NCQ + u) * P, P)]).then_inc(s_w[u], 16)
                sp.dma_start(skr[:, :, :], sub_keys[0].rearrange("h q n d -> n (h q) d")).then_inc(s_sk, 16)
                wq_v = w_query[0].rearrange("(k p) e -> p k e", p=P)
                for i in range(4):
                    sp.dma_start(wq[:, 2 * i:2 * i + 2, :], wq_v[:, 2 * i:2 * i + 2, :]).then_inc(s_wq, 16)

            @block.gpsimd
            def _(pool):
                nc.gpsimd.memset(zpad[:, :], 0.0).then_inc(s_pad, 1)
                nc.gpsimd.memset(nhalf[:, :], -0.5).then_inc(s_pool, 1)
                pool.wait_ge(s_pool, 1)
                pool.sem_inc(s_pool, -1)
                with pool.Fori(0, T // 2) as j:
                    for u in range(2):
                        pool.wait_ge(s_root_in, 1)
                        pool.sem_inc(s_root_in, -1)
                        nc.gpsimd.tensor_tensor(st[:, u, 14:15], st[:, u, 14:15], nhalf[:, 0:1], ALU.pow).then_inc(s_root, 1)

            @block.vector
            def _(dve):
                dve.wait_ge(s_small, 16 * 7)
                with dve.Fori(0, T // 2) as j:
                    for u in range(2):
                        dve.wait_ge(s_x[u], 16)
                        dve.sem_inc(s_x[u], -16)
                        for half in range(2):
                            nc.vector.bn_stats(st[:, u, 6 * half:6 * half + 6],
                                               xin[:, u, 512 * half:512 * half + 512]).then_inc(s_dve, 1)
                        dve.wait_ge(s_dve, 2)
                        dve.sem_inc(s_dve, -2)
                        nc.vector.bn_aggr(st[:, u, 12:14], st[:, u, 0:12]).then_inc(s_dve, 1)
                        dve.wait_ge(s_dve, 1)
                        dve.sem_inc(s_dve, -1)
                        nc.vector.tensor_scalar(st[:, u, 14:15], st[:, u, 13:14], LN_EPS, None, ALU.add).then_inc(s_root_in, 1)
                        dve.wait_ge(s_root, 1)
                        dve.sem_inc(s_root, -1)
                        nc.vector.tensor_scalar(st[:, u, 15:16], st[:, u, 12:13], st[:, u, 14:15], -1.0,
                                                ALU.mult, ALU.mult).then_inc(s_stats[u], 1)
                        dve.wait_ge(s_norm[u], 1)
                        dve.sem_inc(s_norm[u], -1)
                        nc.vector.tensor_tensor(xin[:, u, :], xin[:, u, :], bc[:, 0:D], ALU.mult).then_inc(s_dve, 1)
                        dve.wait_ge(s_dve, 1)
                        dve.sem_inc(s_dve, -1)
                        nc.vector.tensor_tensor(xin[:, u, :], xin[:, u, :], bc[:, D:2 * D], ALU.add).then_inc(s_dve, 1)
                        dve.wait_ge(s_dve, 1)
                        dve.sem_inc(s_dve, -1)
                        dve.sem_inc(s_h_pe[u], 1)
                dve.wait_ge(s_ab_tok, 1)
                dve.sem_inc(s_ab_tok, -1)
                tok = banks[3][:, 0:8 * T].rearrange("p (t g h) -> p t g h", g=2, h=BH)
                g4 = lambda i: gt[:, i, :].rearrange("p (t h) -> p t h", h=BH)
                nc.vector.tensor_tensor(g4(0), tok[:, :, 0, :], hb[:, 0, :].unsqueeze(1).to_broadcast([P, T, BH]),
                                        ALU.add).then_inc(s_dve, 1)
                dve.wait_ge(s_dve, 1)
                dve.sem_inc(s_dve, -1)
                nc.vector.scalar_tensor_tensor(gt[:, 1, :], gt[:, 0, :], -1.0, gt[:, 0, :], ALU.mult, ALU.min).then_inc(s_dve, 1)
                nc.vector.tensor_copy(g4(2), tok[:, :, 1, :]).then_inc(s_dve, 1)
                dve.wait_ge(s_dve, 2)
                dve.sem_inc(s_dve, -2)
                dve.sem_inc(s_soft, 1)
                dve.wait_ge(s_soft2, 1)
                dve.sem_inc(s_soft2, -1)
                nc.vector.tensor_scalar(gt[:, 4, :], gt[:, 3, :], 1.0, None, ALU.subtract).then_inc(s_dve, 1)
                dve.wait_ge(s_dve, 1)
                dve.sem_inc(s_dve, -1)
                nc.vector.tensor_scalar(gt[:, 5, :], gt[:, 4, :], 0.0, None, ALU.is_equal).then_inc(s_dve, 1)
                dve.wait_ge(s_dve, 1)
                dve.sem_inc(s_dve, -1)
                nc.vector.tensor_tensor(gt[:, 4, :], gt[:, 4, :], gt[:, 5, :], ALU.add).then_inc(s_dve, 1)
                dve.wait_ge(s_dve, 1)
                dve.sem_inc(s_dve, -1)
                nc.vector.reciprocal(gt[:, 4, :], gt[:, 4, :]).then_inc(s_dve, 1)
                dve.wait_ge(s_dve, 1)
                dve.sem_inc(s_dve, -1)
                nl = ybuf[:, 0, 0:T * BH]
                nc.vector.tensor_tensor(nl, nl, gt[:, 5, :], ALU.add).then_inc(s_dve, 1)
                dve.wait_ge(s_dve, 1)
                dve.sem_inc(s_dve, -1)
                nc.vector.tensor_tensor(nl, nl, gt[:, 4, :], ALU.mult).then_inc(s_dve, 1)
                dve.wait_ge(s_dve, 1)
                dve.sem_inc(s_dve, -1)
                nc.vector.tensor_tensor(nl, nl, gt[:, 1, :], ALU.mult).then_inc(s_dve, 1)
                dve.wait_ge(s_dve, 1)
                dve.sem_inc(s_dve, -1)
                nc.vector.scalar_tensor_tensor(gt[:, 0, :], gt[:, 0, :], 0.0, nl, ALU.max, ALU.add).then_inc(s_dve, 1)
                dve.wait_ge(s_dve, 1)
                dve.sem_inc(s_dve, -1)
                nc.vector.tensor_scalar(hb[:, 1, :], hb[:, 1, :], -1.0, None, ALU.mult).then_inc(s_dve, 1)
                dve.wait_ge(s_dve, 1)
                dve.sem_inc(s_dve, -1)
                nc.vector.tensor_tensor(gates[:, 0, :, :], g4(0), hb[:, 1, :].unsqueeze(1).to_broadcast([P, T, BH]),
                                        ALU.mult).then_inc(s_dve, 1)
                dve.wait_ge(s_dve, 1)
                dve.sem_inc(s_dve, -1)
                nc.vector.tensor_scalar(gt[:, 2, :], gt[:, 2, :], 1.0, None, ALU.add).then_inc(s_dve, 1)
                dve.wait_ge(s_dve, 1)
                dve.sem_inc(s_dve, -1)
                nc.vector.reciprocal(gates[:, 1, :, :].rearrange("p t h -> p (t h)"), gt[:, 2, :]).then_inc(s_dve, 1)
                dve.wait_ge(s_dve, 1)
                dve.sem_inc(s_dve, -1)
                dve.sem_inc(s_y_free[0], 1)
                dve.wait_ge(s_cw, 1)
                dve.sem_inc(s_cw, -1)
                with dve.Fori(0, NCONV // 2) as j:
                    for u in range(2):
                        ps = banks[u]
                        dve.wait_ge(s_tap0[u], 1)
                        dve.sem_inc(s_tap0[u], -1)
                        for back in range(1, TAPS):
                            nc.vector.scalar_tensor_tensor(
                       ybuf[:, u, back:S], ps[:, 0:S - back],
                       cw[:, bass.ds(2 * j + u + (TAPS - 1 - back) * NCONV, 1)],
                       ybuf[:, u, back:S], ALU.mult, ALU.add).then_inc(s_dve, 1)
                            dve.wait_ge(s_dve, 1)
                            dve.sem_inc(s_dve, -1)
                        dve.sem_inc(s_conv[u], 1)
                        dve.sem_inc(s_proj_free[u], 1)

            @block.tensor
            def _(pe):
                pe.wait_ge(s_const, 16)
                pe.sem_inc(s_const, -16)
                pe.wait_ge(s_small, 16 * 7)
                nc.tensor.transpose(banks[3][:, 512:512 + NTAP + 1], cwr[:, :], ident[0:NTAP + 1, 0:NTAP + 1]).then_inc(s_cw_ps, 1)
                with pe.Fori(0, T // 2) as j:
                    for u in range(2):
                        pe.wait_ge(s_h_pe[u], 1)
                        pe.sem_inc(s_h_pe[u], -1)
                        pe.wait_ge(s_tr_free[u], 1)
                        pe.sem_inc(s_tr_free[u], -1)
                        for k in range(KD):
                            last = nc.tensor.transpose(banks[u][:, k * P:(k + 1) * P], xin[:, u, k * P:(k + 1) * P], ident)
                        last.then_inc(s_hT_ps[u], 1)
                pe.wait_ge(s_hT, T)
                pe.sem_inc(s_hT, -T)
                for half in range(2):
                    for k in range(KD):
                        last = nc.tensor.matmul(banks[2][0:8, 512 * half:512 * half + 512], wab[:, k, :],
                                                hT[:, k, 512 * half:512 * half + 512], start=k == 0, stop=k == KD - 1)
                last.then_inc(s_ab_ps, 1)
                pe.wait_ge(s_abT, 1)
                pe.sem_inc(s_abT, -1)
                pe.wait_ge(s_tr_free[0], 1)
                pe.sem_inc(s_tr_free[0], -1)
                for t in range(T):
                    last = nc.tensor.transpose(banks[3][:, 8 * t:8 * t + 8], abT[:, t * P:(t + 1) * P], ident[0:8, 0:8])
                last.then_inc(s_ab_tok, 1)

                def project(u, parts):
                    pe.wait_ge(s_w[u], 16 * parts)
                    pe.sem_inc(s_w[u], -(16 * parts))
                    pe.wait_ge(s_proj_free[u], 1)
                    pe.sem_inc(s_proj_free[u], -1)
                    for half in range(2):
                        for k in range(KD):
                            last = nc.tensor.matmul(banks[u][:, 512 * half:512 * half + 512], wbuf[:, u, k, :],
                                                    hT[:, k, 512 * half:512 * half + 512], start=k == 0, stop=k == KD - 1)
                    last.then_inc(s_proj[u], 1)

                with pe.Fori(0, NCQ // 2) as j:
                    for u in range(2):
                        project(u, 2)
                with pe.Fori(0, (2 + NCONV + NZ) // 2) as j:
                    for u in range(2):
                        project(u, 1)

                pe.wait_ge(s_sk, 16)
                pe.sem_inc(s_sk, -16)
                for half in range(2):
                    for i in range(8):
                        last = nc.tensor.transpose(banks[2 + half][:, i * P:(i + 1) * P], skr[:, 8 * half + i, :], ident)
                last.then_inc(s_sk_ps, 1)

            @block.scalar
            def _(act):
                act.sem_inc(s_x_free[0], 1)
                act.sem_inc(s_h_out[0], 16)
                act.sem_inc(s_x_free[1], 1)
                act.sem_inc(s_h_out[1], 16)
                act.sem_inc(s_tr_free[0], 1)
                act.sem_inc(s_tr_free[1], 1)
                act.sem_inc(s_w_free[0], 1)
                act.sem_inc(s_w_free[1], 1)
                act.wait_ge(s_cw_ps, 1)
                act.sem_inc(s_cw_ps, -1)
                nc.scalar.copy(cw[:, :], banks[3][:, 512:512 + NTAP + 1]).then_inc(s_cw, 1)
                with act.Fori(0, T // 2) as j:
                    for u in range(2):
                        act.wait_ge(s_stats[u], 1)
                        act.sem_inc(s_stats[u], -1)
                        nc.scalar.activation(xin[:, u, :], xin[:, u, :], ACT.Identity, bias=st[:, u, 15:16],
                                             scale=st[:, u, 14:15]).then_inc(s_norm[u], 1)
                        act.wait_ge(s_hT_ps[u], 1)
                        act.sem_inc(s_hT_ps[u], -1)
                        act.dma_start(h_dram[2 * j + u], xin[:, u, :]).then_inc(s_h_out[u], 16)
                        nc.scalar.copy(hT[:, :, bass.ts(2 * j + u, P)],
                                       banks[u][:, :].rearrange("p (k n) -> p k n", n=P)).then_inc(s_act, 1)
                        act.wait_ge(s_act, 1)
                        act.sem_inc(s_act, -1)
                        act.sem_inc(s_tr_free[u], 1)
                        act.sem_inc(s_x_free[u], 1)
                        act.sem_inc(s_hT, 1)
                act.wait_ge(s_ab_ps, 1)
                act.sem_inc(s_ab_ps, -1)
                nc.scalar.copy(abT[:, :], banks[2][0:8, :]).then_inc(s_abT, 1)
                act.wait_ge(s_soft, 1)
                act.sem_inc(s_soft, -1)
                nl = ybuf[:, 0, 0:T * BH]
                nc.scalar.activation(gt[:, 1, :], gt[:, 1, :], ACT.Exp).then_inc(s_act, 1)
                nc.scalar.activation(gt[:, 2, :], gt[:, 2, :], ACT.Exp, scale=-1.0).then_inc(s_act, 1)
                nc.scalar.activation(hb[:, 1, :], hb[:, 1, :], ACT.Exp).then_inc(s_act, 1)
                act.wait_ge(s_act, 3)
                act.sem_inc(s_act, -3)
                nc.scalar.activation(gt[:, 3, :], gt[:, 1, :], ACT.Copy, bias=1.0).then_inc(s_act, 1)
                act.wait_ge(s_act, 1)
                act.sem_inc(s_act, -1)
                nc.scalar.activation(nl, gt[:, 3, :], ACT.Ln).then_inc(s_act, 1)
                act.wait_ge(s_act, 1)
                act.sem_inc(s_act, -1)
                act.sem_inc(s_soft2, 1)
                act.sem_inc(s_proj_free[0], 1)
                act.sem_inc(s_proj_free[1], 1)

                act.wait_ge(s_pad, 1)
                act.sem_inc(s_pad, -1)
                act.dma_start(ak_dram[:, 0:CHUNK], zpad[:, :]).then_inc(s_pad_out, 16)
                for u in range(2):
                    act.sem_inc(s_stored[u], 16)

                def store(u, dst):
                    act.wait_ge(s_act, 1)
                    act.sem_inc(s_act, -1)
                    act.dma_start(dst, obuf[:, u, :]).then_inc(s_stored[u], 16)

                def plain(u, dst):
                    act.wait_ge(s_proj[u], 1)
                    act.sem_inc(s_proj[u], -1)
                    act.wait_ge(s_stored[u], 16)
                    act.sem_inc(s_stored[u], -16)
                    nc.scalar.copy(obuf[:, u, :], banks[u][:, :]).then_inc(s_act, 1)
                    store(u, dst)
                    act.sem_inc(s_w_free[u], 1)
                    act.sem_inc(s_proj_free[u], 1)

                with act.Fori(0, NCQ // 2) as j:
                    for u in range(2):
                        plain(u, proj_dram[:, 2 * j + u, :])
                plain(0, ak_dram[:, CHUNK:CHUNK + S])
                plain(1, proj_dram[:, AV, :])
                act.wait_ge(s_y_free[0], 1)
                act.sem_inc(s_y_free[0], -1)
                with act.Fori(0, NCONV // 2) as j:
                    for u in range(2):
                        act.wait_ge(s_proj[u], 1)
                        act.sem_inc(s_proj[u], -1)
                        act.sem_inc(s_w_free[u], 1)
                        nc.scalar.activation(ybuf[:, u, :], banks[u][:, :], ACT.Copy,
                                             scale=cw[:, bass.ds(2 * j + u + (TAPS - 1) * NCONV, 1)]).then_inc(s_tap0[u], 1)
                        act.wait_ge(s_conv[u], 1)
                        act.sem_inc(s_conv[u], -1)
                        act.wait_ge(s_stored[u], 16)
                        act.sem_inc(s_stored[u], -16)
                        nc.scalar.activation(obuf[:, u, :], ybuf[:, u, :], ACT.Silu).then_inc(s_act, 1)
                        store(u, proj_dram[:, 2 * j + (CONV0 + u), :])
                with act.Fori(0, NZ // 2) as j:
                    for u in range(2):
                        act.wait_ge(s_proj[u], 1)
                        act.sem_inc(s_proj[u], -1)
                        act.sem_inc(s_w_free[u], 1)
                        nc.scalar.activation(ybuf[:, u, :], banks[u][:, :], ACT.Silu).then_inc(s_act, 1)
                        act.wait_ge(s_act, 1)
                        act.sem_inc(s_act, -1)
                        act.sem_inc(s_proj_free[u], 1)
                        act.wait_ge(s_stored[u], 16)
                        act.sem_inc(s_stored[u], -16)
                        nc.scalar.activation(obuf[:, u, :], ybuf[:, u, :], ACT.Copy,
                                             scale=cw[:, NTAP:NTAP + 1]).then_inc(s_act, 1)
                        store(u, proj_dram[:, 2 * j + (Z0 + u), :])
                act.wait_ge(s_sk_ps, 1)
                act.sem_inc(s_sk_ps, -1)
                for half in range(2):
                    nc.scalar.copy(skT[:, 8 * half:8 * half + 8, :].rearrange("p a n -> p (a n)"), banks[2 + half][:, :]).then_inc(s_act, 1)
                    act.wait_ge(s_act, 1)
                    act.sem_inc(s_act, -1)
                for u in range(2):
                    act.wait_ge(s_stored[u], 16)
                    act.sem_inc(s_stored[u], -16)
                act.wait_ge(s_pad_out, 16)
                act.sem_inc(s_pad_out, -16)
        a.close()
        b = ExitStack()
        scope[0] = b
        arena = sb("arena", [P, ARENA], c=b)

        def view(at, *dims, dt=fp32):
            n = int(np.prod(dims))
            a = arena[:, at:at + n]
            if dt != fp32:
                a = a.bitcast(dt)
            names = " ".join("abc"[:len(dims)])
            return a.rearrange(f"p ({names}) -> p {names}", **dict(zip("abc", dims))) if len(dims) > 1 else a

        qk_tok = view(0, 12, P)
        ML = view(0, 2, BH, P)
        vnew = view(1024, BH, P)
        qk_ch = view(1536, 12, P)
        kdec, kbe, vb = view(3072, BH, P), view(3584, BH, P), view(4096, BH, P)
        sq = view(4608, 8, P)
        wk = view(4608, 2 * BH, P)
        gU, bI = view(5632, BH, P), view(6144, BH, P)
        yT = view(5632, KD, P)
        DT = view(6656, BH, P)
        on = view(6656, BH, P)
        MT, intraT = view(7168, BH, P), view(7680, BH, P)
        prT = view(8192, 2 * BH, P)
        h1T = view(0, KD, P)
        qT = view(1024, 2 * PH, P)
        rest = view(3072, 2 * PH, NK)
        top, itop = view(5120, 2 * PH, TOPK), view(5376, 2 * PH, TOPK, dt=u32)
        ftop = view(5632, PH, 2, TOPK)
        cand, cid, crest = view(5888, PH, NCAND), view(6288, PH, NCAND), view(6688, PH, NCAND)
        best, ibest, fbest = view(7088, PH, TOPK), view(7216, PH, TOPK, dt=u32), view(7344, PH, TOPK)
        fex = view(7472, PH, TOPK)
        den = view(7600, 2, PH)
        eq = view(7616, TOPK, NCAND)

        raw = sb("raw", [P, NPROJ, P], c=b)
        X, XT, Pm = (raw[:, CONV0 + 4 * i:CONV0 + 4 * i + 4, :] for i in range(3))
        zt = raw[:, Z0:Z0 + NZ, :]
        akt = sb("akt", [P, CHUNK + P], c=b)
        vtok = sb("vtok", [P, 2, P], c=b)
        sml = sb("sml", [P, 64], c=b)
        att = sb("att", [P, 32], c=b)
        St = sb("St", [P, BH, P], c=b)
        sc = sb("sc", [P, BH, 192], c=b)
        pr = sb("pr", [P, BH, 256], c=b)
        ytok = sb("ytok", [P, AH * AD], c=b)
        pre = sb("pre", [P, D], c=b)
        h1n = sb("h1n", [P, D], c=b)
        sink = sb("sink", [P, 2, AH], c=b)
        lnr = sb("lnr", [4, D], c=b)
        wo = sb("wo", [P, 2, D], c=b)
        stb = sb("stb", [P, 18], c=b)
        eidx_n = sb("eidx_n", [P, SLOTS], u32, c=b)
        egate_n = sb("egate_n", [P, SLOTS], c=b)
        U = sb("U", [P, GS, D], c=b)
        V = sb("V", [P, GS, D], c=b)
        eidx = sb("eidx", [P, SLOTS], u32, c=b)
        egate = sb("egate", [P, SLOTS], c=b)
        ixu = sb("ixu", [P, 2, GS], u32, c=b)
        ixv = sb("ixv", [P, 2, GS], u32, c=b)
        dots = sb("dots", [P, 2, GS], c=b)
        gl = sb("gl", [P, 2, GS], c=b)
        dg = sb("dg", [P, 2, 2, P], c=b)
        acc = sb("acc", [P, D], c=b)
        h1c = sb("h1c", [P, D], c=b)
        st2 = sb("st2", [P, 18], c=b)

        b0 = banks[0]
        g = [banks[1][:, 0:512], banks[1][:, 512:1024], banks[2][:, 0:512], banks[2][:, 512:1024]]
        acc_ps = banks[3]
        heads = lambda a: a.rearrange("p (h n) -> p h n", h=BH)
        flat = lambda a: a.rearrange("p a n -> p (a n)")
        SS, RS, EG = sml[:, 0:8], sml[:, 8:16], sml[:, 16:32]
        CO = sml[:, 32:52].rearrange("p (c h) -> p c h", h=BH)
        NG4, SO = sml[:, 52:56], sml[:, 56:60]
        e_gc, e_rest, e_last = EG[:, 0:4], EG[:, 4:8], EG[:, 8:16]
        MX, SE, DEN, RD = att[:, 0:8], att[:, 8:16], att[:, 16:24], att[:, 24:32]

        b_raw = sem("b_raw")
        b_raw_free = sem("b_raw_free")
        b_load = sem("b_load")
        b_wo0 = sem("b_wo0")
        b_wo1 = sem("b_wo1")
        b_wo_free0 = sem("b_wo_free0")
        b_wo_free1 = sem("b_wo_free1")
        b_pre_in = sem("b_pre_in")
        b_pre_free = sem("b_pre_free")
        b_tok_raw = sem("b_tok_raw")
        b_squared = sem("b_squared")
        b_root_in = sem("b_root_in")
        b_root = sem("b_root")
        b_oroot_in = sem("b_oroot_in")
        b_oroot = sem("b_oroot")
        b_tok_done = sem("b_tok_done")
        b_tokT = sem("b_tokT")
        b_qkch = sem("b_qkch")
        b_gu = sem("b_gu")
        b_gexp = sem("b_gexp")
        b_arg = sem("b_arg")
        b_decayed = sem("b_decayed")
        b_kk = sem("b_kk")
        b_lvM = sem("b_lvM")
        b_lvP0 = sem("b_lvP0")
        b_lvP = sem("b_lvP")
        b_lvPs = sem("b_lvPs")
        b_lvQ = sem("b_lvQ")
        b_lvX = sem("b_lvX")
        b_wk_ps = sem("b_wk_ps")
        b_wk_done = sem("b_wk_done")
        b_vps = sem("b_vps")
        b_vnew = sem("b_vnew")
        b_o_ds = sem("b_o_ds")
        b_o_done = sem("b_o_done")
        b_osq = sem("b_osq")
        b_state = sem("b_state")
        b_on_ready = sem("b_on_ready")
        b_onT_ps = sem("b_onT_ps")
        b_yT_b = sem("b_yT_b")
        b_osq_in = sem("b_osq_in")
        b_sc_ps = sem("b_sc_ps")
        b_sc_s = sem("b_sc_s")
        b_pexp = sem("b_pexp")
        b_exp_s = sem("b_exp_s")
        b_prT_ps = sem("b_prT_ps")
        b_prT_done = sem("b_prT_done")
        b_pv = sem("b_pv")
        b_pv_read = sem("b_pv_read")
        b_ya = sem("b_ya")
        b_yaT_ps = sem("b_yaT_ps")
        b_yT_a = sem("b_yT_a")
        b_mix_ps = sem("b_mix_ps")
        b_lroot_in = sem("b_lroot_in")
        b_lroot = sem("b_lroot")
        b_norm_in = sem("b_norm_in")
        b_normed = sem("b_normed")
        b_ln_ps = sem("b_ln_ps")
        b_h1 = sem("b_h1")
        b_h1T_ps = sem("b_h1T_ps")
        b_h1T = sem("b_h1T")
        b_q_ps = sem("b_q_ps")
        b_qT = sem("b_qT")
        b_scores = sem("b_scores")
        b_scores_read = sem("b_scores_read")
        b_soft = sem("b_soft")
        b_exped = sem("b_exped")
        g_u = [sem(f"g_u{k}") for k in range(GS)]
        g_v = [sem(f"g_v{k}") for k in range(GS)]
        g_ufree = sem("g_ufree")
        g_vfree = sem("g_vfree")
        g_pfree = sem("g_pfree")
        g_dots = sem("g_dots")
        g_gelu = sem("g_gelu")
        g_seq = sem("g_seq")
        g_w = sem("g_w")
        g_diag = sem("g_diag")
        g_dfree = sem("g_dfree")
        g_accps = sem("g_accps")
        g_accfree = sem("g_accfree")
        g_tile = sem("g_tile")
        s_pe = sem("s_pe")
        t_root_in = sem("t_root_in")
        t_root = sem("t_root")
        t_norm_in = sem("t_norm_in")
        t_normed = sem("t_normed")
        t_ln = sem("t_ln")
        t_lnfree = sem("t_lnfree")
        t_out = sem("t_out")
        t_stored = sem("t_stored")
        t_last = sem("t_last")

        def bc3(a, n=P):
            return a.unsqueeze(2).to_broadcast([a.shape[0], a.shape[1], n])

        def per_head(a):
            return a.unsqueeze(1).to_broadcast([P, BH, P])

        rows = bass.IndirectOffsetOnAxis

        with nc.Block() as block:
            @block.sync
            def _(sp):
                sp.dma_start(lnr[0:1, :], ln1_g).then_inc(b_load, 16)
                sp.dma_start(lnr[1:2, :], ln1_b).then_inc(b_load, 16)
                sp.dma_start(lnr[2:3, :], ln2_g).then_inc(b_load, 16)
                sp.dma_start(lnr[3:4, :], ln2_b).then_inc(b_load, 16)
                sp.dma_start(sink[:, 0, :], a_sinks[0].partition_broadcast(P)).then_inc(b_load, 16)
                wo_v = w_out[0].rearrange("(k p) d -> k p d", p=P)
                with sp.Fori(0, T) as t:
                    sp.wait_ge(b_raw_free, 1)
                    sp.sem_inc(b_raw_free, -1)
                    sp.dma_start(raw[:, :, :], proj_dram[:, :, bass.ts(t, P)]).then_inc(b_raw, 16)
                    sp.dma_start(akt[:, :], ak_dram[:, bass.ds(t * P, CHUNK + P)]).then_inc(b_raw, 16)
                    sp.wait_ge(b_pre_free, 1)
                    sp.sem_inc(b_pre_free, -1)
                    sp.dma_start(pre[:, :], h_dram[t]).then_inc(b_pre_in, 16)
                    for k in range(KD):
                        sp.wait_ge(b_wo_free1 if k % 2 else b_wo_free0, 1)
                        sp.sem_inc(b_wo_free1 if k % 2 else b_wo_free0, -1)
                        sp.dma_start(wo[:, k % 2, :], wo_v[k]).then_inc((b_wo1 if k % 2 else b_wo0), 16)

            @block.gpsimd
            def _(pool):
                def step(s, par, u, v):
                    if u:
                        nc.gpsimd.tensor_copy(ixu[:, par, :], eidx[:, bass.ds(s * GS, GS)]).then_inc(s_pool, 1)
                        pool.wait_ge(s_pool, 1)
                        pool.sem_inc(s_pool, -1)
                    if v:
                        nc.gpsimd.tensor_copy(ixv[:, 1 - par, :], eidx[:, bass.ds(s * GS - GS, GS)]).then_inc(s_pool, 1)
                        pool.wait_ge(s_pool, 1)
                        pool.sem_inc(s_pool, -1)
                    for k in range(GS):
                        if u:
                            pool.wait_ge(g_ufree, 1)
                            pool.sem_inc(g_ufree, -1)
                            pool.indirect_dma_start(U[:, k, :], None, expert_u[0],
                                                    rows(ap=ixu[:, par, k:k + 1], axis=0)).then_inc(g_u[k], 16)
                        if v:
                            if k < 2:
                                pool.wait_ge(g_vfree, 1)
                                pool.sem_inc(g_vfree, -1)
                            else:
                                pool.wait_ge(g_pfree, 1)
                                pool.sem_inc(g_pfree, -1)
                            pool.indirect_dma_start(V[:, k, :], None, expert_v[0],
                                                    rows(ap=ixv[:, 1 - par, k:k + 1], axis=0)).then_inc(g_v[k], 16)

                with pool.Fori(0, T) as t:
                    pool.wait_ge(g_tile, 1)
                    pool.sem_inc(g_tile, -1)
                    step(0, 0, True, False)
                    with pool.Fori(0, NGROUP // 2 - 1) as j:
                        step(2 * j + 1, 1, True, True)
                        step(2 * j + 2, 0, True, True)
                    step(NGROUP - 1, 1, True, True)
                    step(NGROUP, 0, False, True)

            @block.tensor
            def _(pe):
                def level(l):
                    if l:
                        pe.wait_ge(b_lvX, 1)
                        pe.sem_inc(b_lvX, -1)
                    pe.wait_ge(b_lvM, 1)
                    pe.sem_inc(b_lvM, -1)
                    for h in range(BH):
                        last = nc.tensor.matmul(g[0][:, h * P:(h + 1) * P], ML[:, l % 2, h, :], ident if l == 0 else X[:, h, :],
                                                start=True, stop=True)
                    if l == 0:
                        last.then_inc(b_lvP0, 1)
                        return
                    last.then_inc(b_lvP, 1)
                    pe.wait_ge(b_lvPs, 1)
                    pe.sem_inc(b_lvPs, -1)
                    for h in range(BH):
                        if l < 5:
                            nc.tensor.matmul(g[1][:, h * P:(h + 1) * P], XT[:, h, :], Pm[:, h, :], start=True, stop=True)
                        last = nc.tensor.matmul(g[2][:, h * P:(h + 1) * P], Pm[:, h, :], XT[:, h, :], start=True, stop=True)
                    last.then_inc(b_lvQ, 1)

                def scores(hh):
                    lo = 64 * hh
                    for i in range(4):
                        last = nc.tensor.matmul(b0[:, 256 * i:256 * i + 192], raw[lo:lo + 64, i, :], akt[lo:lo + 64, :],
                                                start=True, stop=True)
                    last.then_inc(b_sc_ps, 1)

                def turn_probs():
                    pe.wait_ge(b_pexp, 1)
                    pe.sem_inc(b_pexp, -1)
                    for i in range(8):
                        last = nc.tensor.transpose(b0[:, i * P:(i + 1) * P], pr[:, i // 2, (i % 2) * P:(i % 2 + 1) * P], ident)
                    last.then_inc(b_prT_ps, 1)

                def values(hh):
                    pe.wait_ge(b_prT_done, 1)
                    pe.sem_inc(b_prT_done, -1)
                    for i in range(4):
                        o = b0[:, 64 * i:64 * i + 64]
                        nc.tensor.matmul(o, prT[64:128, 2 * i, :], vtok[64:128, 1, 64 * hh:64 * hh + 64], start=True, stop=False)
                        last = nc.tensor.matmul(o, prT[:, 2 * i + 1, :], vtok[:, 0, 64 * hh:64 * hh + 64], start=False, stop=True)
                    last.then_inc(b_pv, 1)

                def chunk_values(c):
                    lo = 64 * c
                    for h in range(BH):
                        last = nc.tensor.matmul(g[2][lo:lo + 64, h * P:(h + 1) * P], wk[:, BH + h, lo:lo + 64], St[:, h, :],
                                                start=True, stop=True)
                    last.then_inc(b_vps, 1)

                def chunk_output(c):
                    lo = 64 * c
                    pe.wait_ge(b_vnew, 1)
                    pe.sem_inc(b_vnew, -1)
                    for h in range(BH):
                        o = g[3][lo:lo + 64, h * P:(h + 1) * P]
                        nc.tensor.matmul(o, qk_ch[:, 4 + h, lo:lo + 64], St[:, h, :], start=True, stop=False, skip_group_check=True)
                        nc.tensor.matmul(o, intraT[lo:lo + 64, h, lo:lo + 64], vnew[lo:lo + 64, h, :],
                                         start=False, stop=True, skip_group_check=True)
                    for h in range(BH):
                        last = nc.tensor.matmul(g[0][:, h * P:(h + 1) * P], kdec[lo:lo + 64, h, :], vnew[lo:lo + 64, h, :],
                                                start=True, stop=True)
                    last.then_inc(b_o_ds, 1)

                def project_out(ks):
                    for k in ks:
                        pe.wait_ge(b_wo1 if k % 2 else b_wo0, 16)
                        pe.sem_inc(b_wo1 if k % 2 else b_wo0, -16)
                        for n in range(2):
                            last = nc.tensor.matmul(b0[:, 512 * n:512 * n + 512], yT[:, k, :], wo[:, k % 2, 512 * n:512 * n + 512],
                                                    start=k == 0, stop=k == KD - 1)
                        last.then_inc((b_wo_free1 if k % 2 else b_wo_free0), 1)

                def norm_rows(r, s_ready):
                    for i in range(2):
                        for n in range(2):
                            last = nc.tensor.matmul(banks[1 + i][:, 512 * n:512 * n + 512],
                                                    ident[0:4, r + i:r + i + 1].to_broadcast([4, P]),
                                                    lnr[:, 512 * n:512 * n + 512], start=True, stop=True)
                    last.then_inc(s_ready, 1)

                def queries(q):
                    for i in range(4 * q, 4 * q + 4):
                        o = banks[1 + i // 8][:, (i % 8) * P:(i % 8 + 1) * P]
                        for k in range(KD):
                            last = nc.tensor.matmul(o, wq[:, k, i * P:(i + 1) * P], h1T[:, k, :], start=k == 0, stop=k == KD - 1)
                    if q % 2:
                        last.then_inc(b_q_ps, 1)

                def piece(n, t):
                    if n == 0:
                        pe.wait_ge(b_raw, 32)
                        pe.sem_inc(b_raw, -32)
                        for i in range(8):
                            nc.tensor.transpose(banks[1][:, i * P:(i + 1) * P], raw[:, CONV0 + i, :], ident)
                        for i in range(4):
                            last = nc.tensor.transpose(g[2][:, i * P:(i + 1) * P], raw[:, CONV0 + 8 + i, :], ident)
                        gate = gates[:, 0, t, :]
                        nc.tensor.matmul(g[3][:, 0:4], const("upto"), gate, start=True, stop=True)
                        nc.tensor.matmul(g[3][:, 4:8], const("after"), gate, start=True, stop=True)
                        for c in range(2):
                            nc.tensor.matmul(g[3][:, 8 + 4 * c:12 + 4 * c], const("chunk_of")[:, c * P:(c + 1) * P], gate,
                                             start=True, stop=True)
                        nc.tensor.transpose(g[3][:, 128:256], raw[:, AV, :], ident).then_inc(b_tok_raw, 1)
                        scores(0)
                    elif n == 2:
                        pe.wait_ge(b_tok_done, 1)
                        pe.sem_inc(b_tok_done, -1)
                        for i in range(8):
                            nc.tensor.transpose(banks[1][:, i * P:(i + 1) * P], qk_tok[:, i, :], ident)
                        for i in range(4):
                            last = nc.tensor.transpose(g[2][:, i * P:(i + 1) * P], qk_tok[:, 8 + i, :], ident)
                        last.then_inc(b_tokT, 1)
                        pe.wait_ge(b_gu, 1)
                        pe.sem_inc(b_gu, -1)
                        nc.tensor.matmul(g[3], const("ones"), gU, start=True, stop=False)
                        nc.tensor.matmul(g[3], const("upto"), bc3(NG4), start=False, stop=False)
                        nc.tensor.matmul(g[3], ident, per_head(const("decay_mask")), start=False, stop=True).then_inc(b_arg, 1)
                        turn_probs()
                    elif n == 3:
                        pe.wait_ge(b_qkch, 1)
                        pe.sem_inc(b_qkch, -1)
                        for h in range(BH):
                            nc.tensor.matmul(g[0][:, h * P:(h + 1) * P], qk_ch[:, 8 + h, :], qk_ch[:, 8 + h, :], start=True, stop=True)
                            nc.tensor.matmul(g[1][:, h * P:(h + 1) * P], qk_ch[:, 8 + h, :], qk_ch[:, h, :], start=True, stop=True)
                        nc.tensor.matmul(g[2], const("after"), bI, start=True, stop=True).then_inc(b_kk, 1)
                        values(0)
                    elif n == 4:
                        pe.wait_ge(b_pv_read, 1)
                        pe.sem_inc(b_pv_read, -1)
                        scores(1)
                        level(0)
                    elif n == 5:
                        level(1)
                    elif n == 6:
                        level(2)
                        turn_probs()
                    elif n == 7:
                        level(3)
                        values(1)
                    elif n == 8:
                        level(4)
                        pe.wait_ge(b_ya, 1)
                        pe.sem_inc(b_ya, -1)
                        for i in range(4):
                            last = nc.tensor.transpose(b0[:, 512 + i * P:512 + (i + 1) * P], ytok[:, i * P:(i + 1) * P], ident)
                        last.then_inc(b_yaT_ps, 1)
                    elif n == 9:
                        level(5)
                    elif n == 10:
                        pe.wait_ge(b_lvX, 1)
                        pe.sem_inc(b_lvX, -1)
                        for h in range(BH):
                            nc.tensor.matmul(g[0][:, h * P:(h + 1) * P], XT[:, h, :], vb[:, h, :], start=True, stop=True)
                            last = nc.tensor.matmul(g[1][:, h * P:(h + 1) * P], kbe[:, h, :], XT[:, h, :], start=True, stop=True)
                        last.then_inc(b_wk_ps, 1)
                        pe.wait_ge(b_wk_done, 1)
                        pe.sem_inc(b_wk_done, -1)
                        chunk_values(0)
                    elif n == 11:
                        chunk_output(0)
                    elif n == 12:
                        pe.wait_ge(b_state, 1)
                        pe.sem_inc(b_state, -1)
                        chunk_values(1)
                    elif n == 13:
                        chunk_output(1)
                    elif n == 16:
                        pe.wait_ge(b_on_ready, 1)
                        pe.sem_inc(b_on_ready, -1)
                        for i in range(4):
                            last = nc.tensor.transpose(g[1][:, i * P:(i + 1) * P], on[:, i, :], ident)
                        last.then_inc(b_onT_ps, 1)
                    elif n == 17:
                        pe.wait_ge(b_yT_a, 1)
                        pe.sem_inc(b_yT_a, -1)
                        project_out(range(0, 4))
                    elif n == 18:
                        pe.wait_ge(b_yT_b, 1)
                        pe.sem_inc(b_yT_b, -1)
                        project_out(range(4, 8))
                        pe.wait_ge(b_o_done, 1)
                        pe.sem_inc(b_o_done, -1)
                        norm_rows(0, b_mix_ps)
                    elif n == 21:
                        pe.wait_ge(b_h1, 1)
                        pe.sem_inc(b_h1, -1)
                        for k in range(KD):
                            last = nc.tensor.transpose(b0[:, k * P:(k + 1) * P], h1n[:, k * P:(k + 1) * P], ident)
                        last.then_inc(b_h1T_ps, 1)
                    elif 22 <= n <= 25:
                        if n == 22:
                            pe.wait_ge(b_h1T, 1)
                            pe.sem_inc(b_h1T, -1)
                        queries(n - 22)
                    elif n == 26:
                        pe.wait_ge(b_qT, 1)
                        pe.sem_inc(b_qT, -1)
                        for hp in range(2 * PH):
                            last = nc.tensor.matmul(banks[hp // 8][:, (hp % 8) * P:(hp % 8 + 1) * P], qT[:, hp, :], skT[:, hp, :],
                                                    start=True, stop=True)
                        last.then_inc(b_scores, 1)
                    elif n == 30:
                        pe.wait_ge(b_scores_read, 1)
                        pe.sem_inc(b_scores_read, -1)

                def gather(t, s, par, first=False, last_group=False):
                    pe.wait_ge(g_diag, 2)
                    pe.sem_inc(g_diag, -2)
                    if first:
                        pe.wait_ge(g_accfree, 1)
                        pe.sem_inc(g_accfree, -1)
                    for k in range(2, GS):
                        pe.wait_ge(g_v[k], (t * NGROUP + s) * 16)
                        for n in range(2):
                            ins = nc.tensor.matmul(acc_ps[:, 512 * n:512 * n + 512], dg[:, 1 - par, k - 2, :],
                                                   V[:, k, 512 * n:512 * n + 512], start=first and k == 2,
                                                   stop=last_group and k == GS - 1)
                            if k == 2 and n == 0:
                                ins.then_inc(g_dfree, 1)
                        if k < GS - 1 or not last_group:
                            ins.then_inc(g_pfree, 1)
                        else:
                            ins.then_inc(s_pe, 1)
                            pe.wait_ge(s_pe, 1)
                            pe.sem_inc(s_pe, -1)
                            pe.sem_inc(g_pfree, 1)
                            pe.sem_inc(g_accps, 1)

                def tail():
                    norm_rows(2, t_ln)
                    pe.wait_ge(t_lnfree, 1)
                    pe.sem_inc(t_lnfree, -1)

                pe.wait_ge(b_load, 80)
                pe.wait_ge(s_wq, 64)
                pe.sem_inc(s_wq, -64)
                for n in range(NPIECE):
                    piece(n, 0)
                with pe.Fori(0, T - 1) as t:
                    for s in range(NGROUP + 1):
                        if s:
                            gather(t, s, s % 2, s == 1, s == NGROUP)
                        for half in range(2):
                            if 2 * s + half in PIECES:
                                piece(PIECES.index(2 * s + half), t + 1)
                    tail()
                gather(T - 1, 1, 1, True)
                with pe.Fori(0, NGROUP // 2 - 1) as j:
                    gather(T - 1, 2 * j + 2, 0)
                    gather(T - 1, 2 * j + 3, 1)
                gather(T - 1, NGROUP, 0, False, True)
                tail()

            @block.scalar
            def _(act):
                def probs(hh):
                    act.wait_ge(b_sc_s, 1)
                    act.sem_inc(b_sc_s, -1)
                    for i in range(4):
                        h = 4 * hh + i
                        nc.scalar.activation(pr[:, i, CHUNK:CHUNK + 192], sc[:, i, :], ACT.Exp, bias=MX[:, h:h + 1],
                                             scale=float(AD) ** -0.5, accum_out=DEN[:, h:h + 1]).then_inc(s_act, 1)
                    act.wait_ge(s_act, 4)
                    act.sem_inc(s_act, -4)
                    act.sem_inc(b_pexp, 1)
                    nc.scalar.activation(SE[:, 4 * hh:4 * hh + 4], SE[:, 4 * hh:4 * hh + 4], ACT.Exp).then_inc(s_act, 1)
                    act.wait_ge(s_act, 1)
                    act.sem_inc(s_act, -1)
                    act.sem_inc(b_exp_s, 1)

                def turned():
                    act.wait_ge(b_prT_ps, 1)
                    act.sem_inc(b_prT_ps, -1)
                    nc.scalar.copy(flat(prT), b0[:, :]).then_inc(b_prT_done, 1)

                def level():
                    act.wait_ge(b_lvP, 1)
                    act.sem_inc(b_lvP, -1)
                    nc.scalar.copy(flat(Pm), g[0]).then_inc(b_lvPs, 1)

                def piece(n, t):
                    if n == 0:
                        act.wait_ge(b_tok_raw, 1)
                        act.sem_inc(b_tok_raw, -1)
                        nc.scalar.activation(flat(sq), banks[1][:, :], ACT.Square).then_inc(b_squared, 1)
                        nc.scalar.activation(EG, g[3][:, 0:16], ACT.Exp).then_inc(s_act, 1)
                        nc.scalar.copy(vtok[:, 0, :], g[3][:, 128:256]).then_inc(s_act, 1)
                        act.wait_ge(s_act, 2)
                        act.sem_inc(s_act, -2)
                        act.sem_inc(b_gexp, 1)
                    elif n == 1:
                        act.wait_ge(b_root_in, 1)
                        act.sem_inc(b_root_in, -1)
                        nc.scalar.activation(RS, SS, ACT.Sqrt).then_inc(b_root, 1)
                        probs(0)
                    elif n == 2:
                        act.wait_ge(b_tokT, 1)
                        act.sem_inc(b_tokT, -1)
                        nc.scalar.copy(flat(qk_ch[:, 0:8, :]), banks[1][:, :]).then_inc(s_act, 1)
                        nc.scalar.copy(flat(qk_ch[:, 8:12, :]), g[2]).then_inc(s_act, 1)
                        act.wait_ge(s_act, 2)
                        act.sem_inc(s_act, -2)
                        act.sem_inc(b_qkch, 1)
                        act.wait_ge(b_arg, 1)
                        act.sem_inc(b_arg, -1)
                        nc.scalar.activation(flat(DT), g[3], ACT.Exp).then_inc(b_decayed, 1)
                        turned()
                    elif n == 5:
                        level()
                        probs(1)
                    elif n == 6:
                        level()
                        turned()
                    elif n in (7, 9):
                        level()
                    elif n == 8:
                        level()
                        act.wait_ge(b_yaT_ps, 1)
                        act.sem_inc(b_yaT_ps, -1)
                        nc.scalar.copy(flat(yT[:, 0:4, :]), b0[:, 512:1024]).then_inc(b_yT_a, 1)
                    elif n == 10:
                        act.wait_ge(b_wk_ps, 1)
                        act.sem_inc(b_wk_ps, -1)
                        nc.scalar.copy(flat(wk), banks[1][:, :]).then_inc(b_wk_done, 1)
                    elif n == 14:
                        act.wait_ge(b_osq_in, 1)
                        act.sem_inc(b_osq_in, -1)
                        nc.scalar.activation(flat(on), g[3], ACT.Square).then_inc(b_osq, 1)
                    elif n == 15:
                        act.wait_ge(b_oroot_in, 1)
                        act.sem_inc(b_oroot_in, -1)
                        nc.scalar.activation(SO, SO, ACT.Sqrt).then_inc(b_oroot, 1)
                    elif n == 19:
                        act.wait_ge(b_lroot_in, 1)
                        act.sem_inc(b_lroot_in, -1)
                        nc.scalar.activation(stb[:, 14:15], stb[:, 14:15], ACT.Sqrt).then_inc(b_lroot, 1)
                    elif n == 20:
                        act.wait_ge(b_norm_in, 1)
                        act.sem_inc(b_norm_in, -1)
                        nc.scalar.activation(pre[:, :], pre[:, :], ACT.Identity, bias=stb[:, 15:16], scale=stb[:, 14:15]).then_inc(b_normed, 1)
                    elif n == 21:
                        act.wait_ge(b_h1T_ps, 1)
                        act.sem_inc(b_h1T_ps, -1)
                        nc.scalar.copy(flat(h1T), b0[:, :]).then_inc(b_h1T, 1)
                    elif n == 23:
                        act.wait_ge(b_q_ps, 1)
                        act.sem_inc(b_q_ps, -1)
                        nc.scalar.copy(flat(qT[:, 0:8, :]), banks[1][:, :]).then_inc(s_act, 1)
                    elif n == 25:
                        act.wait_ge(b_q_ps, 1)
                        act.sem_inc(b_q_ps, -1)
                        nc.scalar.copy(flat(qT[:, 8:16, :]), banks[2][:, :]).then_inc(s_act, 1)
                        act.wait_ge(s_act, 2)
                        act.sem_inc(s_act, -2)
                        act.sem_inc(b_qT, 1)
                    elif n == 34:
                        act.wait_ge(b_soft, 1)
                        act.sem_inc(b_soft, -1)
                        nc.scalar.activation(best, best, ACT.Exp).then_inc(b_exped, 1)

                def diagonals(par):
                    act.wait_ge(g_w, 1)
                    act.sem_inc(g_w, -1)
                    act.wait_ge(g_dfree, 1)
                    act.sem_inc(g_dfree, -1)
                    for k in range(2, GS):
                        nc.scalar.activation(dg[:, 1 - par, k - 2, :], ident, ACT.Copy, scale=gl[:, 1 - par, k:k + 1]).then_inc(g_diag, 1)

                def gelu(par):
                    act.wait_ge(g_dots, 1)
                    act.sem_inc(g_dots, -1)
                    nc.scalar.activation(gl[:, par, :], dots[:, par, :], ACT.Gelu).then_inc(g_gelu, 1)

                def tail():
                    act.wait_ge(t_root_in, 1)
                    act.sem_inc(t_root_in, -1)
                    nc.scalar.activation(st2[:, 14:15], st2[:, 14:15], ACT.Sqrt).then_inc(t_root, 1)
                    act.wait_ge(t_norm_in, 1)
                    act.sem_inc(t_norm_in, -1)
                    nc.scalar.activation(acc[:, :], acc[:, :], ACT.Identity, bias=st2[:, 15:16], scale=st2[:, 14:15]).then_inc(t_normed, 1)
                    act.wait_ge(t_out, 1)
                    act.sem_inc(t_out, -1)
                    act.dma_start(out[0, tail_rows(tail_t[0]), :], acc[:, :]).then_inc(t_stored, 16)

                act.sem_inc(g_dfree, 1)
                for n in range(NPIECE):
                    piece(n, 0)
                tail_t = [None]
                tail_rows = lambda t: bass.ts(t, P)
                with act.Fori(0, T - 1) as t:
                    for s in range(NGROUP + 1):
                        if s:
                            diagonals(s % 2)
                        if 2 * s in PIECES:
                            piece(PIECES.index(2 * s), t + 1)
                        if s < NGROUP:
                            gelu(s % 2)
                        if 2 * s + 1 in PIECES:
                            piece(PIECES.index(2 * s + 1), t + 1)
                    tail_t[0] = t
                    tail()
                gelu(0)
                with act.Fori(0, NGROUP // 2 - 1) as j:
                    for par in (1, 0):
                        diagonals(par)
                        gelu(par)
                diagonals(1)
                gelu(1)
                diagonals(0)
                tail_t[0] = T - 1
                tail()
                act.wait_ge(t_last, 1)
                act.sem_inc(t_last, -1)

            @block.vector
            def _(dve):
                def soften(hh):
                    dve.wait_ge(b_sc_ps, 1)
                    dve.sem_inc(b_sc_ps, -1)
                    for i in range(4):
                        nc.vector.scalar_tensor_tensor(sc[:, i, :], const("dist"), -float(AD) ** 0.5 * 2.0 ** -(4 * hh + i + 1),
                                                       b0[:, 256 * i:256 * i + 192], ALU.mult, ALU.add).then_inc(s_dve, 1)
                    dve.wait_ge(s_dve, 4)
                    dve.sem_inc(s_dve, -4)
                    mx, se = MX[:, 4 * hh:4 * hh + 4], SE[:, 4 * hh:4 * hh + 4]
                    nc.vector.reduce_max(mx, sc[:, :, :], AX.X).then_inc(s_dve, 1)
                    dve.wait_ge(s_dve, 1)
                    dve.sem_inc(s_dve, -1)
                    nc.vector.tensor_tensor(mx, mx, sink[:, 1, 4 * hh:4 * hh + 4], ALU.max).then_inc(s_dve, 1)
                    dve.wait_ge(s_dve, 1)
                    dve.sem_inc(s_dve, -1)
                    nc.vector.tensor_scalar(mx, mx, -float(AD) ** -0.5, None, ALU.mult).then_inc(s_dve, 1)
                    dve.wait_ge(s_dve, 1)
                    dve.sem_inc(s_dve, -1)
                    nc.vector.tensor_tensor(se, sink[:, 0, 4 * hh:4 * hh + 4], mx, ALU.add).then_inc(s_dve, 1)
                    dve.wait_ge(s_dve, 1)
                    dve.sem_inc(s_dve, -1)
                    dve.sem_inc(b_sc_s, 1)

                def divide(hh):
                    dve.wait_ge(b_exp_s, 1)
                    dve.sem_inc(b_exp_s, -1)
                    d, r = DEN[:, 4 * hh:4 * hh + 4], RD[:, 4 * hh:4 * hh + 4]
                    nc.vector.tensor_tensor(d, d, SE[:, 4 * hh:4 * hh + 4], ALU.add).then_inc(s_dve, 1)
                    dve.wait_ge(s_dve, 1)
                    dve.sem_inc(s_dve, -1)
                    nc.vector.reciprocal(r, d).then_inc(s_dve, 1)
                    dve.wait_ge(s_dve, 1)
                    dve.sem_inc(s_dve, -1)
                    dve.wait_ge(b_pv, 1)
                    dve.sem_inc(b_pv, -1)
                    nc.vector.tensor_tensor(ytok[:, 256 * hh:256 * hh + 256].rearrange("p (h d) -> p h d", d=AD),
                                            b0[:, 0:256].rearrange("p (h d) -> p h d", d=AD), bc3(r, AD), ALU.mult).then_inc(s_dve, 1)
                    dve.wait_ge(s_dve, 1)
                    dve.sem_inc(s_dve, -1)

                def mask(l):
                    nc.vector.tensor_tensor(ML[:, l % 2, :, :], MT, per_head(const("level")[:, l * P:(l + 1) * P]), ALU.mult).then_inc(s_dve, 1)
                    dve.wait_ge(s_dve, 1)
                    dve.sem_inc(s_dve, -1)
                    dve.sem_inc(b_lvM, 1)

                def grow(l):
                    if l == 0:
                        dve.wait_ge(b_lvP0, 1)
                        dve.sem_inc(b_lvP0, -1)
                        nc.vector.tensor_tensor(X, per_head(ident), heads(g[0]), ALU.subtract).then_inc(s_dve, 1)
                        nc.vector.tensor_tensor(XT, per_head(ident), ML[:, 0, :, :], ALU.subtract).then_inc(s_dve, 1)
                        dve.wait_ge(s_dve, 2)
                        dve.sem_inc(s_dve, -2)
                    else:
                        dve.wait_ge(b_lvQ, 1)
                        dve.sem_inc(b_lvQ, -1)
                        nc.vector.tensor_tensor(XT, XT, heads(g[2]), ALU.subtract).then_inc(s_dve, 1)
                        if l < 5:
                            nc.vector.tensor_tensor(X, X, heads(g[1]), ALU.subtract).then_inc(s_dve, 1)
                        dve.wait_ge(s_dve, 2 if l < 5 else 1)
                        dve.sem_inc(s_dve, -(2 if l < 5 else 1))
                    dve.sem_inc(b_lvX, 1)

                def new_values(c):
                    lo = 64 * c
                    dve.wait_ge(b_vps, 1)
                    dve.sem_inc(b_vps, -1)
                    nc.vector.tensor_tensor(vnew[lo:lo + 64, :, :], wk[lo:lo + 64, 0:BH, :], heads(g[2])[lo:lo + 64],
                                            ALU.subtract).then_inc(b_vnew, 1)

                def new_state(c):
                    nc.vector.tensor_tensor(St[:, :, :], St[:, :, :], bc3(e_last[:, 4 * c:4 * c + 4]), ALU.mult).then_inc(s_dve, 1)
                    dve.wait_ge(s_dve, 1)
                    dve.sem_inc(s_dve, -1)
                    nc.vector.tensor_tensor(St[:, :, :], St[:, :, :], heads(g[0]), ALU.add).then_inc(s_dve, 1)
                    dve.wait_ge(s_dve, 1)
                    dve.sem_inc(s_dve, -1)

                def statistics(x, st, s_root_in):
                    for half in range(2):
                        nc.vector.bn_stats(st[:, 6 * half:6 * half + 6], x[:, 512 * half:512 * half + 512]).then_inc(s_dve, 1)
                    dve.wait_ge(s_dve, 2)
                    dve.sem_inc(s_dve, -2)
                    nc.vector.bn_aggr(st[:, 12:14], st[:, 0:12]).then_inc(s_dve, 1)
                    dve.wait_ge(s_dve, 1)
                    dve.sem_inc(s_dve, -1)
                    nc.vector.tensor_scalar(st[:, 14:15], st[:, 13:14], LN_EPS, None, ALU.add).then_inc(s_dve, 1)
                    dve.wait_ge(s_dve, 1)
                    dve.sem_inc(s_dve, -1)
                    dve.sem_inc(s_root_in, 1)

                def norm_factors(st, s_root, s_norm_in):
                    dve.wait_ge(s_root, 1)
                    dve.sem_inc(s_root, -1)
                    nc.vector.reciprocal(st[:, 14:15], st[:, 14:15]).then_inc(s_dve, 1)
                    dve.wait_ge(s_dve, 1)
                    dve.sem_inc(s_dve, -1)
                    nc.vector.tensor_scalar(st[:, 15:16], st[:, 12:13], st[:, 14:15], -1.0, ALU.mult, ALU.mult).then_inc(s_dve, 1)
                    dve.wait_ge(s_dve, 1)
                    dve.sem_inc(s_dve, -1)
                    dve.sem_inc(s_norm_in, 1)

                def find(h0, h1, width, values, order, ids, left):
                    for h in range(h0, h1):
                        nc.vector.max_index(ids[:, h, 0:8], order[:, h, 0:8], values(h)).then_inc(s_dve, 1)
                        nc.vector.match_replace(left[:, h, :], order[:, h, 0:8], values(h), LEAST).then_inc(s_dve, 1)
                    dve.wait_ge(s_dve, 2 * (h1 - h0))
                    dve.sem_inc(s_dve, -(2 * (h1 - h0)))

                score = lambda hp: banks[hp // 8][:, (hp % 8) * P:(hp % 8 + 1) * P]

                def piece(n, t):
                    beta = gates[:, 1, t, :]
                    if n == 1:
                        nc.vector.tensor_tensor(gU, per_head(const("upto")), bc3(gates[:, 0, t, :]), ALU.mult).then_inc(s_dve, 1)
                        nc.vector.tensor_tensor(bI, per_head(ident), bc3(beta), ALU.mult).then_inc(s_dve, 1)
                        nc.vector.tensor_scalar(NG4, gates[:, 0, t, :], -1.0, None, ALU.mult).then_inc(s_dve, 1)
                        dve.wait_ge(s_dve, 3)
                        dve.sem_inc(s_dve, -3)
                        dve.sem_inc(b_gu, 1)
                        dve.wait_ge(b_squared, 1)
                        dve.sem_inc(b_squared, -1)
                        nc.vector.reduce_sum(SS, sq, AX.X).then_inc(s_dve, 1)
                        dve.wait_ge(s_dve, 1)
                        dve.sem_inc(s_dve, -1)
                        nc.vector.tensor_scalar(SS, SS, NORM_EPS, None, ALU.add).then_inc(s_dve, 1)
                        dve.wait_ge(s_dve, 1)
                        dve.sem_inc(s_dve, -1)
                        dve.sem_inc(b_root_in, 1)
                        soften(0)
                    elif n == 2:
                        dve.wait_ge(b_root, 1)
                        dve.sem_inc(b_root, -1)
                        dve.wait_ge(b_gexp, 1)
                        dve.sem_inc(b_gexp, -1)
                        nc.vector.reciprocal(RS, RS).then_inc(s_dve, 1)
                        dve.wait_ge(s_dve, 1)
                        dve.sem_inc(s_dve, -1)
                        nc.vector.tensor_scalar(CO[:, 0, :], RS[:, 0:4], float(BD) ** -0.5, None, ALU.mult).then_inc(s_dve, 1)
                        nc.vector.tensor_copy(CO[:, 2, :], RS[:, 4:8]).then_inc(s_dve, 1)
                        nc.vector.tensor_tensor(CO[:, 3, :], RS[:, 4:8], e_rest, ALU.mult).then_inc(s_dve, 1)
                        nc.vector.tensor_tensor(CO[:, 4, :], RS[:, 4:8], e_gc, ALU.mult).then_inc(s_dve, 1)
                        dve.wait_ge(s_dve, 4)
                        dve.sem_inc(s_dve, -4)
                        nc.vector.tensor_tensor(CO[:, 1, :], CO[:, 0, :], e_gc, ALU.mult).then_inc(s_dve, 1)
                        nc.vector.tensor_tensor(CO[:, 4, :], CO[:, 4, :], beta, ALU.mult).then_inc(s_dve, 1)
                        dve.wait_ge(s_dve, 2)
                        dve.sem_inc(s_dve, -2)
                        for dst, src, i in ((qk_tok[:, 0:4, :], g[0], 0), (qk_tok[:, 4:8, :], g[0], 1), (qk_tok[:, 8:12, :], g[1], 2),
                                            (kdec, g[1], 3), (kbe, g[1], 4)):
                            nc.vector.tensor_tensor(dst, heads(src), bc3(CO[:, i, :]), ALU.mult).then_inc(s_dve, 1)
                        nc.vector.tensor_tensor(vb, heads(g[2]), bc3(beta), ALU.mult).then_inc(s_dve, 1)
                        dve.wait_ge(s_dve, 6)
                        dve.sem_inc(s_dve, -6)
                        dve.sem_inc(b_tok_done, 1)
                    elif n == 4:
                        divide(0)
                        dve.sem_inc(b_pv_read, 1)
                        dve.wait_ge(b_decayed, 1)
                        dve.sem_inc(b_decayed, -1)
                        dve.wait_ge(b_kk, 1)
                        dve.sem_inc(b_kk, -1)
                        nc.vector.tensor_tensor(MT, DT, heads(g[2]), ALU.mult).then_inc(s_dve, 1)
                        dve.wait_ge(s_dve, 1)
                        dve.sem_inc(s_dve, -1)
                        nc.vector.tensor_tensor(MT, MT, heads(g[0]), ALU.mult).then_inc(s_dve, 1)
                        dve.wait_ge(s_dve, 1)
                        dve.sem_inc(s_dve, -1)
                        nc.vector.tensor_tensor(intraT, DT, heads(g[1]), ALU.mult).then_inc(s_dve, 1)
                        dve.wait_ge(s_dve, 1)
                        dve.sem_inc(s_dve, -1)
                        mask(0)
                        mask(1)
                    elif n == 5:
                        grow(0)
                        soften(1)
                        nc.vector.tensor_copy(const("dist")[:, 0:CHUNK], const("dist_past")).then_inc(s_dve, 1)
                        dve.wait_ge(s_dve, 1)
                        dve.sem_inc(s_dve, -1)
                    elif n in (6, 7, 8, 9):
                        grow(n - 5)
                        mask(n - 4)
                        if n == 8:
                            divide(1)
                            dve.sem_inc(b_ya, 1)
                    elif n == 10:
                        grow(5)
                    elif n == 11:
                        new_values(0)
                    elif n == 12:
                        dve.wait_ge(b_o_ds, 1)
                        dve.sem_inc(b_o_ds, -1)
                        new_state(0)
                        dve.sem_inc(b_state, 1)
                    elif n == 13:
                        new_values(1)
                    elif n == 14:
                        dve.wait_ge(b_o_ds, 1)
                        dve.sem_inc(b_o_ds, -1)
                        dve.sem_inc(b_osq_in, 1)
                        new_state(1)
                        nc.vector.tensor_copy(vtok[:, 1, :], vtok[:, 0, :]).then_inc(s_dve, 1)
                        dve.wait_ge(s_dve, 1)
                        dve.sem_inc(s_dve, -1)
                    elif n == 15:
                        dve.wait_ge(b_osq, 1)
                        dve.sem_inc(b_osq, -1)
                        nc.vector.reduce_sum(SO, on, AX.X).then_inc(s_dve, 1)
                        dve.wait_ge(s_dve, 1)
                        dve.sem_inc(s_dve, -1)
                        nc.vector.tensor_scalar(SO, SO, 1.0 / BD, NORM_EPS, ALU.mult, ALU.add).then_inc(s_dve, 1)
                        dve.wait_ge(s_dve, 1)
                        dve.sem_inc(s_dve, -1)
                        dve.sem_inc(b_oroot_in, 1)
                    elif n == 16:
                        dve.wait_ge(b_oroot, 1)
                        dve.sem_inc(b_oroot, -1)
                        nc.vector.reciprocal(SO, SO).then_inc(s_dve, 1)
                        dve.wait_ge(s_dve, 1)
                        dve.sem_inc(s_dve, -1)
                        nc.vector.tensor_tensor(on, heads(g[3]), bc3(SO), ALU.mult).then_inc(b_on_ready, 1)
                    elif n == 17:
                        dve.wait_ge(b_onT_ps, 1)
                        dve.sem_inc(b_onT_ps, -1)
                        nc.vector.tensor_tensor(yT[:, 4:8, :], zt, heads(g[1]), ALU.mult).then_inc(s_dve, 1)
                        dve.wait_ge(s_dve, 1)
                        dve.sem_inc(s_dve, -1)
                        dve.sem_inc(b_yT_b, 1)
                        dve.sem_inc(b_raw_free, 1)
                        dve.sem_inc(b_o_done, 1)
                    elif n == 19:
                        dve.wait_ge(b_mix_ps, 1)
                        dve.sem_inc(b_mix_ps, -1)
                        dve.wait_ge(b_pre_in, 16)
                        dve.sem_inc(b_pre_in, -16)
                        nc.vector.scalar_tensor_tensor(pre[:, :], pre[:, :], ALPHA, b0[:, :], ALU.mult, ALU.add).then_inc(s_dve, 1)
                        dve.wait_ge(s_dve, 1)
                        dve.sem_inc(s_dve, -1)
                        statistics(pre, stb, b_lroot_in)
                    elif n == 20:
                        norm_factors(stb, b_lroot, b_norm_in)
                    elif n == 21:
                        dve.wait_ge(b_normed, 1)
                        dve.sem_inc(b_normed, -1)
                        nc.vector.tensor_tensor(pre[:, :], pre[:, :], banks[1][:, :], ALU.mult).then_inc(s_dve, 1)
                        dve.wait_ge(s_dve, 1)
                        dve.sem_inc(s_dve, -1)
                        nc.vector.tensor_tensor(h1n[:, :], pre[:, :], banks[2][:, :], ALU.add).then_inc(s_dve, 1)
                        dve.wait_ge(s_dve, 1)
                        dve.sem_inc(s_dve, -1)
                        dve.sem_inc(b_h1, 1)
                        dve.sem_inc(b_pre_free, 1)
                    elif n == 27:
                        dve.wait_ge(b_scores, 1)
                        dve.sem_inc(b_scores, -1)
                        for hp in range(2 * PH):
                            nc.vector.max(top[:, hp, 0:8], score(hp)).then_inc(s_dve, 1)
                        dve.wait_ge(s_dve, 2 * PH)
                        dve.sem_inc(s_dve, -(2 * PH))
                    elif n == 28:
                        find(0, PH, NK, score, top, itop, rest)
                    elif n == 29:
                        find(PH, 2 * PH, NK, score, top, itop, rest)
                        dve.sem_inc(b_scores_read, 1)
                    elif n == 30:
                        for hp in range(2 * PH):
                            nc.vector.max(top[:, hp, 8:16], rest[:, hp, :]).then_inc(s_dve, 1)
                        dve.wait_ge(s_dve, 2 * PH)
                        dve.sem_inc(s_dve, -(2 * PH))
                    elif n == 31:
                        for hp in range(2 * PH):
                            nc.vector.max_index(itop[:, hp, 8:16], top[:, hp, 8:16], rest[:, hp, :]).then_inc(s_dve, 1)
                        dve.wait_ge(s_dve, 2 * PH)
                        dve.sem_inc(s_dve, -(2 * PH))
                    elif n == 32:
                        nc.vector.tensor_copy(ftop.rearrange("p h q k -> p (h q k)"), flat(itop)).then_inc(s_dve, 1)
                        dve.wait_ge(s_dve, 1)
                        dve.sem_inc(s_dve, -1)
                        nc.vector.tensor_scalar(ftop[:, :, 0, :], ftop[:, :, 0, :], float(NK), None, ALU.mult).then_inc(s_dve, 1)
                        dve.wait_ge(s_dve, 1)
                        dve.sem_inc(s_dve, -1)
                        tv = top.rearrange("p (h q) k -> p h q k", q=2)
                        for dst, src in ((cand, tv), (cid, ftop)):
                            for i0, i1, w, at in PAIR_ROWS:
                                o = dst[:, :, at:at + (i1 - i0) * w].rearrange("p h (i j) -> p h i j", j=w)
                                nc.vector.tensor_tensor(o, src[:, :, 0, i0:i1].unsqueeze(3).to_broadcast([P, PH, i1 - i0, w]),
                                                        src[:, :, 1, 0:w].unsqueeze(2).to_broadcast([P, PH, i1 - i0, w]),
                                                        ALU.add).then_inc(s_dve, 1)
                        dve.wait_ge(s_dve, 2 * len(PAIR_ROWS))
                        dve.sem_inc(s_dve, -(2 * len(PAIR_ROWS)))
                    elif n == 33:
                        for h in range(PH):
                            nc.vector.max(best[:, h, 0:8], cand[:, h, :]).then_inc(s_dve, 1)
                        dve.wait_ge(s_dve, PH)
                        dve.sem_inc(s_dve, -PH)
                        find(0, PH, NCAND, lambda h: cand[:, h, :], best, ibest, crest)
                    elif n == 34:
                        for h in range(PH):
                            nc.vector.max(best[:, h, 8:16], crest[:, h, :]).then_inc(s_dve, 1)
                        dve.wait_ge(s_dve, PH)
                        dve.sem_inc(s_dve, -PH)
                        for h in range(PH):
                            nc.vector.max_index(ibest[:, h, 8:16], best[:, h, 8:16], crest[:, h, :]).then_inc(s_dve, 1)
                        dve.wait_ge(s_dve, PH)
                        dve.sem_inc(s_dve, -PH)
                        nc.vector.tensor_copy(fbest, ibest).then_inc(s_dve, 1)
                        dve.wait_ge(s_dve, 1)
                        dve.sem_inc(s_dve, -1)
                        nc.vector.tensor_copy(den[:, 0, :], best[:, :, 0]).then_inc(s_dve, 1)
                        dve.wait_ge(s_dve, 1)
                        dve.sem_inc(s_dve, -1)
                        nc.vector.tensor_tensor(best, best, den[:, 0, :].unsqueeze(2).to_broadcast([P, PH, TOPK]), ALU.subtract).then_inc(s_dve, 1)
                        dve.wait_ge(s_dve, 1)
                        dve.sem_inc(s_dve, -1)
                        dve.sem_inc(b_soft, 1)
                    elif 35 <= n <= 38:
                        for h in range(2 * (n - 35), 2 * (n - 35) + 2):
                            nc.vector.tensor_tensor(eq, const("iota50").unsqueeze(1).to_broadcast([P, TOPK, NCAND]),
                                                    fbest[:, h, :].unsqueeze(2).to_broadcast([P, TOPK, NCAND]), ALU.is_equal).then_inc(s_dve, 1)
                            dve.wait_ge(s_dve, 1)
                            dve.sem_inc(s_dve, -1)
                            nc.vector.tensor_tensor(eq, eq, cid[:, h, :].unsqueeze(1).to_broadcast([P, TOPK, NCAND]), ALU.mult).then_inc(s_dve, 1)
                            dve.wait_ge(s_dve, 1)
                            dve.sem_inc(s_dve, -1)
                            nc.vector.reduce_sum(fex[:, h, :], eq, AX.X).then_inc(s_dve, 1)
                            dve.wait_ge(s_dve, 1)
                            dve.sem_inc(s_dve, -1)
                    elif n == 39:
                        nc.vector.tensor_copy(eidx_n[:, :], flat(fex)).then_inc(s_dve, 1)
                        dve.wait_ge(s_dve, 1)
                        dve.sem_inc(s_dve, -1)
                        dve.wait_ge(b_exped, 1)
                        dve.sem_inc(b_exped, -1)
                        nc.vector.reduce_sum(den[:, 0, :], best, AX.X).then_inc(s_dve, 1)
                        dve.wait_ge(s_dve, 1)
                        dve.sem_inc(s_dve, -1)
                        nc.vector.reciprocal(den[:, 1, :], den[:, 0, :]).then_inc(s_dve, 1)
                        dve.wait_ge(s_dve, 1)
                        dve.sem_inc(s_dve, -1)
                        nc.vector.tensor_tensor(egate_n[:, :].rearrange("p (h k) -> p h k", h=PH), best,
                                                den[:, 1, :].unsqueeze(2).to_broadcast([P, PH, TOPK]), ALU.mult).then_inc(s_dve, 1)
                        dve.wait_ge(s_dve, 1)
                        dve.sem_inc(s_dve, -1)

                def dot(t, s, par, k):
                    dve.wait_ge(g_u[k], (t * NGROUP + s) * 16 + 16)
                    return nc.vector.tensor_tensor_reduce(out=U[:, k, :], in0=U[:, k, :], in1=h1c[:, :], scale=1.0, scalar=0.0,
                                                          op0=ALU.mult, op1=ALU.add, accum_out=dots[:, par, k:k + 1])

                def add(t, s, par, k, first):
                    dve.wait_ge(g_v[k], (t * NGROUP + s) * 16)
                    w = gl[:, 1 - par, k:k + 1]
                    if first and k == 0:
                        return nc.vector.tensor_scalar(acc[:, :], V[:, 0, :], w, None, ALU.mult)
                    return nc.vector.scalar_tensor_tensor(out=acc[:, :], in0=V[:, k, :], scalar=w, in1=acc[:, :],
                                                          op0=ALU.mult, op1=ALU.add)

                def weigh(s, par):
                    dve.wait_ge(g_gelu, 1)
                    dve.sem_inc(g_gelu, -1)
                    w = gl[:, 1 - par, :]
                    nc.vector.tensor_tensor(w, w, egate[:, bass.ds(s * GS - GS, GS)], ALU.mult).then_inc(s_dve, 1)
                    dve.wait_ge(s_dve, 1)
                    dve.sem_inc(s_dve, -1)
                    dve.sem_inc(g_w, 1)
                    dve.sem_inc(g_ufree, 1)

                def gather_a(t, s, par, first=False):
                    weigh(s, par)
                    dot(t, s, par, 0).then_inc(g_ufree, 1)
                    if first:
                        dve.wait_ge(t_stored, 16)
                        dve.sem_inc(t_stored, -16)
                    add(t, s, par, 0, first).then_inc(g_vfree, 1)
                    dot(t, s, par, 1).then_inc(g_seq, 1)

                def gather_b(t, s, par):
                    dot(t, s, par, 2).then_inc(g_ufree, 2)
                    dve.wait_ge(g_seq, 1)
                    dve.sem_inc(g_seq, -1)
                    add(t, s, par, 1, False).then_inc(g_vfree, 1)
                    dot(t, s, par, 3).then_inc(g_dots, 1)

                def gather_first(t):
                    for k in range(GS):
                        dot(t, 0, 0, k).then_inc(g_ufree if k < GS - 1 else g_dots, 1)

                def gather_last(t):
                    weigh(NGROUP, 0)
                    for k in range(2):
                        add(t, NGROUP, 0, k, False).then_inc(s_dve, 1)
                        dve.wait_ge(s_dve, 1)
                        dve.sem_inc(s_dve, -1)
                        dve.sem_inc(g_vfree, 1)

                def start_tile():
                    nc.vector.tensor_copy(eidx[:, :], eidx_n[:, :]).then_inc(s_dve, 1)
                    nc.vector.tensor_copy(egate[:, :], egate_n[:, :]).then_inc(s_dve, 1)
                    dve.wait_ge(s_dve, 2)
                    dve.sem_inc(s_dve, -2)
                    dve.sem_inc(g_tile, 1)
                    nc.vector.tensor_copy(h1c[:, :], h1n[:, :]).then_inc(s_dve, 1)
                    dve.wait_ge(s_dve, 1)
                    dve.sem_inc(s_dve, -1)

                def finish_sum():
                    dve.wait_ge(g_accps, 1)
                    dve.sem_inc(g_accps, -1)
                    nc.vector.tensor_tensor(acc[:, :], acc[:, :], acc_ps[:, :], ALU.add).then_inc(s_dve, 1)
                    dve.wait_ge(s_dve, 1)
                    dve.sem_inc(s_dve, -1)
                    dve.sem_inc(g_accfree, 1)
                    nc.vector.scalar_tensor_tensor(acc[:, :], h1c[:, :], ALPHA, acc[:, :], ALU.mult, ALU.add).then_inc(s_dve, 1)
                    dve.wait_ge(s_dve, 1)
                    dve.sem_inc(s_dve, -1)

                def tail():
                    statistics(acc, st2, t_root_in)
                    norm_factors(st2, t_root, t_norm_in)
                    dve.wait_ge(t_normed, 1)
                    dve.sem_inc(t_normed, -1)
                    dve.wait_ge(t_ln, 1)
                    dve.sem_inc(t_ln, -1)
                    nc.vector.tensor_tensor(acc[:, :], acc[:, :], banks[1][:, :], ALU.mult).then_inc(s_dve, 1)
                    dve.wait_ge(s_dve, 1)
                    dve.sem_inc(s_dve, -1)
                    nc.vector.tensor_tensor(acc[:, :], acc[:, :], banks[2][:, :], ALU.add).then_inc(s_dve, 1)
                    dve.wait_ge(s_dve, 1)
                    dve.sem_inc(s_dve, -1)
                    dve.sem_inc(t_lnfree, 1)
                    dve.sem_inc(t_out, 1)

                dve.sem_inc(b_raw_free, 1)
                dve.sem_inc(b_pre_free, 1)
                dve.sem_inc(b_wo_free0, 1)
                dve.sem_inc(b_wo_free1, 1)
                dve.sem_inc(g_ufree, GS)
                dve.sem_inc(g_vfree, 2)
                dve.sem_inc(g_pfree, 2)
                dve.sem_inc(g_accfree, 1)
                dve.sem_inc(t_stored, 16)
                dve.wait_ge(b_load, 80)
                nc.vector.tensor_scalar(sink[:, 1, :], sink[:, 0, :], float(AD) ** 0.5, None, ALU.mult).then_inc(s_dve, 1)
                nc.vector.memset(vtok[:, 1, :], 0.0).then_inc(s_dve, 1)
                nc.vector.memset(pr[:, :, :], 0.0).then_inc(s_dve, 1)
                nc.vector.memset(St[:, :, :], 0.0).then_inc(s_dve, 1)
                dve.wait_ge(s_dve, 4)
                dve.sem_inc(s_dve, -4)
                for n in range(NPIECE):
                    piece(n, 0)
                start_tile()
                with dve.Fori(0, T - 1) as t:
                    for s in range(NGROUP + 1):
                        if s == 0:
                            gather_first(t)
                        elif s == NGROUP:
                            gather_last(t)
                        else:
                            gather_a(t, s, s % 2, s == 1)
                        if 2 * s in PIECES:
                            piece(PIECES.index(2 * s), t + 1)
                        if 0 < s < NGROUP:
                            gather_b(t, s, s % 2)
                        if 2 * s + 1 in PIECES:
                            piece(PIECES.index(2 * s + 1), t + 1)
                    finish_sum()
                    start_tile()
                    tail()
                gather_first(T - 1)
                gather_a(T - 1, 1, 1, True)
                gather_b(T - 1, 1, 1)
                with dve.Fori(0, NGROUP // 2 - 1) as j:
                    for par in range(2):
                        gather_a(T - 1, 2 * j + (2 + par), par)
                        gather_b(T - 1, 2 * j + (2 + par), par)
                gather_last(T - 1)
                finish_sum()
                tail()
                dve.wait_ge(t_stored, 16)
                dve.sem_inc(t_stored, -16)
                dve.sem_inc(t_last, 1)
        b.close()


_INS = ['x', 'ln_in_g', 'ln_in_b', 'w_in', 'conv_w', 'a_sinks', 'b_a_log', 'b_dt_bias', 'b_norm_w', 'w_out',
        'ln1_g', 'ln1_b', 'w_query', 'sub_keys', 'expert_u', 'expert_v', 'ln2_g', 'ln2_b']


def kernel(**inputs):
    import numpy as _np
    import concourse.bacc as _bacc
    from concourse import mybir as _mybir
    from concourse.bass_utils import run_bass_kernel_spmd as _run

    nc = _bacc.Bacc("TRN2", target_bir_lowering=False, num_devices=1)
    arrays, args = {}, []
    arrays["constants"] = constant_table()
    args.append(nc.dram_tensor("constants", (P, NCONST), _mybir.dt.float32, kind="ExternalInput").ap())
    for name in _INS:
        a = _np.ascontiguousarray(inputs[name])
        arrays[f"in_{name}"] = a
        args.append(nc.dram_tensor(f"in_{name}", a.shape, _mybir.dt.from_np(a.dtype), kind="ExternalInput").ap())
    args.append(nc.dram_tensor("out_0", (1, S, D), _mybir.dt.float32, kind="ExternalOutput").ap())
    build(nc, *args)
    r = _run(nc, [arrays], core_ids=[0])
    return r.results[0]["out_0"]
```

```python
import concourse.bass as bass
from concourse import mybir
from contextlib import ExitStack
import numpy as np

P = 128
S = 1024
D = 1024
T = S // P
KD = D // P
CHUNK = 64
AH, AKV, AD = 8, 2, 64
BH, BD = 4, 128
TAPS = 4
PH, NK, TOPK = 8, 128, 16
SLOTS = PH * TOPK
NCQ = AH * AD // P
NCONV = 3 * BH
NZ = BH
IN_W = 2824
AV, CONV0, Z0 = NCQ, NCQ + 1, NCQ + 1 + NCONV
NPROJ = Z0 + NZ
PAIR_ROWS = [(0, 1, 16, 0), (1, 2, 8, 16), (2, 3, 5, 24), (3, 4, 4, 29), (4, 5, 3, 33), (5, 8, 2, 36), (8, 16, 1, 42)]
NCAND = 50
LEAST = -3.0e38
GS = 4
NGROUP = SLOTS // GS
NPIECE = 49
VECTOR_AT = [6, 8, 10, 12, 14, 16, 18, 19, 21, 22, 23, 24, 26, 27, 29, 30, 31, 33, 34, 35, 37, 38, 39] + [40] * 8 + [
    45, 46, 47, 48, 49, 50, 51, 52, 53, 54, 55, 56, 57, 58, 59, 60, 61, 62]
TENSOR_AT = [6, 8, 10, 12, 14, 16, 18, 19, 21, 22, 23, 24, 26, 27, 28, 30, 32, 33, 34, 35, 37, 38, 39,
             40, 40, 41, 42, 42, 43, 44, 44, 45, 46, 48] + VECTOR_AT[34:]
SCALAR_AT = [7, 8, 11, 12, 14, 16, 18, 19, 21, 22, 23, 24, 26, 27, 29, 30, 32, 33, 34, 35, 37, 38, 39,
             40, 40, 41, 42, 43, 43, 44, 45, 45] + VECTOR_AT[32:]
PLAIN = 2
ON_VECTOR = [2, 2, 2, 2, 2, 1] + [2] * 14 + [4] * 3 + [0] * 9 + [2]
ARENA = 9216
LN_EPS = 1e-5
NORM_EPS = 1e-6
ALPHA = 2.0 ** 0.25
NEG = -1.0e30
FAR = 1.0e30

CONST_COLS = {}
_at = 0
for _name, _n in (("ident", P), ("upto", P), ("after", P), ("decay_mask", P), ("ones", P), ("chunk_of", 2 * P),
                  ("level", 6 * P), ("dist", 192), ("dist_past", 64), ("iota50", 50)):
    CONST_COLS[_name] = (_at, _at + _n)
    _at += _n
NCONST = _at


def pieces(table, half):
    return [n for n in range(NPIECE) if table[n] == half]


def constant_table():
    t = np.zeros((P, NCONST), np.float32)

    def put(name, a):
        lo, hi = CONST_COLS[name]
        t[:, lo:hi] = a.reshape(a.shape[0], -1)

    r = np.arange(P)
    same = (r[:, None] // CHUNK) == (r[None, :] // CHUNK)
    put("ident", np.eye(P, dtype=np.float32))
    put("upto", (same & (r[:, None] <= r[None, :])).astype(np.float32))
    put("after", (same & (r[:, None] > r[None, :])).astype(np.float32))
    put("decay_mask", np.where(same & (r[:, None] <= r[None, :]), 0.0, NEG).astype(np.float32))
    put("ones", np.ones((P, P), np.float32))
    put("chunk_of", np.stack([np.repeat((r // CHUNK == c)[:, None], P, 1) for c in range(2)], 1).astype(np.float32))
    lv = []
    for l in range(6):
        b = 1 << l
        j, i = r[:, None], r[None, :]
        lv.append((j // (2 * b) == i // (2 * b)) & (j % (2 * b) < b) & (i % (2 * b) >= b))
    put("level", np.stack(lv, 1).astype(np.float32))
    q = np.arange(P)[:, None]
    k = np.arange(192)[None, :] - 64
    qc, kc = q // 64, np.floor_divide(k, 64)
    ok = (kc == qc) | (kc == qc - 1)
    dist = np.where(ok, np.abs(q - k), FAR).astype(np.float32)
    put("dist_past", dist[:, 0:64])
    dist[:, 0:64] = FAR
    put("dist", dist)
    put("iota50", np.tile(np.arange(50, dtype=np.float32)[None], (P, 1)))
    return t


def build(nc, consts, x, ln_in_g, ln_in_b, w_in, conv_w, a_sinks, b_a_log, b_dt_bias, b_norm_w, w_out,
          ln1_g, ln1_b, w_query, sub_keys, expert_u, expert_v, ln2_g, ln2_b, out):
    fp32, u32 = mybir.dt.float32, mybir.dt.uint32
    ALU, ACT, AX = mybir.AluOpType, mybir.ActivationFunctionType, mybir.AxisListType

    ctx = ExitStack()
    with ctx:
        def sb(name, shape, dt=fp32, c=ctx):
            return c.enter_context(nc.sbuf_tensor(name, shape, dt))

        scope = [ctx]

        def sem(name):
            return scope[0].enter_context(nc.semaphore(name))

        s_dve = sem("s_dve")
        s_act = sem("s_act")
        s_pool = sem("s_pool")

        C = sb("C", [P, NCONST])

        def const(name):
            lo, hi = CONST_COLS[name]
            return C[:, lo:hi]

        ident = const("ident")
        nhalf = sb("nhalf", [P, 8])
        banks = [ctx.enter_context(nc.psum_tensor(f"bank{i}", [P, 1024], fp32)) for i in range(4)]

        proj_dram = nc.dram_tensor("proj_dram", (P, NPROJ, S), fp32).ap()
        h_dram = nc.dram_tensor("h_dram", (T, P, D), fp32).ap()
        ak_dram = nc.dram_tensor("ak_dram", (P, CHUNK + S), fp32).ap()
        gates = sb("gates", [P, 2, T, BH])

        wq = sb("wq", [P, KD, 2 * PH * P])
        skT = sb("skT", [P, 2 * PH, P])
        s_wq = sem("s_wq")
        s_sk = sem("s_sk")

        a = ExitStack()
        scope[0] = a
        XB = 4
        hT = sb("hT", [P, KD, S], c=a)
        cw = sb("cw", [P, TAPS * NCONV + 1], c=a)
        bc = sb("bc", [P, 2 * D], c=a)
        skr = sb("skr", [P, 2 * PH, P], c=a)
        xin = sb("xin", [P, XB, D], c=a)
        wbuf = sb("wbuf", [P, 2, KD, P], c=a)
        ybuf = sb("ybuf", [P, 2, S], c=a)
        obuf = sb("obuf", [P, 2, S], c=a)
        zpad = sb("zpad", [P, CHUNK], c=a)
        st = sb("st", [P, XB, 18], c=a)
        wab = sb("wab", [P, KD, 8], c=a)
        abT = sb("abT", [8, S], c=a)
        cwr = sb("cwr", [TAPS * NCONV + 1, P], c=a)
        hb = sb("hb", [P, 2, BH], c=a)
        gt = sb("gt", [P, 6, T * BH], c=a)

        s_const = sem("s_const")
        s_small = sem("s_small")
        s_x = [sem(f"s_x{u}") for u in range(XB)]
        s_stats = [sem(f"s_stats{u}") for u in range(XB)]
        s_norm = [sem(f"s_norm{u}") for u in range(XB)]
        s_h_pe = [sem(f"s_h_pe{u}") for u in range(XB)]
        s_h_out = [sem(f"s_h_out{u}") for u in range(XB)]
        s_hT_ps = [sem(f"s_hT_ps{u}") for u in range(2)]
        s_x_free = [sem(f"s_x_free{u}") for u in range(XB)]
        s_tr_free = [sem(f"s_tr_free{u}") for u in range(2)]
        s_hT = sem("s_hT")
        s_w = [sem(f"s_w{u}") for u in range(2)]
        s_w_free = [sem(f"s_w_free{u}") for u in range(2)]
        s_proj = [sem(f"s_proj{u}") for u in range(2)]
        s_proj_free = [sem(f"s_proj_free{u}") for u in range(2)]
        s_tap0 = [sem(f"s_tap0{u}") for u in range(2)]
        s_conv = [sem(f"s_conv{u}") for u in range(2)]
        s_y_free = [sem(f"s_y_free{u}") for u in range(2)]
        s_cw_ps = sem("s_cw_ps")
        s_cw = sem("s_cw")
        s_ab_ps = sem("s_ab_ps")
        s_abT = sem("s_abT")
        s_ab_tok = sem("s_ab_tok")
        s_soft = sem("s_soft")
        s_soft2 = sem("s_soft2")
        s_pad = sem("s_pad")
        s_root_in = sem("s_root_in")
        s_root = sem("s_root")
        s_pad_out = sem("s_pad_out")
        s_sk_ps = sem("s_sk_ps")
        s_stored = [sem(f"s_stored{u}") for u in range(2)]

        NTAP = TAPS * NCONV
        w_in_v = w_in[0].rearrange("(k p) e -> p k e", p=P)
        x_v = x[0].rearrange("(t p) d -> t p d", p=P)

        with nc.Block() as block:
            @block.sync
            def _(sp):
                sp.dma_start(C[:, :], consts).then_inc(s_const, 16)
                sp.dma_start(bc[:, 0:D], ln_in_g.partition_broadcast(P)).then_inc(s_small, 16)
                sp.dma_start(bc[:, D:2 * D], ln_in_b.partition_broadcast(P)).then_inc(s_small, 16)
                sp.dma_start(cwr[0:NTAP, :], conv_w[0].rearrange("t (c p) -> (t c) p", p=P)).then_inc(s_small, 16)
                sp.dma_start(cwr[NTAP:NTAP + 1, :], b_norm_w).then_inc(s_small, 16)
                sp.dma_start(hb[:, 0, :], b_dt_bias[0].partition_broadcast(P)).then_inc(s_small, 16)
                sp.dma_start(hb[:, 1, :], b_a_log[0].partition_broadcast(P)).then_inc(s_small, 16)
                sp.dma_start(wab[:, :, :], w_in_v[:, :, IN_W - 8:IN_W]).then_inc(s_small, 16)
                with sp.Fori(0, T // XB) as j:
                    for u in range(XB):
                        sp.wait_ge(s_x_free[u], 1)
                        sp.sem_inc(s_x_free[u], -1)
                        sp.wait_ge(s_h_out[u], 16)
                        sp.sem_inc(s_h_out[u], -16)
                        sp.dma_start(xin[:, u, :], x_v[XB * j + u]).then_inc(s_x[u], 16)
                for u in range(XB):
                    sp.wait_ge(s_h_out[u], 16)
                    sp.sem_inc(s_h_out[u], -16)
                with sp.Fori(0, NCQ // 2) as j:
                    for u in range(2):
                        sp.wait_ge(s_w_free[u], 1)
                        sp.sem_inc(s_w_free[u], -1)
                        for half in range(2):
                            sp.dma_start(wbuf[:, u, :, 64 * half:64 * half + 64],
                                         w_in_v[:, :, bass.ds(j * 128 + u * 64 + 256 * half, 64)]).then_inc(s_w[u], 16)
                with sp.Fori(0, (2 + NCONV + NZ) // 2) as j:
                    for u in range(2):
                        sp.wait_ge(s_w_free[u], 1)
                        sp.sem_inc(s_w_free[u], -1)
                        sp.dma_start(wbuf[:, u, :, :],
                                     w_in_v[:, :, bass.ds(j * 256 + (NCQ + u) * P, P)]).then_inc(s_w[u], 16)
                sp.dma_start(skr[:, :, :], sub_keys[0].rearrange("h q n d -> n (h q) d")).then_inc(s_sk, 16)
                wq_v = w_query[0].rearrange("(k p) e -> p k e", p=P)
                for i in range(4):
                    sp.dma_start(wq[:, 2 * i:2 * i + 2, :], wq_v[:, 2 * i:2 * i + 2, :]).then_inc(s_wq, 16)

            @block.gpsimd
            def _(pool):
                nc.gpsimd.memset(zpad[:, :], 0.0).then_inc(s_pad, 1)
                nc.gpsimd.memset(nhalf[:, :], -0.5).then_inc(s_pool, 1)
                pool.wait_ge(s_pool, 1)
                pool.sem_inc(s_pool, -1)
                with pool.Fori(0, T // XB) as j:
                    for u in range(XB):
                        pool.wait_ge(s_root_in, 1)
                        pool.sem_inc(s_root_in, -1)
                        nc.gpsimd.tensor_tensor(st[:, u, 14:15], st[:, u, 14:15], nhalf[:, 0:1], ALU.pow).then_inc(s_root, 1)

            @block.vector
            def _(dve):
                dve.wait_ge(s_small, 16 * 7)

                def tile_statistics(u):
                    dve.wait_ge(s_x[u], 16)
                    dve.sem_inc(s_x[u], -16)
                    for half in range(2):
                        nc.vector.bn_stats(st[:, u, 6 * half:6 * half + 6],
                                           xin[:, u, 512 * half:512 * half + 512]).then_inc(s_dve, 1)
                    dve.wait_ge(s_dve, 2)
                    dve.sem_inc(s_dve, -2)
                    nc.vector.bn_aggr(st[:, u, 12:14], st[:, u, 0:12]).then_inc(s_dve, 1)
                    dve.wait_ge(s_dve, 1)
                    dve.sem_inc(s_dve, -1)
                    nc.vector.tensor_scalar(st[:, u, 14:15], st[:, u, 13:14], LN_EPS, None, ALU.add).then_inc(s_root_in, 1)

                def tile_factor(u):
                    dve.wait_ge(s_root, 1)
                    dve.sem_inc(s_root, -1)
                    nc.vector.tensor_scalar(st[:, u, 15:16], st[:, u, 12:13], st[:, u, 14:15], -1.0,
                                            ALU.mult, ALU.mult).then_inc(s_stats[u], 1)

                def tile_affine(u):
                    dve.wait_ge(s_norm[u], 1)
                    dve.sem_inc(s_norm[u], -1)
                    nc.vector.tensor_tensor(xin[:, u, :], xin[:, u, :], bc[:, 0:D], ALU.mult).then_inc(s_dve, 1)
                    dve.wait_ge(s_dve, 1)
                    dve.sem_inc(s_dve, -1)
                    nc.vector.tensor_tensor(xin[:, u, :], xin[:, u, :], bc[:, D:2 * D], ALU.add).then_inc(s_dve, 1)
                    dve.wait_ge(s_dve, 1)
                    dve.sem_inc(s_dve, -1)
                    dve.sem_inc(s_h_pe[u], 1)

                tile_statistics(0)
                tile_factor(0)
                with dve.Fori(0, T // XB - 1) as j:
                    for u in range(XB):
                        tile_statistics((u + 1) % XB)
                        tile_affine(u)
                        tile_factor((u + 1) % XB)
                for u in range(XB):
                    if u < XB - 1:
                        tile_statistics(u + 1)
                    tile_affine(u)
                    if u < XB - 1:
                        tile_factor(u + 1)
                dve.wait_ge(s_ab_tok, 1)
                dve.sem_inc(s_ab_tok, -1)
                tok = banks[3][:, 0:8 * T].rearrange("p (t g h) -> p t g h", g=2, h=BH)
                g4 = lambda i: gt[:, i, :].rearrange("p (t h) -> p t h", h=BH)
                nc.vector.tensor_tensor(g4(0), tok[:, :, 0, :], hb[:, 0, :].unsqueeze(1).to_broadcast([P, T, BH]),
                                        ALU.add).then_inc(s_dve, 1)
                dve.wait_ge(s_dve, 1)
                dve.sem_inc(s_dve, -1)
                nc.vector.scalar_tensor_tensor(gt[:, 1, :], gt[:, 0, :], -1.0, gt[:, 0, :], ALU.mult, ALU.min).then_inc(s_dve, 1)
                nc.vector.tensor_copy(g4(2), tok[:, :, 1, :]).then_inc(s_dve, 1)
                dve.wait_ge(s_dve, 2)
                dve.sem_inc(s_dve, -2)
                dve.sem_inc(s_soft, 1)
                dve.wait_ge(s_soft2, 1)
                dve.sem_inc(s_soft2, -1)
                nc.vector.tensor_scalar(gt[:, 4, :], gt[:, 3, :], 1.0, None, ALU.subtract).then_inc(s_dve, 1)
                dve.wait_ge(s_dve, 1)
                dve.sem_inc(s_dve, -1)
                nc.vector.tensor_scalar(gt[:, 5, :], gt[:, 4, :], 0.0, None, ALU.is_equal).then_inc(s_dve, 1)
                dve.wait_ge(s_dve, 1)
                dve.sem_inc(s_dve, -1)
                nc.vector.tensor_tensor(gt[:, 4, :], gt[:, 4, :], gt[:, 5, :], ALU.add).then_inc(s_dve, 1)
                dve.wait_ge(s_dve, 1)
                dve.sem_inc(s_dve, -1)
                nc.vector.reciprocal(gt[:, 4, :], gt[:, 4, :]).then_inc(s_dve, 1)
                dve.wait_ge(s_dve, 1)
                dve.sem_inc(s_dve, -1)
                nl = ybuf[:, 0, 0:T * BH]
                nc.vector.tensor_tensor(nl, nl, gt[:, 5, :], ALU.add).then_inc(s_dve, 1)
                dve.wait_ge(s_dve, 1)
                dve.sem_inc(s_dve, -1)
                nc.vector.tensor_tensor(nl, nl, gt[:, 4, :], ALU.mult).then_inc(s_dve, 1)
                dve.wait_ge(s_dve, 1)
                dve.sem_inc(s_dve, -1)
                nc.vector.tensor_tensor(nl, nl, gt[:, 1, :], ALU.mult).then_inc(s_dve, 1)
                dve.wait_ge(s_dve, 1)
                dve.sem_inc(s_dve, -1)
                nc.vector.scalar_tensor_tensor(gt[:, 0, :], gt[:, 0, :], 0.0, nl, ALU.max, ALU.add).then_inc(s_dve, 1)
                dve.wait_ge(s_dve, 1)
                dve.sem_inc(s_dve, -1)
                nc.vector.tensor_scalar(hb[:, 1, :], hb[:, 1, :], -1.0, None, ALU.mult).then_inc(s_dve, 1)
                dve.wait_ge(s_dve, 1)
                dve.sem_inc(s_dve, -1)
                nc.vector.tensor_tensor(gates[:, 0, :, :], g4(0), hb[:, 1, :].unsqueeze(1).to_broadcast([P, T, BH]),
                                        ALU.mult).then_inc(s_dve, 1)
                dve.wait_ge(s_dve, 1)
                dve.sem_inc(s_dve, -1)
                nc.vector.tensor_scalar(gt[:, 2, :], gt[:, 2, :], 1.0, None, ALU.add).then_inc(s_dve, 1)
                dve.wait_ge(s_dve, 1)
                dve.sem_inc(s_dve, -1)
                nc.vector.reciprocal(gates[:, 1, :, :].rearrange("p t h -> p (t h)"), gt[:, 2, :]).then_inc(s_dve, 1)
                dve.wait_ge(s_dve, 1)
                dve.sem_inc(s_dve, -1)
                dve.sem_inc(s_y_free[0], 1)
                dve.wait_ge(s_cw, 1)
                dve.sem_inc(s_cw, -1)
                with dve.Fori(0, NCONV // 2) as j:
                    for u in range(2):
                        ps = banks[u]
                        dve.wait_ge(s_tap0[u], 1)
                        dve.sem_inc(s_tap0[u], -1)
                        for back in range(1, TAPS):
                            nc.vector.scalar_tensor_tensor(
                       ybuf[:, u, back:S], ps[:, 0:S - back],
                       cw[:, bass.ds(2 * j + u + (TAPS - 1 - back) * NCONV, 1)],
                       ybuf[:, u, back:S], ALU.mult, ALU.add).then_inc(s_dve, 1)
                            dve.wait_ge(s_dve, 1)
                            dve.sem_inc(s_dve, -1)
                        dve.sem_inc(s_conv[u], 1)
                        dve.sem_inc(s_proj_free[u], 1)

            @block.tensor
            def _(pe):
                pe.wait_ge(s_const, 16)
                pe.sem_inc(s_const, -16)
                pe.wait_ge(s_small, 16 * 7)
                nc.tensor.transpose(banks[3][:, 512:512 + NTAP + 1], cwr[:, :], ident[0:NTAP + 1, 0:NTAP + 1]).then_inc(s_cw_ps, 1)
                with pe.Fori(0, T // XB) as j:
                    for u in range(XB):
                        pe.wait_ge(s_h_pe[u], 1)
                        pe.sem_inc(s_h_pe[u], -1)
                        pe.wait_ge(s_tr_free[u % 2], 1)
                        pe.sem_inc(s_tr_free[u % 2], -1)
                        for k in range(KD):
                            last = nc.tensor.transpose(banks[u % 2][:, k * P:(k + 1) * P], xin[:, u, k * P:(k + 1) * P], ident)
                        last.then_inc(s_hT_ps[u % 2], 1)
                pe.wait_ge(s_hT, T)
                pe.sem_inc(s_hT, -T)
                for half in range(2):
                    for k in range(KD):
                        last = nc.tensor.matmul(banks[2][0:8, 512 * half:512 * half + 512], wab[:, k, :],
                                                hT[:, k, 512 * half:512 * half + 512], start=k == 0, stop=k == KD - 1)
                last.then_inc(s_ab_ps, 1)
                pe.wait_ge(s_abT, 1)
                pe.sem_inc(s_abT, -1)
                pe.wait_ge(s_tr_free[0], 1)
                pe.sem_inc(s_tr_free[0], -1)
                for t in range(T):
                    last = nc.tensor.transpose(banks[3][:, 8 * t:8 * t + 8], abT[:, t * P:(t + 1) * P], ident[0:8, 0:8])
                last.then_inc(s_ab_tok, 1)

                def project(u, parts):
                    pe.wait_ge(s_w[u], 16 * parts)
                    pe.sem_inc(s_w[u], -(16 * parts))
                    pe.wait_ge(s_proj_free[u], 1)
                    pe.sem_inc(s_proj_free[u], -1)
                    for half in range(2):
                        for k in range(KD):
                            last = nc.tensor.matmul(banks[u][:, 512 * half:512 * half + 512], wbuf[:, u, k, :],
                                                    hT[:, k, 512 * half:512 * half + 512], start=k == 0, stop=k == KD - 1)
                    last.then_inc(s_proj[u], 1)

                with pe.Fori(0, NCQ // 2) as j:
                    for u in range(2):
                        project(u, 2)
                with pe.Fori(0, (2 + NCONV + NZ) // 2) as j:
                    for u in range(2):
                        project(u, 1)

                pe.wait_ge(s_sk, 16)
                pe.sem_inc(s_sk, -16)
                for half in range(2):
                    for i in range(8):
                        last = nc.tensor.transpose(banks[2 + half][:, i * P:(i + 1) * P], skr[:, 8 * half + i, :], ident)
                last.then_inc(s_sk_ps, 1)

            @block.scalar
            def _(act):
                for u in range(XB):
                    act.sem_inc(s_x_free[u], 1)
                    act.sem_inc(s_h_out[u], 16)
                act.sem_inc(s_tr_free[0], 1)
                act.sem_inc(s_tr_free[1], 1)
                act.sem_inc(s_w_free[0], 1)
                act.sem_inc(s_w_free[1], 1)
                act.wait_ge(s_cw_ps, 1)
                act.sem_inc(s_cw_ps, -1)
                nc.scalar.copy(cw[:, :], banks[3][:, 512:512 + NTAP + 1]).then_inc(s_cw, 1)

                def normalize(u):
                    act.wait_ge(s_stats[u], 1)
                    act.sem_inc(s_stats[u], -1)
                    nc.scalar.activation(xin[:, u, :], xin[:, u, :], ACT.Identity, bias=st[:, u, 15:16],
                                         scale=st[:, u, 14:15]).then_inc(s_norm[u], 1)

                def keep(j, u):
                    act.wait_ge(s_hT_ps[u % 2], 1)
                    act.sem_inc(s_hT_ps[u % 2], -1)
                    act.dma_start(h_dram[XB * j + u], xin[:, u, :]).then_inc(s_h_out[u], 16)
                    nc.scalar.copy(hT[:, :, bass.ts(XB * j + u, P)],
                                   banks[u % 2][:, :].rearrange("p (k n) -> p k n", n=P)).then_inc(s_act, 1)
                    act.wait_ge(s_act, 1)
                    act.sem_inc(s_act, -1)
                    act.sem_inc(s_tr_free[u % 2], 1)
                    act.sem_inc(s_x_free[u], 1)
                    act.sem_inc(s_hT, 1)

                normalize(0)
                with act.Fori(0, T // XB - 1) as j:
                    for u in range(XB):
                        normalize((u + 1) % XB)
                        keep(j, u)
                for u in range(XB):
                    if u < XB - 1:
                        normalize(u + 1)
                    keep(T // XB - 1, u)
                act.wait_ge(s_ab_ps, 1)
                act.sem_inc(s_ab_ps, -1)
                nc.scalar.copy(abT[:, :], banks[2][0:8, :]).then_inc(s_abT, 1)
                act.sem_inc(s_proj_free[0], 1)
                act.sem_inc(s_proj_free[1], 1)
                act.wait_ge(s_soft, 1)
                act.sem_inc(s_soft, -1)
                nl = ybuf[:, 0, 0:T * BH]
                nc.scalar.activation(gt[:, 1, :], gt[:, 1, :], ACT.Exp).then_inc(s_act, 1)
                nc.scalar.activation(gt[:, 2, :], gt[:, 2, :], ACT.Exp, scale=-1.0).then_inc(s_act, 1)
                nc.scalar.activation(hb[:, 1, :], hb[:, 1, :], ACT.Exp).then_inc(s_act, 1)
                act.wait_ge(s_act, 3)
                act.sem_inc(s_act, -3)
                nc.scalar.activation(gt[:, 3, :], gt[:, 1, :], ACT.Copy, bias=1.0).then_inc(s_act, 1)
                act.wait_ge(s_act, 1)
                act.sem_inc(s_act, -1)
                nc.scalar.activation(nl, gt[:, 3, :], ACT.Ln).then_inc(s_act, 1)
                act.wait_ge(s_act, 1)
                act.sem_inc(s_act, -1)
                act.sem_inc(s_soft2, 1)
                act.wait_ge(s_pad, 1)
                act.sem_inc(s_pad, -1)
                act.dma_start(ak_dram[:, 0:CHUNK], zpad[:, :]).then_inc(s_pad_out, 16)
                for u in range(2):
                    act.sem_inc(s_stored[u], 16)

                def store(u, dst):
                    act.wait_ge(s_act, 1)
                    act.sem_inc(s_act, -1)
                    act.dma_start(dst, obuf[:, u, :]).then_inc(s_stored[u], 16)

                def plain(u, dst):
                    act.wait_ge(s_proj[u], 1)
                    act.sem_inc(s_proj[u], -1)
                    act.wait_ge(s_stored[u], 16)
                    act.sem_inc(s_stored[u], -16)
                    nc.scalar.copy(obuf[:, u, :], banks[u][:, :]).then_inc(s_act, 1)
                    store(u, dst)
                    act.sem_inc(s_w_free[u], 1)
                    act.sem_inc(s_proj_free[u], 1)

                with act.Fori(0, NCQ // 2) as j:
                    for u in range(2):
                        plain(u, proj_dram[:, 2 * j + u, :])
                plain(0, ak_dram[:, CHUNK:CHUNK + S])
                plain(1, proj_dram[:, AV, :])
                act.wait_ge(s_y_free[0], 1)
                act.sem_inc(s_y_free[0], -1)
                with act.Fori(0, NCONV // 2) as j:
                    for u in range(2):
                        act.wait_ge(s_proj[u], 1)
                        act.sem_inc(s_proj[u], -1)
                        act.sem_inc(s_w_free[u], 1)
                        nc.scalar.activation(ybuf[:, u, :], banks[u][:, :], ACT.Copy,
                                             scale=cw[:, bass.ds(2 * j + u + (TAPS - 1) * NCONV, 1)]).then_inc(s_tap0[u], 1)
                        act.wait_ge(s_conv[u], 1)
                        act.sem_inc(s_conv[u], -1)
                        act.wait_ge(s_stored[u], 16)
                        act.sem_inc(s_stored[u], -16)
                        nc.scalar.activation(obuf[:, u, :], ybuf[:, u, :], ACT.Silu).then_inc(s_act, 1)
                        store(u, proj_dram[:, 2 * j + (CONV0 + u), :])
                with act.Fori(0, NZ // 2) as j:
                    for u in range(2):
                        act.wait_ge(s_proj[u], 1)
                        act.sem_inc(s_proj[u], -1)
                        act.sem_inc(s_w_free[u], 1)
                        nc.scalar.activation(ybuf[:, u, :], banks[u][:, :], ACT.Silu).then_inc(s_act, 1)
                        act.wait_ge(s_act, 1)
                        act.sem_inc(s_act, -1)
                        act.sem_inc(s_proj_free[u], 1)
                        act.wait_ge(s_stored[u], 16)
                        act.sem_inc(s_stored[u], -16)
                        nc.scalar.activation(obuf[:, u, :], ybuf[:, u, :], ACT.Copy,
                                             scale=cw[:, NTAP:NTAP + 1]).then_inc(s_act, 1)
                        store(u, proj_dram[:, 2 * j + (Z0 + u), :])
                act.wait_ge(s_sk_ps, 1)
                act.sem_inc(s_sk_ps, -1)
                for half in range(2):
                    nc.scalar.copy(skT[:, 8 * half:8 * half + 8, :].rearrange("p a n -> p (a n)"), banks[2 + half][:, :]).then_inc(s_act, 1)
                    act.wait_ge(s_act, 1)
                    act.sem_inc(s_act, -1)
                for u in range(2):
                    act.wait_ge(s_stored[u], 16)
                    act.sem_inc(s_stored[u], -16)
                act.wait_ge(s_pad_out, 16)
                act.sem_inc(s_pad_out, -16)
        a.close()
        b = ExitStack()
        scope[0] = b
        arena = sb("arena", [P, ARENA], c=b)

        def view(at, *dims, dt=fp32):
            n = int(np.prod(dims))
            a = arena[:, at:at + n]
            if dt != fp32:
                a = a.bitcast(dt)
            names = " ".join("abc"[:len(dims)])
            return a.rearrange(f"p ({names}) -> p {names}", **dict(zip("abc", dims))) if len(dims) > 1 else a

        qk_tok = view(0, 12, P)
        ML = view(0, 2, BH, P)
        vnew = view(1024, BH, P)
        qk_ch = view(1536, 12, P)
        kdec, kbe, vb = view(3072, BH, P), view(3584, BH, P), view(4096, BH, P)
        sq = view(4608, 8, P)
        wk = view(4608, 2 * BH, P)
        gU, bI = view(5632, BH, P), view(6144, BH, P)
        yT = view(5632, KD, P)
        DT = view(6656, BH, P)
        on = view(6656, BH, P)
        MT, intraT = view(7168, BH, P), view(7680, BH, P)
        prT = view(8192, 2 * BH, P)
        h1T = view(0, KD, P)
        qT = view(1024, 2 * PH, P)
        rest = view(3072, 2 * PH, NK)
        top, itop = view(5120, 2 * PH, TOPK), view(5376, 2 * PH, TOPK, dt=u32)
        ftop = view(5632, PH, 2, TOPK)
        cand, cid, crest = view(5888, PH, NCAND), view(6288, PH, NCAND), view(6688, PH, NCAND)
        best, ibest, fbest = view(7088, PH, TOPK), view(7216, PH, TOPK, dt=u32), view(7344, PH, TOPK)
        fex = view(7472, PH, TOPK)
        den = view(7600, 2, PH)
        eq = view(7616, TOPK, NCAND)

        raw = sb("raw", [P, NPROJ, P], c=b)
        X, XT, Pm = (raw[:, CONV0 + 4 * i:CONV0 + 4 * i + 4, :] for i in range(3))
        zt = raw[:, Z0:Z0 + NZ, :]
        akt = sb("akt", [P, CHUNK + P], c=b)
        vtok = sb("vtok", [P, 2, P], c=b)
        sml = sb("sml", [P, 64], c=b)
        att = sb("att", [P, 32], c=b)
        St = sb("St", [P, BH, P], c=b)
        sc = sb("sc", [P, BH, 192], c=b)
        pr = sb("pr", [P, BH, 256], c=b)
        ytok = sb("ytok", [P, AH * AD], c=b)
        pre = sb("pre", [P, D], c=b)
        h1n = sb("h1n", [P, D], c=b)
        sink = sb("sink", [P, 2, AH], c=b)
        lnr = sb("lnr", [4, D], c=b)
        wo = sb("wo", [P, 2, D], c=b)
        stb = sb("stb", [P, 18], c=b)
        eidx_n = sb("eidx_n", [P, SLOTS], u32, c=b)
        egate_n = sb("egate_n", [P, SLOTS], c=b)
        U = sb("U", [P, GS, D], c=b)
        V = sb("V", [P, GS, D], c=b)
        eidx = sb("eidx", [P, SLOTS], u32, c=b)
        egate = sb("egate", [P, SLOTS], c=b)
        ixu = sb("ixu", [P, 2, GS], u32, c=b)
        ixv = sb("ixv", [P, 2, GS], u32, c=b)
        dots = sb("dots", [P, 2, GS], c=b)
        gl = sb("gl", [P, 2, GS], c=b)
        dg = sb("dg", [P, 2, GS, P], c=b)
        acc = sb("acc", [P, D], c=b)
        h1c = sb("h1c", [P, D], c=b)
        st2 = sb("st2", [P, 18], c=b)

        b0 = banks[0]
        g = [banks[1][:, 0:512], banks[1][:, 512:1024], banks[2][:, 0:512], banks[2][:, 512:1024]]
        acc_ps = banks[3]
        heads = lambda a: a.rearrange("p (h n) -> p h n", h=BH)
        flat = lambda a: a.rearrange("p a n -> p (a n)")
        SS, RS, EG = sml[:, 0:8], sml[:, 8:16], sml[:, 16:32]
        CO = sml[:, 32:52].rearrange("p (c h) -> p c h", h=BH)
        NG4, SO = sml[:, 52:56], sml[:, 56:60]
        e_gc, e_rest, e_last = EG[:, 0:4], EG[:, 4:8], EG[:, 8:16]
        MX, SE, DEN, RD = att[:, 0:8], att[:, 8:16], att[:, 16:24], att[:, 24:32]

        b_raw = sem("b_raw")
        b_raw_free = sem("b_raw_free")
        b_load = sem("b_load")
        b_h1n_free = sem("b_h1n_free")
        b_wo_last = sem("b_wo_last")
        b_wo0 = sem("b_wo0")
        b_wo1 = sem("b_wo1")
        b_wo_free0 = sem("b_wo_free0")
        b_wo_free1 = sem("b_wo_free1")
        b_pre_in = sem("b_pre_in")
        b_pre_free = sem("b_pre_free")
        b_tok_raw = sem("b_tok_raw")
        b_squared = sem("b_squared")
        b_root_in = sem("b_root_in")
        b_root = sem("b_root")
        b_oroot_in = sem("b_oroot_in")
        b_oroot = sem("b_oroot")
        b_tok_done = sem("b_tok_done")
        b_tokT = sem("b_tokT")
        b_qkch = sem("b_qkch")
        b_gu = sem("b_gu")
        b_gexp = sem("b_gexp")
        b_arg = sem("b_arg")
        b_decayed = sem("b_decayed")
        b_kk = sem("b_kk")
        b_lvM = sem("b_lvM")
        b_lvP0 = sem("b_lvP0")
        b_lvP = sem("b_lvP")
        b_lvPs = sem("b_lvPs")
        b_lvQ = sem("b_lvQ")
        b_lvX = sem("b_lvX")
        b_wk_ps = sem("b_wk_ps")
        b_wk_done = sem("b_wk_done")
        b_vps = sem("b_vps")
        b_vnew = sem("b_vnew")
        b_o_ds = sem("b_o_ds")
        b_o_done = sem("b_o_done")
        b_osq = sem("b_osq")
        b_state = sem("b_state")
        b_on_ready = sem("b_on_ready")
        b_onT_ps = sem("b_onT_ps")
        b_yT_b = sem("b_yT_b")
        b_osq_in = sem("b_osq_in")
        b_sc_ps = sem("b_sc_ps")
        b_sc_s = sem("b_sc_s")
        b_pexp = sem("b_pexp")
        b_exp_s = sem("b_exp_s")
        b_prT_ps = sem("b_prT_ps")
        b_prT_done = sem("b_prT_done")
        b_pv = sem("b_pv")
        b_pv_read = sem("b_pv_read")
        b_ya = sem("b_ya")
        b_yaT_ps = sem("b_yaT_ps")
        b_yT_a = sem("b_yT_a")
        b_mix_ps = sem("b_mix_ps")
        b_rows_ps = sem("b_rows_ps")
        b_lroot_in = sem("b_lroot_in")
        b_lroot = sem("b_lroot")
        b_norm_in = sem("b_norm_in")
        b_normed = sem("b_normed")
        b_h1 = sem("b_h1")
        b_h1T_ps = sem("b_h1T_ps")
        b_h1T = sem("b_h1T")
        b_q_ps = sem("b_q_ps")
        b_qT = sem("b_qT")
        b_qT_a = sem("b_qT_a")
        b_scores_a = sem("b_scores_a")
        b_scores = sem("b_scores")
        b_scores_read = sem("b_scores_read")
        b_soft = sem("b_soft")
        b_exped = sem("b_exped")
        g_u = [sem(f"g_u{k}") for k in range(GS)]
        g_v = [sem(f"g_v{k}") for k in range(GS)]
        g_ufree = [sem(f"g_ufree{k}") for k in range(GS)]
        g_vfree = [sem(f"g_vfree{k}") for k in range(GS)]
        g_dots = sem("g_dots")
        g_gelu = sem("g_gelu")
        g_w = sem("g_w")
        g_diag = sem("g_diag")
        g_dfree = sem("g_dfree")
        g_accps = sem("g_accps")
        g_accfree = sem("g_accfree")
        g_tile = sem("g_tile")
        g_indexfree = sem("g_indexfree")
        s_pe = sem("s_pe")
        t_root_in = sem("t_root_in")
        t_root = sem("t_root")
        t_norm_in = sem("t_norm_in")
        t_normed = sem("t_normed")
        t_ln = sem("t_ln")
        t_lnfree = sem("t_lnfree")
        t_out = sem("t_out")
        t_stored = sem("t_stored")
        t_free = sem("t_free")

        def bc3(a, n=P):
            return a.unsqueeze(2).to_broadcast([a.shape[0], a.shape[1], n])

        def per_head(a):
            return a.unsqueeze(1).to_broadcast([P, BH, P])

        rows = bass.IndirectOffsetOnAxis

        with nc.Block() as block:
            @block.sync
            def _(sp):
                sp.dma_start(lnr[0:1, :], ln1_g).then_inc(b_load, 16)
                sp.dma_start(lnr[1:2, :], ln1_b).then_inc(b_load, 16)
                sp.dma_start(lnr[2:3, :], ln2_g).then_inc(b_load, 16)
                sp.dma_start(lnr[3:4, :], ln2_b).then_inc(b_load, 16)
                sp.dma_start(sink[:, 0, :], a_sinks[0].partition_broadcast(P)).then_inc(b_load, 16)
                wo_v = w_out[0].rearrange("(k p) d -> k p d", p=P)

                def loads(t):
                    sp.wait_ge(b_raw_free, 1)
                    sp.sem_inc(b_raw_free, -1)
                    sp.dma_start(raw[:, :, :], proj_dram[:, :, bass.ts(t, P)]).then_inc(b_raw, 16)
                    sp.dma_start(akt[:, :], ak_dram[:, bass.ds(t * P, CHUNK + P)]).then_inc(b_raw, 16)
                    sp.wait_ge(b_pre_free, 1)
                    sp.sem_inc(b_pre_free, -1)

                def more_loads(t):
                    sp.dma_start(pre[:, :], h_dram[t]).then_inc(b_pre_in, 16)
                    for k in range(KD - 2):
                        sp.wait_ge(b_wo_free1 if k % 2 else b_wo_free0, 1)
                        sp.sem_inc(b_wo_free1 if k % 2 else b_wo_free0, -1)
                        sp.dma_start(wo[:, k % 2, :], wo_v[k]).then_inc((b_wo1 if k % 2 else b_wo0), 16)
                    sp.wait_ge(b_h1n_free, 1)
                    sp.sem_inc(b_h1n_free, -1)
                    sp.dma_start(h1n[:, :], wo_v[KD - 1]).then_inc(b_wo_last, 16)
                    sp.wait_ge(b_wo_free0, 1)
                    sp.sem_inc(b_wo_free0, -1)
                    sp.dma_start(wo[:, 0, :], wo_v[KD - 2]).then_inc(b_wo0, 16)

                def store(t):
                    sp.wait_ge(t_out, 1)
                    sp.sem_inc(t_out, -1)
                    sp.dma_start(out[0, bass.ts(t, P), :], pre[:, :]).then_inc(t_stored, 16)
                    sp.wait_ge(t_stored, 16)
                    sp.sem_inc(t_stored, -16)

                for t in range(2):
                    loads(t)
                    more_loads(t)
                with sp.Fori(0, T - 2) as t:
                    loads(t + 2)
                    store(t)
                    more_loads(t + 2)
                store(T - 2)
                sp.sem_inc(t_free, 1)
                store(T - 1)

            @block.gpsimd
            def _(pool):
                def fetch(par, u, v):
                    for k in range(GS):
                        if u:
                            pool.wait_ge(g_ufree[k], 1)
                            pool.sem_inc(g_ufree[k], -1)
                            pool.indirect_dma_start(U[:, k, :], None, expert_u[0],
                                                    rows(ap=ixu[:, par, k:k + 1], axis=0)).then_inc(g_u[k], 16)
                        if v:
                            pool.wait_ge(g_vfree[k], 1)
                            pool.sem_inc(g_vfree[k], -1)
                            pool.indirect_dma_start(V[:, k, :], None, expert_v[0],
                                                    rows(ap=ixv[:, 1 - par, k:k + 1], axis=0)).then_inc(g_v[k], 16)

                def step(s, par):
                    nc.gpsimd.tensor_copy(ixu[:, par, :], eidx[:, bass.ds(s * GS, GS)]).then_inc(s_pool, 1)
                    pool.wait_ge(s_pool, 1)
                    pool.sem_inc(s_pool, -1)
                    nc.gpsimd.tensor_copy(ixv[:, 1 - par, :], eidx[:, bass.ds(s * GS - GS, GS)]).then_inc(s_pool, 1)
                    pool.wait_ge(s_pool, 1)
                    pool.sem_inc(s_pool, -1)
                    fetch(par, True, True)

                def steps():
                    with pool.Fori(0, NGROUP // 2 - 1) as j:
                        step(2 * j + 1, 1)
                        step(2 * j + 2, 0)
                    step(NGROUP - 1, 1)

                def next_tile():
                    pool.wait_ge(g_tile, 1)
                    pool.sem_inc(g_tile, -1)
                    nc.gpsimd.tensor_copy(eidx[:, :], eidx_n[:, :]).then_inc(s_pool, 1)
                    pool.wait_ge(s_pool, 1)
                    pool.sem_inc(s_pool, -1)
                    pool.sem_inc(g_indexfree, 1)
                    nc.gpsimd.tensor_copy(ixu[:, 0, :], eidx[:, 0:GS]).then_inc(s_pool, 1)
                    pool.wait_ge(s_pool, 1)
                    pool.sem_inc(s_pool, -1)

                next_tile()
                fetch(0, True, False)
                with pool.Fori(0, T - 1) as t:
                    steps()
                    nc.gpsimd.tensor_copy(ixv[:, 1, :], eidx[:, SLOTS - GS:SLOTS]).then_inc(s_pool, 1)
                    pool.wait_ge(s_pool, 1)
                    pool.sem_inc(s_pool, -1)
                    next_tile()
                    fetch(0, True, True)
                steps()
                nc.gpsimd.tensor_copy(ixv[:, 1, :], eidx[:, SLOTS - GS:SLOTS]).then_inc(s_pool, 1)
                pool.wait_ge(s_pool, 1)
                pool.sem_inc(s_pool, -1)
                fetch(0, False, True)

            @block.tensor
            def _(pe):
                def level(l):
                    if l:
                        pe.wait_ge(b_lvX, 1)
                        pe.sem_inc(b_lvX, -1)
                    pe.wait_ge(b_lvM, 1)
                    pe.sem_inc(b_lvM, -1)
                    for h in range(BH):
                        last = nc.tensor.matmul(g[0][:, h * P:(h + 1) * P], ML[:, l % 2, h, :], ident if l == 0 else X[:, h, :],
                                                start=True, stop=True)
                    if l == 0:
                        last.then_inc(b_lvP0, 1)
                        return
                    last.then_inc(b_lvP, 1)
                    pe.wait_ge(b_lvPs, 1)
                    pe.sem_inc(b_lvPs, -1)
                    for h in range(BH):
                        if l < 5:
                            nc.tensor.matmul(g[1][:, h * P:(h + 1) * P], XT[:, h, :], Pm[:, h, :], start=True, stop=True)
                        last = nc.tensor.matmul(g[2][:, h * P:(h + 1) * P], Pm[:, h, :], XT[:, h, :], start=True, stop=True)
                    last.then_inc(b_lvQ, 1)

                def scores(hh):
                    lo = 64 * hh
                    for i in range(4):
                        last = nc.tensor.matmul(b0[:, 256 * i:256 * i + 192], raw[lo:lo + 64, i, :], akt[lo:lo + 64, :],
                                                start=True, stop=True)
                    last.then_inc(b_sc_ps, 1)

                def turn_probs():
                    pe.wait_ge(b_pexp, 1)
                    pe.sem_inc(b_pexp, -1)
                    for i in range(8):
                        last = nc.tensor.transpose(b0[:, i * P:(i + 1) * P], pr[:, i // 2, (i % 2) * P:(i % 2 + 1) * P], ident)
                    last.then_inc(b_prT_ps, 1)

                def values(hh):
                    pe.wait_ge(b_prT_done, 1)
                    pe.sem_inc(b_prT_done, -1)
                    for i in range(4):
                        o = b0[:, 64 * i:64 * i + 64]
                        nc.tensor.matmul(o, prT[64:128, 2 * i, :], vtok[64:128, 1, 64 * hh:64 * hh + 64], start=True, stop=False)
                        last = nc.tensor.matmul(o, prT[:, 2 * i + 1, :], vtok[:, 0, 64 * hh:64 * hh + 64], start=False, stop=True)
                    last.then_inc(b_pv, 1)

                def chunk_values(c):
                    lo = 64 * c
                    for h in range(BH):
                        last = nc.tensor.matmul(g[2][lo:lo + 64, h * P:(h + 1) * P], wk[:, BH + h, lo:lo + 64], St[:, h, :],
                                                start=True, stop=True)
                    last.then_inc(b_vps, 1)

                def chunk_output(c):
                    lo = 64 * c
                    pe.wait_ge(b_vnew, 1)
                    pe.sem_inc(b_vnew, -1)
                    for h in range(BH):
                        o = g[3][lo:lo + 64, h * P:(h + 1) * P]
                        nc.tensor.matmul(o, qk_ch[:, 4 + h, lo:lo + 64], St[:, h, :], start=True, stop=False, skip_group_check=True)
                        nc.tensor.matmul(o, intraT[lo:lo + 64, h, lo:lo + 64], vnew[lo:lo + 64, h, :],
                                         start=False, stop=True, skip_group_check=True)
                    for h in range(BH):
                        last = nc.tensor.matmul(g[0][:, h * P:(h + 1) * P], kdec[lo:lo + 64, h, :], vnew[lo:lo + 64, h, :],
                                                start=True, stop=True)
                    last.then_inc(b_o_ds, 1)

                def out_slice(k, n):
                    w = h1n if k == KD - 1 else wo[:, k % 2, :]
                    return nc.tensor.matmul(b0[:, 512 * n:512 * n + 512], yT[:, k, :], w[:, 512 * n:512 * n + 512],
                                            start=k == 0, stop=k == KD - 2)

                def project_out(ks):
                    for k in ks:
                        pe.wait_ge(b_wo1 if k % 2 else b_wo0, 16)
                        pe.sem_inc(b_wo1 if k % 2 else b_wo0, -16)
                        for n in range(2):
                            last = out_slice(k, n)
                        last.then_inc((b_wo_free1 if k % 2 else b_wo_free0), 1)

                def norm_rows(r, s_ready):
                    for i in range(2):
                        for n in range(2):
                            last = nc.tensor.matmul(banks[1 + i][:, 512 * n:512 * n + 512],
                                                    ident[0:4, r + i:r + i + 1].to_broadcast([4, P]),
                                                    lnr[:, 512 * n:512 * n + 512], start=True, stop=True)
                    last.then_inc(s_ready, 1)

                def queries(q):
                    for i in range(2 * q, 2 * q + 2):
                        o = banks[1 + i // 8][:, (i % 8) * P:(i % 8 + 1) * P]
                        for k in range(KD):
                            last = nc.tensor.matmul(o, wq[:, k, i * P:(i + 1) * P], h1T[:, k, :], start=k == 0, stop=k == KD - 1)
                    if q % 4 == 3:
                        last.then_inc(b_q_ps, 1)

                def sub_scores(half, s_ready):
                    for hp in range(8 * half, 8 * half + 8):
                        last = nc.tensor.matmul(banks[half][:, (hp % 8) * P:(hp % 8 + 1) * P], qT[:, hp, :], skT[:, hp, :],
                                                start=True, stop=True)
                    last.then_inc(s_ready, 1)

                def piece(n, t):
                    if n == 0:
                        pe.wait_ge(b_raw, 32)
                        pe.sem_inc(b_raw, -32)
                        for i in range(8):
                            nc.tensor.transpose(banks[1][:, i * P:(i + 1) * P], raw[:, CONV0 + i, :], ident)
                        for i in range(4):
                            last = nc.tensor.transpose(g[2][:, i * P:(i + 1) * P], raw[:, CONV0 + 8 + i, :], ident)
                        gate = gates[:, 0, t, :]
                        nc.tensor.matmul(g[3][:, 0:4], const("upto"), gate, start=True, stop=True)
                        nc.tensor.matmul(g[3][:, 4:8], const("after"), gate, start=True, stop=True)
                        for c in range(2):
                            nc.tensor.matmul(g[3][:, 8 + 4 * c:12 + 4 * c], const("chunk_of")[:, c * P:(c + 1) * P], gate,
                                             start=True, stop=True)
                        nc.tensor.transpose(g[3][:, 128:256], raw[:, AV, :], ident).then_inc(b_tok_raw, 1)
                        scores(0)
                    elif n == 2:
                        pe.wait_ge(b_tok_done, 1)
                        pe.sem_inc(b_tok_done, -1)
                        for i in range(8):
                            nc.tensor.transpose(banks[1][:, i * P:(i + 1) * P], qk_tok[:, i, :], ident)
                        for i in range(4):
                            last = nc.tensor.transpose(g[2][:, i * P:(i + 1) * P], qk_tok[:, 8 + i, :], ident)
                        last.then_inc(b_tokT, 1)
                        pe.wait_ge(b_gu, 1)
                        pe.sem_inc(b_gu, -1)
                        nc.tensor.matmul(g[3], const("ones"), gU, start=True, stop=False)
                        nc.tensor.matmul(g[3], const("upto"), bc3(NG4), start=False, stop=False)
                        nc.tensor.matmul(g[3], ident, per_head(const("decay_mask")), start=False, stop=True).then_inc(b_arg, 1)
                        turn_probs()
                    elif n == 3:
                        pe.wait_ge(b_qkch, 1)
                        pe.sem_inc(b_qkch, -1)
                        for h in range(BH):
                            nc.tensor.matmul(g[0][:, h * P:(h + 1) * P], qk_ch[:, 8 + h, :], qk_ch[:, 8 + h, :], start=True, stop=True)
                            nc.tensor.matmul(g[1][:, h * P:(h + 1) * P], qk_ch[:, 8 + h, :], qk_ch[:, h, :], start=True, stop=True)
                        nc.tensor.matmul(g[2], const("after"), bI, start=True, stop=True).then_inc(b_kk, 1)
                        values(0)
                    elif n == 4:
                        pe.wait_ge(b_pv_read, 1)
                        pe.sem_inc(b_pv_read, -1)
                        scores(1)
                        level(0)
                    elif n == 5:
                        level(1)
                    elif n == 6:
                        level(2)
                        turn_probs()
                    elif n == 7:
                        level(3)
                        values(1)
                    elif n == 8:
                        level(4)
                    elif n == 9:
                        level(5)
                    elif n == 10:
                        pe.wait_ge(b_lvX, 1)
                        pe.sem_inc(b_lvX, -1)
                        for h in range(BH):
                            nc.tensor.matmul(g[0][:, h * P:(h + 1) * P], XT[:, h, :], vb[:, h, :], start=True, stop=True)
                            last = nc.tensor.matmul(g[1][:, h * P:(h + 1) * P], kbe[:, h, :], XT[:, h, :], start=True, stop=True)
                        last.then_inc(b_wk_ps, 1)
                        pe.wait_ge(b_ya, 1)
                        pe.sem_inc(b_ya, -1)
                        for i in range(4):
                            last = nc.tensor.transpose(b0[:, 512 + i * P:512 + (i + 1) * P], ytok[:, i * P:(i + 1) * P], ident)
                        last.then_inc(b_yaT_ps, 1)
                        pe.wait_ge(b_wk_done, 1)
                        pe.sem_inc(b_wk_done, -1)
                        chunk_values(0)
                    elif n == 11:
                        chunk_output(0)
                        pe.wait_ge(b_yT_a, 1)
                        pe.sem_inc(b_yT_a, -1)
                        project_out((0, 1))
                    elif n == 12:
                        pe.wait_ge(b_state, 1)
                        pe.sem_inc(b_state, -1)
                        chunk_values(1)
                    elif n == 13:
                        chunk_output(1)
                    elif n == 15:
                        project_out((2, 3))
                    elif n == 16:
                        pe.wait_ge(b_on_ready, 1)
                        pe.sem_inc(b_on_ready, -1)
                        for i in range(4):
                            last = nc.tensor.transpose(g[1][:, i * P:(i + 1) * P], on[:, i, :], ident)
                        last.then_inc(b_onT_ps, 1)
                    elif n == 18:
                        pe.wait_ge(b_yT_b, 1)
                        pe.sem_inc(b_yT_b, -1)
                        project_out((4, 5))
                        pe.wait_ge(b_wo_last, 16)
                        pe.sem_inc(b_wo_last, -16)
                        for n in range(2):
                            out_slice(KD - 1, n)
                    elif n == 19:
                        pe.wait_ge(b_wo0, 16)
                        pe.sem_inc(b_wo0, -16)
                        for n in range(2):
                            last = out_slice(KD - 2, n)
                        last.then_inc(s_pe, 1)
                        pe.wait_ge(s_pe, 1)
                        pe.sem_inc(s_pe, -1)
                        pe.sem_inc(b_wo_free0, 1)
                        pe.sem_inc(b_mix_ps, 1)
                    elif n == 20:
                        pe.wait_ge(b_o_done, 1)
                        pe.sem_inc(b_o_done, -1)
                        norm_rows(0, b_rows_ps)
                    elif n == 22:
                        pe.wait_ge(b_h1, 1)
                        pe.sem_inc(b_h1, -1)
                        for k in range(KD):
                            last = nc.tensor.transpose(b0[:, k * P:(k + 1) * P], h1n[:, k * P:(k + 1) * P], ident)
                        last.then_inc(b_h1T_ps, 1)
                    elif 23 <= n <= 30:
                        if n == 23:
                            pe.wait_ge(b_h1T, 1)
                            pe.sem_inc(b_h1T, -1)
                        queries(n - 23)
                        if n == 28:
                            pe.wait_ge(b_qT_a, 1)
                            pe.sem_inc(b_qT_a, -1)
                            sub_scores(0, b_scores_a)
                    elif n == 31:
                        pe.wait_ge(b_qT, 1)
                        pe.sem_inc(b_qT, -1)
                        sub_scores(1, b_scores)
                    elif n == 35:
                        pe.wait_ge(b_scores_read, 1)
                        pe.sem_inc(b_scores_read, -1)

                def gather(t, s, par, nv=2, first=False, last_group=False):
                    if nv == GS:
                        return
                    pe.wait_ge(g_diag, GS - nv)
                    pe.sem_inc(g_diag, -(GS - nv))
                    if first:
                        pe.wait_ge(g_accfree, 1)
                        pe.sem_inc(g_accfree, -1)
                    for k in range(GS - nv):
                        pe.wait_ge(g_v[k], (t * NGROUP + s) * 16)
                        for n in range(2):
                            ins = nc.tensor.matmul(acc_ps[:, 512 * n:512 * n + 512], dg[:, 1 - par, k, :],
                                                   V[:, k, 512 * n:512 * n + 512], start=first and k == 0,
                                                   stop=last_group and k == GS - nv - 1)
                            if k == 0 and n == 0:
                                ins.then_inc(g_dfree, 1)
                        if k < GS - nv - 1 or not last_group:
                            ins.then_inc(g_vfree[k], 1)
                        else:
                            ins.then_inc(s_pe, 1)
                            pe.wait_ge(s_pe, 1)
                            pe.sem_inc(s_pe, -1)
                            pe.sem_inc(g_vfree[k], 1)
                            pe.sem_inc(g_accps, 1)

                def plain_steps(t, after_tile):
                    for s in range(1, PLAIN + 1):
                        gather(t, s, s % 2, ON_VECTOR[s], s == 1)
                        if after_tile and s == 1:
                            norm_rows(2, t_ln)
                    if after_tile:
                        pe.wait_ge(t_lnfree, 1)
                        pe.sem_inc(t_lnfree, -1)

                pe.wait_ge(b_load, 80)
                for n in range(NPIECE):
                    if n == 23:
                        pe.wait_ge(s_wq, 64)
                        pe.sem_inc(s_wq, -64)
                    piece(n, 0)
                plain_steps(0, False)
                with pe.Fori(0, T - 1) as t:
                    for s in range(PLAIN + 1, NGROUP + 1):
                        gather(t, s, s % 2, ON_VECTOR[s], False, s == NGROUP)
                        for n in pieces(TENSOR_AT, 2 * s) + pieces(TENSOR_AT, 2 * s + 1):
                            piece(n, t + 1)
                    plain_steps(t + 1, True)
                with pe.Fori(0, (NGROUP - PLAIN) // 2 - 1) as j:
                    gather(T - 1, 2 * j + 3, 1)
                    gather(T - 1, 2 * j + 4, 0)
                gather(T - 1, NGROUP - 1, 1)
                gather(T - 1, NGROUP, 0, 2, False, True)
                norm_rows(2, t_ln)
                pe.wait_ge(t_lnfree, 1)
                pe.sem_inc(t_lnfree, -1)

            @block.scalar
            def _(act):
                def probs(hh):
                    act.wait_ge(b_sc_s, 1)
                    act.sem_inc(b_sc_s, -1)
                    for i in range(4):
                        h = 4 * hh + i
                        nc.scalar.activation(pr[:, i, CHUNK:CHUNK + 192], sc[:, i, :], ACT.Exp, bias=MX[:, h:h + 1],
                                             scale=float(AD) ** -0.5, accum_out=DEN[:, h:h + 1]).then_inc(s_act, 1)
                    act.wait_ge(s_act, 4)
                    act.sem_inc(s_act, -4)
                    act.sem_inc(b_pexp, 1)
                    nc.scalar.activation(SE[:, 4 * hh:4 * hh + 4], SE[:, 4 * hh:4 * hh + 4], ACT.Exp).then_inc(s_act, 1)
                    act.wait_ge(s_act, 1)
                    act.sem_inc(s_act, -1)
                    act.sem_inc(b_exp_s, 1)

                def turned():
                    act.wait_ge(b_prT_ps, 1)
                    act.sem_inc(b_prT_ps, -1)
                    nc.scalar.copy(flat(prT), b0[:, :]).then_inc(b_prT_done, 1)

                def level():
                    act.wait_ge(b_lvP, 1)
                    act.sem_inc(b_lvP, -1)
                    nc.scalar.copy(flat(Pm), g[0]).then_inc(b_lvPs, 1)

                def piece(n, t):
                    if n == 0:
                        act.wait_ge(b_tok_raw, 1)
                        act.sem_inc(b_tok_raw, -1)
                        nc.scalar.activation(flat(sq), banks[1][:, :], ACT.Square).then_inc(b_squared, 1)
                        nc.scalar.activation(EG, g[3][:, 0:16], ACT.Exp).then_inc(s_act, 1)
                        nc.scalar.copy(vtok[:, 0, :], g[3][:, 128:256]).then_inc(s_act, 1)
                        act.wait_ge(s_act, 2)
                        act.sem_inc(s_act, -2)
                        act.sem_inc(b_gexp, 1)
                    elif n == 1:
                        act.wait_ge(b_root_in, 1)
                        act.sem_inc(b_root_in, -1)
                        nc.scalar.activation(RS, SS, ACT.Sqrt).then_inc(b_root, 1)
                        probs(0)
                    elif n == 2:
                        act.wait_ge(b_tokT, 1)
                        act.sem_inc(b_tokT, -1)
                        nc.scalar.copy(flat(qk_ch[:, 0:8, :]), banks[1][:, :]).then_inc(s_act, 1)
                        nc.scalar.copy(flat(qk_ch[:, 8:12, :]), g[2]).then_inc(s_act, 1)
                        act.wait_ge(s_act, 2)
                        act.sem_inc(s_act, -2)
                        act.sem_inc(b_qkch, 1)
                        act.wait_ge(b_arg, 1)
                        act.sem_inc(b_arg, -1)
                        nc.scalar.activation(flat(DT), g[3], ACT.Exp).then_inc(b_decayed, 1)
                        turned()
                    elif n == 5:
                        level()
                        probs(1)
                    elif n == 6:
                        level()
                        turned()
                    elif n in (7, 8, 9):
                        level()
                    elif n == 10:
                        act.wait_ge(b_wk_ps, 1)
                        act.sem_inc(b_wk_ps, -1)
                        nc.scalar.copy(flat(wk), banks[1][:, :]).then_inc(b_wk_done, 1)
                        act.wait_ge(b_yaT_ps, 1)
                        act.sem_inc(b_yaT_ps, -1)
                        nc.scalar.copy(flat(yT[:, 0:4, :]), b0[:, 512:1024]).then_inc(b_yT_a, 1)
                    elif n == 14:
                        act.wait_ge(b_osq_in, 1)
                        act.sem_inc(b_osq_in, -1)
                        nc.scalar.activation(flat(on), g[3], ACT.Square).then_inc(b_osq, 1)
                    elif n == 15:
                        act.wait_ge(b_oroot_in, 1)
                        act.sem_inc(b_oroot_in, -1)
                        nc.scalar.activation(SO, SO, ACT.Sqrt).then_inc(b_oroot, 1)
                    elif n == 20:
                        act.wait_ge(b_lroot_in, 1)
                        act.sem_inc(b_lroot_in, -1)
                        nc.scalar.activation(stb[:, 14:15], stb[:, 14:15], ACT.Sqrt).then_inc(b_lroot, 1)
                    elif n == 21:
                        act.wait_ge(b_norm_in, 1)
                        act.sem_inc(b_norm_in, -1)
                        nc.scalar.activation(pre[:, :], pre[:, :], ACT.Identity, bias=stb[:, 15:16], scale=stb[:, 14:15]).then_inc(b_normed, 1)
                    elif n == 22:
                        act.wait_ge(b_h1T_ps, 1)
                        act.sem_inc(b_h1T_ps, -1)
                        nc.scalar.copy(flat(h1T), b0[:, :]).then_inc(b_h1T, 1)
                    elif n == 26:
                        act.wait_ge(b_q_ps, 1)
                        act.sem_inc(b_q_ps, -1)
                        nc.scalar.copy(flat(qT[:, 0:8, :]), banks[1][:, :]).then_inc(b_qT_a, 1)
                    elif n == 30:
                        act.wait_ge(b_q_ps, 1)
                        act.sem_inc(b_q_ps, -1)
                        nc.scalar.copy(flat(qT[:, 8:16, :]), banks[2][:, :]).then_inc(b_qT, 1)
                    elif n == 39:
                        act.wait_ge(b_soft, 1)
                        act.sem_inc(b_soft, -1)
                        nc.scalar.activation(best, best, ACT.Exp).then_inc(b_exped, 1)

                def diagonals(par, nv=2):
                    act.wait_ge(g_w, 1)
                    act.sem_inc(g_w, -1)
                    if nv < GS:
                        act.wait_ge(g_dfree, 1)
                        act.sem_inc(g_dfree, -1)
                    for k in range(GS - nv):
                        nc.scalar.activation(dg[:, 1 - par, k, :], ident, ACT.Copy, scale=gl[:, 1 - par, k:k + 1]).then_inc(g_diag, 1)

                def gelu(par):
                    act.wait_ge(g_dots, 1)
                    act.sem_inc(g_dots, -1)
                    act.sem_inc(g_ufree[GS - 1], 1)
                    nc.scalar.activation(gl[:, par, :], dots[:, par, :], ACT.Gelu).then_inc(g_gelu, 1)

                def root():
                    act.wait_ge(t_root_in, 1)
                    act.sem_inc(t_root_in, -1)
                    nc.scalar.activation(st2[:, 14:15], st2[:, 14:15], ACT.Sqrt).then_inc(t_root, 1)

                def norm():
                    act.wait_ge(t_norm_in, 1)
                    act.sem_inc(t_norm_in, -1)
                    nc.scalar.activation(pre[:, :], pre[:, :], ACT.Identity, bias=st2[:, 15:16], scale=st2[:, 14:15]).then_inc(t_normed, 1)

                def plain_steps(after_tile):
                    for s in range(1, PLAIN + 1):
                        diagonals(s % 2, ON_VECTOR[s])
                        if after_tile:
                            if s == 1:
                                root()
                            else:
                                norm()
                        gelu(s % 2)

                act.sem_inc(g_dfree, 1)
                for n in range(NPIECE):
                    piece(n, 0)
                gelu(0)
                plain_steps(False)
                with act.Fori(0, T - 1) as t:
                    for s in range(PLAIN + 1, NGROUP + 1):
                        diagonals(s % 2, ON_VECTOR[s])
                        for n in pieces(SCALAR_AT, 2 * s):
                            piece(n, t + 1)
                        gelu(s % 2)
                        for n in pieces(SCALAR_AT, 2 * s + 1):
                            piece(n, t + 1)
                    plain_steps(True)
                with act.Fori(0, (NGROUP - PLAIN) // 2 - 1) as j:
                    for par in (1, 0):
                        diagonals(par)
                        gelu(par)
                diagonals(1)
                gelu(1)
                diagonals(0)
                root()
                norm()

            @block.vector
            def _(dve):
                def soften(hh):
                    dve.wait_ge(b_sc_ps, 1)
                    dve.sem_inc(b_sc_ps, -1)
                    for i in range(4):
                        nc.vector.scalar_tensor_tensor(sc[:, i, :], const("dist"), -float(AD) ** 0.5 * 2.0 ** -(4 * hh + i + 1),
                                                       b0[:, 256 * i:256 * i + 192], ALU.mult, ALU.add).then_inc(s_dve, 1)
                    dve.wait_ge(s_dve, 4)
                    dve.sem_inc(s_dve, -4)
                    mx, se = MX[:, 4 * hh:4 * hh + 4], SE[:, 4 * hh:4 * hh + 4]
                    nc.vector.reduce_max(mx, sc[:, :, :], AX.X).then_inc(s_dve, 1)
                    dve.wait_ge(s_dve, 1)
                    dve.sem_inc(s_dve, -1)
                    nc.vector.tensor_tensor(mx, mx, sink[:, 1, 4 * hh:4 * hh + 4], ALU.max).then_inc(s_dve, 1)
                    dve.wait_ge(s_dve, 1)
                    dve.sem_inc(s_dve, -1)
                    nc.vector.tensor_scalar(mx, mx, -float(AD) ** -0.5, None, ALU.mult).then_inc(s_dve, 1)
                    dve.wait_ge(s_dve, 1)
                    dve.sem_inc(s_dve, -1)
                    nc.vector.tensor_tensor(se, sink[:, 0, 4 * hh:4 * hh + 4], mx, ALU.add).then_inc(s_dve, 1)
                    dve.wait_ge(s_dve, 1)
                    dve.sem_inc(s_dve, -1)
                    dve.sem_inc(b_sc_s, 1)

                def divide(hh):
                    dve.wait_ge(b_exp_s, 1)
                    dve.sem_inc(b_exp_s, -1)
                    d, r = DEN[:, 4 * hh:4 * hh + 4], RD[:, 4 * hh:4 * hh + 4]
                    nc.vector.tensor_tensor(d, d, SE[:, 4 * hh:4 * hh + 4], ALU.add).then_inc(s_dve, 1)
                    dve.wait_ge(s_dve, 1)
                    dve.sem_inc(s_dve, -1)
                    nc.vector.reciprocal(r, d).then_inc(s_dve, 1)
                    dve.wait_ge(s_dve, 1)
                    dve.sem_inc(s_dve, -1)
                    dve.wait_ge(b_pv, 1)
                    dve.sem_inc(b_pv, -1)
                    nc.vector.tensor_tensor(ytok[:, 256 * hh:256 * hh + 256].rearrange("p (h d) -> p h d", d=AD),
                                            b0[:, 0:256].rearrange("p (h d) -> p h d", d=AD), bc3(r, AD), ALU.mult).then_inc(s_dve, 1)
                    dve.wait_ge(s_dve, 1)
                    dve.sem_inc(s_dve, -1)

                def mask(l):
                    nc.vector.tensor_tensor(ML[:, l % 2, :, :], MT, per_head(const("level")[:, l * P:(l + 1) * P]), ALU.mult).then_inc(s_dve, 1)
                    dve.wait_ge(s_dve, 1)
                    dve.sem_inc(s_dve, -1)
                    dve.sem_inc(b_lvM, 1)

                def grow(l):
                    if l == 0:
                        dve.wait_ge(b_lvP0, 1)
                        dve.sem_inc(b_lvP0, -1)
                        nc.vector.tensor_tensor(X, per_head(ident), heads(g[0]), ALU.subtract).then_inc(s_dve, 1)
                        nc.vector.tensor_tensor(XT, per_head(ident), ML[:, 0, :, :], ALU.subtract).then_inc(s_dve, 1)
                        dve.wait_ge(s_dve, 2)
                        dve.sem_inc(s_dve, -2)
                    else:
                        dve.wait_ge(b_lvQ, 1)
                        dve.sem_inc(b_lvQ, -1)
                        nc.vector.tensor_tensor(XT, XT, heads(g[2]), ALU.subtract).then_inc(s_dve, 1)
                        if l < 5:
                            nc.vector.tensor_tensor(X, X, heads(g[1]), ALU.subtract).then_inc(s_dve, 1)
                        dve.wait_ge(s_dve, 2 if l < 5 else 1)
                        dve.sem_inc(s_dve, -(2 if l < 5 else 1))
                    dve.sem_inc(b_lvX, 1)

                def new_values(c):
                    lo = 64 * c
                    dve.wait_ge(b_vps, 1)
                    dve.sem_inc(b_vps, -1)
                    nc.vector.tensor_tensor(vnew[lo:lo + 64, :, :], wk[lo:lo + 64, 0:BH, :], heads(g[2])[lo:lo + 64],
                                            ALU.subtract).then_inc(b_vnew, 1)

                def new_state(c):
                    nc.vector.tensor_tensor(St[:, :, :], St[:, :, :], bc3(e_last[:, 4 * c:4 * c + 4]), ALU.mult).then_inc(s_dve, 1)
                    dve.wait_ge(s_dve, 1)
                    dve.sem_inc(s_dve, -1)
                    nc.vector.tensor_tensor(St[:, :, :], St[:, :, :], heads(g[0]), ALU.add).then_inc(s_dve, 1)
                    dve.wait_ge(s_dve, 1)
                    dve.sem_inc(s_dve, -1)

                def statistics(x, st, s_root_in):
                    for half in range(2):
                        nc.vector.bn_stats(st[:, 6 * half:6 * half + 6], x[:, 512 * half:512 * half + 512]).then_inc(s_dve, 1)
                    dve.wait_ge(s_dve, 2)
                    dve.sem_inc(s_dve, -2)
                    nc.vector.bn_aggr(st[:, 12:14], st[:, 0:12]).then_inc(s_dve, 1)
                    dve.wait_ge(s_dve, 1)
                    dve.sem_inc(s_dve, -1)
                    nc.vector.tensor_scalar(st[:, 14:15], st[:, 13:14], LN_EPS, None, ALU.add).then_inc(s_dve, 1)
                    dve.wait_ge(s_dve, 1)
                    dve.sem_inc(s_dve, -1)
                    dve.sem_inc(s_root_in, 1)

                def norm_factors(st, s_root, s_norm_in):
                    dve.wait_ge(s_root, 1)
                    dve.sem_inc(s_root, -1)
                    nc.vector.reciprocal(st[:, 14:15], st[:, 14:15]).then_inc(s_dve, 1)
                    dve.wait_ge(s_dve, 1)
                    dve.sem_inc(s_dve, -1)
                    nc.vector.tensor_scalar(st[:, 15:16], st[:, 12:13], st[:, 14:15], -1.0, ALU.mult, ALU.mult).then_inc(s_dve, 1)
                    dve.wait_ge(s_dve, 1)
                    dve.sem_inc(s_dve, -1)
                    dve.sem_inc(s_norm_in, 1)

                def find(h0, h1, width, values, order, ids, left):
                    for h in range(h0, h1):
                        nc.vector.max_index(ids[:, h, 0:8], order[:, h, 0:8], values(h)).then_inc(s_dve, 1)
                        nc.vector.match_replace(left[:, h, :], order[:, h, 0:8], values(h), LEAST).then_inc(s_dve, 1)
                    dve.wait_ge(s_dve, 2 * (h1 - h0))
                    dve.sem_inc(s_dve, -(2 * (h1 - h0)))

                score = lambda hp: banks[hp // 8][:, (hp % 8) * P:(hp % 8 + 1) * P]

                def piece(n, t):
                    beta = gates[:, 1, t, :]
                    if n == 0:
                        nc.vector.tensor_tensor(gU, per_head(const("upto")), bc3(gates[:, 0, t, :]), ALU.mult).then_inc(s_dve, 1)
                        nc.vector.tensor_tensor(bI, per_head(ident), bc3(beta), ALU.mult).then_inc(s_dve, 1)
                        nc.vector.tensor_scalar(NG4, gates[:, 0, t, :], -1.0, None, ALU.mult).then_inc(s_dve, 1)
                        dve.wait_ge(s_dve, 3)
                        dve.sem_inc(s_dve, -3)
                        dve.sem_inc(b_gu, 1)
                    elif n == 1:
                        dve.wait_ge(b_squared, 1)
                        dve.sem_inc(b_squared, -1)
                        nc.vector.reduce_sum(SS, sq, AX.X).then_inc(s_dve, 1)
                        dve.wait_ge(s_dve, 1)
                        dve.sem_inc(s_dve, -1)
                        nc.vector.tensor_scalar(SS, SS, NORM_EPS, None, ALU.add).then_inc(s_dve, 1)
                        dve.wait_ge(s_dve, 1)
                        dve.sem_inc(s_dve, -1)
                        dve.sem_inc(b_root_in, 1)
                        soften(0)
                    elif n == 2:
                        dve.wait_ge(b_root, 1)
                        dve.sem_inc(b_root, -1)
                        dve.wait_ge(b_gexp, 1)
                        dve.sem_inc(b_gexp, -1)
                        nc.vector.reciprocal(RS, RS).then_inc(s_dve, 1)
                        dve.wait_ge(s_dve, 1)
                        dve.sem_inc(s_dve, -1)
                        nc.vector.tensor_scalar(CO[:, 0, :], RS[:, 0:4], float(BD) ** -0.5, None, ALU.mult).then_inc(s_dve, 1)
                        nc.vector.tensor_copy(CO[:, 2, :], RS[:, 4:8]).then_inc(s_dve, 1)
                        nc.vector.tensor_tensor(CO[:, 3, :], RS[:, 4:8], e_rest, ALU.mult).then_inc(s_dve, 1)
                        nc.vector.tensor_tensor(CO[:, 4, :], RS[:, 4:8], e_gc, ALU.mult).then_inc(s_dve, 1)
                        dve.wait_ge(s_dve, 4)
                        dve.sem_inc(s_dve, -4)
                        nc.vector.tensor_tensor(CO[:, 1, :], CO[:, 0, :], e_gc, ALU.mult).then_inc(s_dve, 1)
                        nc.vector.tensor_tensor(CO[:, 4, :], CO[:, 4, :], beta, ALU.mult).then_inc(s_dve, 1)
                        dve.wait_ge(s_dve, 2)
                        dve.sem_inc(s_dve, -2)
                        for dst, src, i in ((qk_tok[:, 0:4, :], g[0], 0), (qk_tok[:, 4:8, :], g[0], 1), (qk_tok[:, 8:12, :], g[1], 2),
                                            (kdec, g[1], 3), (kbe, g[1], 4)):
                            nc.vector.tensor_tensor(dst, heads(src), bc3(CO[:, i, :]), ALU.mult).then_inc(s_dve, 1)
                        nc.vector.tensor_tensor(vb, heads(g[2]), bc3(beta), ALU.mult).then_inc(s_dve, 1)
                        dve.wait_ge(s_dve, 6)
                        dve.sem_inc(s_dve, -6)
                        dve.sem_inc(b_tok_done, 1)
                    elif n == 4:
                        divide(0)
                        dve.sem_inc(b_pv_read, 1)
                        dve.wait_ge(b_decayed, 1)
                        dve.sem_inc(b_decayed, -1)
                        dve.wait_ge(b_kk, 1)
                        dve.sem_inc(b_kk, -1)
                        nc.vector.tensor_tensor(MT, DT, heads(g[2]), ALU.mult).then_inc(s_dve, 1)
                        dve.wait_ge(s_dve, 1)
                        dve.sem_inc(s_dve, -1)
                        nc.vector.tensor_tensor(MT, MT, heads(g[0]), ALU.mult).then_inc(s_dve, 1)
                        dve.wait_ge(s_dve, 1)
                        dve.sem_inc(s_dve, -1)
                        nc.vector.tensor_tensor(intraT, DT, heads(g[1]), ALU.mult).then_inc(s_dve, 1)
                        dve.wait_ge(s_dve, 1)
                        dve.sem_inc(s_dve, -1)
                        mask(0)
                        mask(1)
                    elif n == 5:
                        grow(0)
                        soften(1)
                        nc.vector.tensor_copy(const("dist")[:, 0:CHUNK], const("dist_past")).then_inc(s_dve, 1)
                        dve.wait_ge(s_dve, 1)
                        dve.sem_inc(s_dve, -1)
                    elif n in (6, 7, 8, 9):
                        grow(n - 5)
                        mask(n - 4)
                    elif n == 10:
                        grow(5)
                        divide(1)
                        dve.sem_inc(b_ya, 1)
                    elif n == 11:
                        new_values(0)
                    elif n == 12:
                        dve.wait_ge(b_o_ds, 1)
                        dve.sem_inc(b_o_ds, -1)
                        new_state(0)
                        dve.sem_inc(b_state, 1)
                    elif n == 13:
                        new_values(1)
                    elif n == 14:
                        dve.wait_ge(b_o_ds, 1)
                        dve.sem_inc(b_o_ds, -1)
                        dve.sem_inc(b_osq_in, 1)
                        new_state(1)
                        nc.vector.tensor_copy(vtok[:, 1, :], vtok[:, 0, :]).then_inc(s_dve, 1)
                        dve.wait_ge(s_dve, 1)
                        dve.sem_inc(s_dve, -1)
                    elif n == 15:
                        dve.wait_ge(b_osq, 1)
                        dve.sem_inc(b_osq, -1)
                        nc.vector.reduce_sum(SO, on, AX.X).then_inc(s_dve, 1)
                        dve.wait_ge(s_dve, 1)
                        dve.sem_inc(s_dve, -1)
                        nc.vector.tensor_scalar(SO, SO, 1.0 / BD, NORM_EPS, ALU.mult, ALU.add).then_inc(s_dve, 1)
                        dve.wait_ge(s_dve, 1)
                        dve.sem_inc(s_dve, -1)
                        dve.sem_inc(b_oroot_in, 1)
                    elif n == 16:
                        dve.wait_ge(b_oroot, 1)
                        dve.sem_inc(b_oroot, -1)
                        nc.vector.reciprocal(SO, SO).then_inc(s_dve, 1)
                        dve.wait_ge(s_dve, 1)
                        dve.sem_inc(s_dve, -1)
                        nc.vector.tensor_tensor(on, heads(g[3]), bc3(SO), ALU.mult).then_inc(b_on_ready, 1)
                    elif n == 17:
                        dve.wait_ge(b_onT_ps, 1)
                        dve.sem_inc(b_onT_ps, -1)
                        nc.vector.tensor_tensor(yT[:, 4:8, :], zt, heads(g[1]), ALU.mult).then_inc(s_dve, 1)
                        dve.wait_ge(s_dve, 1)
                        dve.sem_inc(s_dve, -1)
                        dve.sem_inc(b_yT_b, 1)
                        dve.sem_inc(b_raw_free, 1)
                        dve.sem_inc(b_o_done, 1)
                    elif n == 20:
                        dve.wait_ge(b_mix_ps, 1)
                        dve.sem_inc(b_mix_ps, -1)
                        dve.wait_ge(b_pre_in, 16)
                        dve.sem_inc(b_pre_in, -16)
                        nc.vector.scalar_tensor_tensor(pre[:, :], pre[:, :], ALPHA, b0[:, :], ALU.mult, ALU.add).then_inc(s_dve, 1)
                        dve.wait_ge(s_dve, 1)
                        dve.sem_inc(s_dve, -1)
                        statistics(pre, stb, b_lroot_in)
                    elif n == 21:
                        norm_factors(stb, b_lroot, b_norm_in)
                    elif n == 22:
                        dve.wait_ge(b_normed, 1)
                        dve.sem_inc(b_normed, -1)
                        dve.wait_ge(b_rows_ps, 1)
                        dve.sem_inc(b_rows_ps, -1)
                        nc.vector.tensor_tensor(pre[:, :], pre[:, :], banks[1][:, :], ALU.mult).then_inc(s_dve, 1)
                        dve.wait_ge(s_dve, 1)
                        dve.sem_inc(s_dve, -1)
                        nc.vector.tensor_tensor(h1n[:, :], pre[:, :], banks[2][:, :], ALU.add).then_inc(s_dve, 1)
                        dve.wait_ge(s_dve, 1)
                        dve.sem_inc(s_dve, -1)
                        dve.sem_inc(b_h1, 1)
                        dve.sem_inc(b_pre_free, 1)
                    elif n in (31, 33):
                        if n == 31:
                            dve.wait_ge(b_scores_a, 1)
                            dve.sem_inc(b_scores_a, -1)
                        else:
                            dve.wait_ge(b_scores, 1)
                            dve.sem_inc(b_scores, -1)
                        half = (n - 31) // 2
                        for hp in range(PH * half, PH * half + PH):
                            nc.vector.max(top[:, hp, 0:8], score(hp)).then_inc(s_dve, 1)
                        dve.wait_ge(s_dve, PH)
                        dve.sem_inc(s_dve, -PH)
                    elif n == 32:
                        find(0, PH, NK, score, top, itop, rest)
                    elif n == 34:
                        find(PH, 2 * PH, NK, score, top, itop, rest)
                        dve.sem_inc(b_scores_read, 1)
                    elif n == 35:
                        for hp in range(2 * PH):
                            nc.vector.max(top[:, hp, 8:16], rest[:, hp, :]).then_inc(s_dve, 1)
                        dve.wait_ge(s_dve, 2 * PH)
                        dve.sem_inc(s_dve, -(2 * PH))
                    elif n == 36:
                        for hp in range(2 * PH):
                            nc.vector.max_index(itop[:, hp, 8:16], top[:, hp, 8:16], rest[:, hp, :]).then_inc(s_dve, 1)
                        dve.wait_ge(s_dve, 2 * PH)
                        dve.sem_inc(s_dve, -(2 * PH))
                    elif n == 37:
                        nc.vector.tensor_copy(ftop.rearrange("p h q k -> p (h q k)"), flat(itop)).then_inc(s_dve, 1)
                        dve.wait_ge(s_dve, 1)
                        dve.sem_inc(s_dve, -1)
                        nc.vector.tensor_scalar(ftop[:, :, 0, :], ftop[:, :, 0, :], float(NK), None, ALU.mult).then_inc(s_dve, 1)
                        dve.wait_ge(s_dve, 1)
                        dve.sem_inc(s_dve, -1)
                        tv = top.rearrange("p (h q) k -> p h q k", q=2)
                        for dst, src in ((cand, tv), (cid, ftop)):
                            for i0, i1, w, at in PAIR_ROWS:
                                o = dst[:, :, at:at + (i1 - i0) * w].rearrange("p h (i j) -> p h i j", j=w)
                                nc.vector.tensor_tensor(o, src[:, :, 0, i0:i1].unsqueeze(3).to_broadcast([P, PH, i1 - i0, w]),
                                                        src[:, :, 1, 0:w].unsqueeze(2).to_broadcast([P, PH, i1 - i0, w]),
                                                        ALU.add).then_inc(s_dve, 1)
                        dve.wait_ge(s_dve, 2 * len(PAIR_ROWS))
                        dve.sem_inc(s_dve, -(2 * len(PAIR_ROWS)))
                    elif n == 38:
                        for h in range(PH):
                            nc.vector.max(best[:, h, 0:8], cand[:, h, :]).then_inc(s_dve, 1)
                        dve.wait_ge(s_dve, PH)
                        dve.sem_inc(s_dve, -PH)
                        find(0, PH, NCAND, lambda h: cand[:, h, :], best, ibest, crest)
                    elif n == 39:
                        for h in range(PH):
                            nc.vector.max(best[:, h, 8:16], crest[:, h, :]).then_inc(s_dve, 1)
                        dve.wait_ge(s_dve, PH)
                        dve.sem_inc(s_dve, -PH)
                        for h in range(PH):
                            nc.vector.max_index(ibest[:, h, 8:16], best[:, h, 8:16], crest[:, h, :]).then_inc(s_dve, 1)
                        dve.wait_ge(s_dve, PH)
                        dve.sem_inc(s_dve, -PH)
                        nc.vector.tensor_copy(fbest, ibest).then_inc(s_dve, 1)
                        dve.wait_ge(s_dve, 1)
                        dve.sem_inc(s_dve, -1)
                        nc.vector.tensor_copy(den[:, 0, :], best[:, :, 0]).then_inc(s_dve, 1)
                        dve.wait_ge(s_dve, 1)
                        dve.sem_inc(s_dve, -1)
                        nc.vector.tensor_tensor(best, best, den[:, 0, :].unsqueeze(2).to_broadcast([P, PH, TOPK]), ALU.subtract).then_inc(s_dve, 1)
                        dve.wait_ge(s_dve, 1)
                        dve.sem_inc(s_dve, -1)
                        dve.sem_inc(b_soft, 1)
                    elif 40 <= n <= 47:
                        for h in range(n - 40, n - 39):
                            nc.vector.tensor_tensor(eq, const("iota50").unsqueeze(1).to_broadcast([P, TOPK, NCAND]),
                                                    fbest[:, h, :].unsqueeze(2).to_broadcast([P, TOPK, NCAND]), ALU.is_equal).then_inc(s_dve, 1)
                            dve.wait_ge(s_dve, 1)
                            dve.sem_inc(s_dve, -1)
                            nc.vector.tensor_tensor(eq, eq, cid[:, h, :].unsqueeze(1).to_broadcast([P, TOPK, NCAND]), ALU.mult).then_inc(s_dve, 1)
                            dve.wait_ge(s_dve, 1)
                            dve.sem_inc(s_dve, -1)
                            nc.vector.reduce_sum(fex[:, h, :], eq, AX.X).then_inc(s_dve, 1)
                            dve.wait_ge(s_dve, 1)
                            dve.sem_inc(s_dve, -1)
                    elif n == 48:
                        dve.wait_ge(g_indexfree, 1)
                        dve.sem_inc(g_indexfree, -1)
                        nc.vector.tensor_copy(eidx_n[:, :], flat(fex)).then_inc(s_dve, 1)
                        dve.wait_ge(s_dve, 1)
                        dve.sem_inc(s_dve, -1)
                        dve.sem_inc(g_tile, 1)
                        dve.wait_ge(b_exped, 1)
                        dve.sem_inc(b_exped, -1)
                        nc.vector.reduce_sum(den[:, 0, :], best, AX.X).then_inc(s_dve, 1)
                        dve.wait_ge(s_dve, 1)
                        dve.sem_inc(s_dve, -1)
                        nc.vector.reciprocal(den[:, 1, :], den[:, 0, :]).then_inc(s_dve, 1)
                        dve.wait_ge(s_dve, 1)
                        dve.sem_inc(s_dve, -1)
                        nc.vector.tensor_tensor(egate_n[:, :].rearrange("p (h k) -> p h k", h=PH), best,
                                                den[:, 1, :].unsqueeze(2).to_broadcast([P, PH, TOPK]), ALU.mult).then_inc(s_dve, 1)
                        dve.wait_ge(s_dve, 1)
                        dve.sem_inc(s_dve, -1)

                def dot(t, s, par, k):
                    dve.wait_ge(g_u[k], (t * NGROUP + s) * 16 + 16)
                    return nc.vector.tensor_tensor_reduce(out=U[:, k, :], in0=U[:, k, :], in1=h1c[:, :], scale=1.0, scalar=0.0,
                                                          op0=ALU.mult, op1=ALU.add, accum_out=dots[:, par, k:k + 1])

                def add(t, s, par, k):
                    dve.wait_ge(g_v[k], (t * NGROUP + s) * 16)
                    return nc.vector.scalar_tensor_tensor(out=acc[:, :], in0=V[:, k, :], scalar=gl[:, 1 - par, k:k + 1],
                                                          in1=acc[:, :], op0=ALU.mult, op1=ALU.add)

                def weigh(s, par):
                    dve.wait_ge(g_gelu, 1)
                    dve.sem_inc(g_gelu, -1)
                    w = gl[:, 1 - par, :]
                    nc.vector.tensor_tensor(w, w, egate[:, bass.ds(s * GS - GS, GS)], ALU.mult).then_inc(s_dve, 1)
                    dve.wait_ge(s_dve, 1)
                    dve.sem_inc(s_dve, -1)
                    dve.sem_inc(g_w, 1)

                def dot_of(t, s, par, k):
                    dot(t, s, par, k).then_inc(g_ufree[k] if k < GS - 1 else g_dots, 1)

                def add_of(t, s, par, k, nv):
                    if k >= GS - nv:
                        add(t, s, par, k).then_inc(s_dve, 1)
                        dve.wait_ge(s_dve, 1)
                        dve.sem_inc(s_dve, -1)
                        dve.sem_inc(g_vfree[k], 1)

                def gather_a(t, s, par, nv=2):
                    dot_of(t, s, par, 0)
                    weigh(s, par)
                    add_of(t, s, par, 0, nv)
                    dot_of(t, s, par, 1)
                    add_of(t, s, par, 1, nv)

                def gather_b(t, s, par, nv=2):
                    dot_of(t, s, par, 2)
                    add_of(t, s, par, 2, nv)
                    dot_of(t, s, par, 3)
                    add_of(t, s, par, 3, nv)

                def finish_sum():
                    dve.wait_ge(g_accps, 1)
                    dve.sem_inc(g_accps, -1)
                    nc.vector.tensor_tensor(pre[:, :], acc[:, :], acc_ps[:, :], ALU.add).then_inc(s_dve, 1)
                    dve.wait_ge(s_dve, 1)
                    dve.sem_inc(s_dve, -1)
                    dve.sem_inc(g_accfree, 1)

                def boundary(t):
                    weigh(NGROUP, 0)
                    nc.vector.tensor_copy(h1c[:, :], h1n[:, :]).then_inc(s_dve, 1)
                    dve.wait_ge(s_dve, 1)
                    dve.sem_inc(s_dve, -1)
                    dve.sem_inc(b_h1n_free, 1)
                    dot_of(t, NGROUP, 0, 0)
                    nc.vector.tensor_copy(egate[:, :], egate_n[:, :]).then_inc(s_dve, 1)
                    dve.wait_ge(s_dve, 1)
                    dve.sem_inc(s_dve, -1)
                    dot_of(t, NGROUP, 0, 1)
                    gather_b(t, NGROUP, 0)
                    finish_sum()

                def norm():
                    dve.wait_ge(t_normed, 1)
                    dve.sem_inc(t_normed, -1)
                    dve.wait_ge(t_ln, 1)
                    dve.sem_inc(t_ln, -1)
                    nc.vector.tensor_tensor(pre[:, :], pre[:, :], banks[1][:, :], ALU.mult).then_inc(s_dve, 1)
                    dve.wait_ge(s_dve, 1)
                    dve.sem_inc(s_dve, -1)
                    nc.vector.tensor_tensor(pre[:, :], pre[:, :], banks[2][:, :], ALU.add).then_inc(s_dve, 1)
                    dve.wait_ge(s_dve, 1)
                    dve.sem_inc(s_dve, -1)
                    dve.sem_inc(t_lnfree, 1)
                    dve.sem_inc(t_out, 1)

                def plain_steps(t, after_tile):
                    if after_tile:
                        statistics(pre, st2, t_root_in)
                    nc.vector.tensor_scalar(acc[:, :], h1c[:, :], ALPHA, None, ALU.mult).then_inc(s_dve, 1)
                    dve.wait_ge(s_dve, 1)
                    dve.sem_inc(s_dve, -1)
                    gather_a(t, 1, 1)
                    if after_tile:
                        norm_factors(st2, t_root, t_norm_in)
                    gather_b(t, 1, 1)
                    for s in range(2, PLAIN + 1):
                        gather_a(t, s, s % 2)
                        gather_b(t, s, s % 2)
                    if after_tile:
                        norm()

                dve.sem_inc(b_raw_free, 1)
                dve.sem_inc(b_pre_free, 1)
                dve.sem_inc(b_h1n_free, 1)
                dve.sem_inc(b_wo_free0, 1)
                dve.sem_inc(b_wo_free1, 1)
                for k in range(GS):
                    dve.sem_inc(g_ufree[k], 1)
                    dve.sem_inc(g_vfree[k], 1)
                dve.sem_inc(g_accfree, 1)
                dve.sem_inc(g_indexfree, 1)
                dve.wait_ge(b_load, 80)
                nc.vector.tensor_scalar(sink[:, 1, :], sink[:, 0, :], float(AD) ** 0.5, None, ALU.mult).then_inc(s_dve, 1)
                nc.vector.memset(vtok[:, 1, :], 0.0).then_inc(s_dve, 1)
                nc.vector.memset(pr[:, :, :], 0.0).then_inc(s_dve, 1)
                nc.vector.memset(St[:, :, :], 0.0).then_inc(s_dve, 1)
                dve.wait_ge(s_dve, 4)
                dve.sem_inc(s_dve, -4)
                for n in range(NPIECE):
                    piece(n, 0)
                nc.vector.tensor_copy(egate[:, :], egate_n[:, :]).then_inc(s_dve, 1)
                nc.vector.tensor_copy(h1c[:, :], h1n[:, :]).then_inc(s_dve, 1)
                dve.wait_ge(s_dve, 2)
                dve.sem_inc(s_dve, -2)
                dve.sem_inc(b_h1n_free, 1)
                for k in range(GS):
                    dot_of(0, 0, 0, k)
                plain_steps(0, False)
                with dve.Fori(0, T - 1) as t:
                    for s in range(PLAIN + 1, NGROUP + 1):
                        if s == NGROUP:
                            boundary(t)
                        else:
                            gather_a(t, s, s % 2, ON_VECTOR[s])
                            for n in pieces(VECTOR_AT, 2 * s):
                                piece(n, t + 1)
                            gather_b(t, s, s % 2, ON_VECTOR[s])
                            for n in pieces(VECTOR_AT, 2 * s + 1):
                                piece(n, t + 1)
                    plain_steps(t + 1, True)
                with dve.Fori(0, (NGROUP - PLAIN) // 2 - 1) as j:
                    for s in range(3, 5):
                        gather_a(T - 1, 2 * j + s, s % 2)
                        gather_b(T - 1, 2 * j + s, s % 2)
                gather_a(T - 1, NGROUP - 1, 1)
                gather_b(T - 1, NGROUP - 1, 1)
                weigh(NGROUP, 0)
                for k in range(GS):
                    add_of(T - 1, NGROUP, 0, k, 2)
                dve.wait_ge(t_free, 1)
                dve.sem_inc(t_free, -1)
                finish_sum()
                statistics(pre, st2, t_root_in)
                norm_factors(st2, t_root, t_norm_in)
                norm()
        b.close()


_INS = ['x', 'ln_in_g', 'ln_in_b', 'w_in', 'conv_w', 'a_sinks', 'b_a_log', 'b_dt_bias', 'b_norm_w', 'w_out',
        'ln1_g', 'ln1_b', 'w_query', 'sub_keys', 'expert_u', 'expert_v', 'ln2_g', 'ln2_b']


def kernel(**inputs):
    import numpy as _np
    import concourse.bacc as _bacc
    from concourse import mybir as _mybir
    from concourse.bass_utils import run_bass_kernel_spmd as _run

    nc = _bacc.Bacc("TRN2", target_bir_lowering=False, num_devices=1)
    arrays, args = {}, []
    arrays["constants"] = constant_table()
    args.append(nc.dram_tensor("constants", (P, NCONST), _mybir.dt.float32, kind="ExternalInput").ap())
    for name in _INS:
        a = _np.ascontiguousarray(inputs[name])
        arrays[f"in_{name}"] = a
        args.append(nc.dram_tensor(f"in_{name}", a.shape, _mybir.dt.from_np(a.dtype), kind="ExternalInput").ap())
    args.append(nc.dram_tensor("out_0", (1, S, D), _mybir.dt.float32, kind="ExternalOutput").ap())
    build(nc, *args)
    r = _run(nc, [arrays], core_ids=[0])
    return r.results[0]["out_0"]
```
